# Optimizing a Trainium2 kernel written in Bass

```python
import jax, jax.numpy as jnp
from jax import lax
import numpy as np
import math

D_MODEL = 1024
BATCH = 1
SEQ = 256
DEPTH = 1

CHUNK = 64
Q_BLOCK = 128
A_HEADS = 8
A_HEAD_DIM = D_MODEL // 16
A_WIDTH = A_HEADS * A_HEAD_DIM
POOL_WINDOWS = (2, 4, 8, 16)
POOL_GROUPS = len(POOL_WINDOWS)
POOL_WIDTH = D_MODEL // 4
POOL_GROUP_DIM = POOL_WIDTH // POOL_GROUPS
CONV_WIDTH = D_MODEL // 4
CONV_K = 3
N_BRANCH = 3
MIX_WIDTH = A_WIDTH + POOL_WIDTH + CONV_WIDTH
D_FF = 4 * D_MODEL
RMS_EPS = 1e-6
NEG_INF = -1e30
IN_COLS = 3 * A_WIDTH + A_HEADS + POOL_WIDTH + 3 * CONV_WIDTH + N_BRANCH * D_MODEL


def rmsnorm(x, g):
    xf = x.astype(jnp.float32)
    y = xf * lax.rsqrt(jnp.mean(xf * xf, axis=-1, keepdims=True) + RMS_EPS)
    return (y * g.astype(jnp.float32)).astype(x.dtype)

def forgetting_attention(q, k, v, f_logit):
    b, s, h, dh = q.shape
    q = q.transpose(0, 2, 1, 3)
    k = k.transpose(0, 2, 1, 3)
    v = v.transpose(0, 2, 1, 3)
    log_f = jax.nn.log_sigmoid(f_logit.astype(jnp.float32))
    cum_f = jnp.cumsum(log_f, axis=1).transpose(0, 2, 1)
    scale = dh ** -0.5
    outs = []
    for i in range(s // Q_BLOCK):
        qs, qe = i * Q_BLOCK, (i + 1) * Q_BLOCK
        qb = q[:, :, qs:qe]
        kb = k[:, :, :qe]
        vb = v[:, :, :qe]
        logits = jnp.einsum('bhqd,bhkd->bhqk', qb, kb).astype(jnp.float32) * scale
        logits = logits + cum_f[:, :, qs:qe, None] - cum_f[:, :, None, :qe]
        causal = jnp.arange(qs, qe)[:, None] >= jnp.arange(qe)[None, :]
        logits = jnp.where(causal[None, None], logits, NEG_INF)
        p = jax.nn.softmax(logits, axis=-1).astype(v.dtype)
        outs.append(jnp.einsum('bhqk,bhkd->bhqd', p, vb))
    o = jnp.concatenate(outs, axis=2)
    return o.transpose(0, 2, 1, 3).reshape(b, s, h * dh)

def pool_mixer(u, w_pool, pool_scale):
    b, s, _ = u.shape
    uf = u.astype(jnp.float32)
    cs = jnp.cumsum(uf, axis=1)
    groups = []
    for g, w in enumerate(POOL_WINDOWS):
        sl = slice(g * POOL_GROUP_DIM, (g + 1) * POOL_GROUP_DIM)
        cs_g = cs[..., sl]
        lagged = jnp.pad(cs_g, ((0, 0), (w, 0), (0, 0)))[:, :s]
        count = jnp.minimum(jnp.arange(1, s + 1, dtype=jnp.float32), float(w))
        groups.append((cs_g - lagged) / count[None, :, None] - uf[..., sl])
    p = jnp.stack(groups, axis=2).astype(u.dtype)
    y = jnp.einsum('bsgc,gcd->bsgd', p, w_pool).reshape(b, s, POOL_WIDTH)
    return y * pool_scale

def short_conv(h, b_gate, c_gate, conv_w):
    u = c_gate * h
    y = lax.conv_general_dilated(
        u, conv_w[:, None, :].astype(u.dtype), window_strides=(1,), padding=[(CONV_K - 1, 0)],
        dimension_numbers=('NWC', 'WIO', 'NWC'), feature_group_count=CONV_WIDTH)
    return b_gate * y

def hybrid_layer(x, c, w_ada, b_ada, g_mix_pre, g_mix_post, g_ff_pre, g_ff_post, w_in, b_f,
                 w_pool, pool_scale, conv_w, w_branch, w_out, w_ff1, w_ff2):
    b, s, d = x.shape
    mod = jax.nn.silu(c) @ w_ada + b_ada
    shift_m, scale_m, gate_m, shift_f, scale_f, gate_f = jnp.split(mod, 6, axis=-1)

    h = rmsnorm(x, g_mix_pre) * (1.0 + scale_m[:, None]) + shift_m[:, None]
    z = h @ w_in
    sizes = [A_WIDTH, A_WIDTH, A_WIDTH, A_HEADS, POOL_WIDTH, CONV_WIDTH, CONV_WIDTH, CONV_WIDTH]
    cuts = [int(v) for v in np.cumsum(sizes)]
    q, k, v, fl, pu, ch, cb, cc, gl = jnp.split(z, cuts, axis=-1)
    heads = (b, s, A_HEADS, A_HEAD_DIM)
    br_a = forgetting_attention(q.reshape(heads), k.reshape(heads), v.reshape(heads), fl + b_f)
    br_b = pool_mixer(pu, w_pool, pool_scale)
    br_c = short_conv(ch, cb, cc, conv_w)
    gates = jax.nn.sigmoid(gl).reshape(b, s, N_BRANCH, d)
    wa = w_branch[:A_WIDTH]
    wb = w_branch[A_WIDTH:A_WIDTH + POOL_WIDTH]
    wc = w_branch[A_WIDTH + POOL_WIDTH:]
    merged = gates[:, :, 0] * (br_a @ wa) + gates[:, :, 1] * (br_b @ wb) + gates[:, :, 2] * (br_c @ wc)
    y = merged @ w_out
    x = x + gate_m[:, None] * rmsnorm(y, g_mix_post)

    h2 = rmsnorm(x, g_ff_pre) * (1.0 + scale_f[:, None]) + shift_f[:, None]
    y2 = jnp.square(jax.nn.relu(h2 @ w_ff1)) @ w_ff2
    return x + gate_f[:, None] * rmsnorm(y2, g_ff_post)

def first_inputs(seed: int = 0) -> dict:
    key = jax.random.key(seed)
    ks = jax.random.split(key, 20)

    def nrm(k, shape, std):
        return jax.random.normal(k, shape, jnp.float32) * std

    d = D_MODEL
    branch_row_scale = jnp.concatenate([
        jnp.full((A_WIDTH,), A_WIDTH ** -0.5, jnp.float32),
        jnp.full((POOL_WIDTH,), POOL_WIDTH ** -0.5, jnp.float32),
        jnp.full((CONV_WIDTH,), CONV_WIDTH ** -0.5, jnp.float32)])
    return {
        'x': nrm(ks[0], (BATCH, SEQ, d), 1.0),
        'c': nrm(ks[1], (BATCH, d), 1.0),
        'w_ada': nrm(ks[2], (DEPTH, d, 6 * d), 0.5 * d ** -0.5),
        'b_ada': nrm(ks[3], (DEPTH, 6 * d), 0.02),
        'g_mix_pre': 1.0 + nrm(ks[4], (DEPTH, d), 0.05),
        'g_mix_post': 1.0 + nrm(ks[5], (DEPTH, d), 0.05),
        'g_ff_pre': 1.0 + nrm(ks[6], (DEPTH, d), 0.05),
        'g_ff_post': 1.0 + nrm(ks[7], (DEPTH, d), 0.05),
        'w_in': nrm(ks[8], (DEPTH, d, IN_COLS), d ** -0.5),
        'b_f': 3.0 + nrm(ks[9], (DEPTH, A_HEADS), 0.1),
        'w_pool': nrm(ks[10], (DEPTH, POOL_GROUPS, POOL_GROUP_DIM, POOL_GROUP_DIM), POOL_GROUP_DIM ** -0.5),
        'pool_scale': 1.0 + nrm(ks[11], (DEPTH, POOL_WIDTH), 0.1),
        'conv_w': nrm(ks[12], (DEPTH, CONV_K, CONV_WIDTH), CONV_K ** -0.5),
        'w_branch': nrm(ks[13], (DEPTH, MIX_WIDTH, d), 1.0) * branch_row_scale[None, :, None],
        'w_out': nrm(ks[14], (DEPTH, d, d), d ** -0.5),
        'w_ff1': nrm(ks[15], (DEPTH, d, D_FF), d ** -0.5),
        'w_ff2': nrm(ks[16], (DEPTH, D_FF, d), D_FF ** -0.5),
    }

def first_block(x, c, w_ada, b_ada, g_mix_pre, g_mix_post, g_ff_pre, g_ff_post, w_in, b_f,
              w_pool, pool_scale, conv_w, w_branch, w_out, w_ff1, w_ff2):
    for l in range(DEPTH):
        x = hybrid_layer(x, c, w_ada[l], b_ada[l], g_mix_pre[l], g_mix_post[l], g_ff_pre[l], g_ff_post[l],
                         w_in[l], b_f[l], w_pool[l], pool_scale[l], conv_w[l], w_branch[l], w_out[l],
                         w_ff1[l], w_ff2[l])
    return x


MIX_WIDTH_2 = D_MODEL
HEAD_DIM = 64
A_WIDTH_2 = D_MODEL // 4
B_WIDTH = D_MODEL // 2
C_WIDTH = D_MODEL // 4
A_HEADS_2 = A_WIDTH_2 // HEAD_DIM
B_HEADS = B_WIDTH // HEAD_DIM
C_GROUPS = C_WIDTH // HEAD_DIM
IN_COLS_2 = 2 * A_WIDTH_2 + 3 * B_WIDTH + 2 * C_WIDTH
CHUNK_2 = 128
MOBA_BLOCK = 256
MOBA_TOPK = 3
Q_BLK = 64
CONV_WIDTH_2 = 31
MEM_LEN = 256
X_HEADS = 4
X_HEAD_DIM = D_MODEL // X_HEADS
D_FF_2 = 4 * D_MODEL
EPS = 1e-6


def rms_norm(x, g):
    xf = x.astype(jnp.float32)
    y = xf * lax.rsqrt(jnp.mean(xf * xf, axis=-1, keepdims=True) + EPS)
    return (y * g.astype(jnp.float32)).astype(x.dtype)

def layer_norm(x, g, b):
    xf = x.astype(jnp.float32)
    mu = jnp.mean(xf, axis=-1, keepdims=True)
    xc = xf - mu
    var = jnp.mean(xc * xc, axis=-1, keepdims=True)
    y = xc * lax.rsqrt(var + EPS) * g.astype(jnp.float32) + b.astype(jnp.float32)
    return y.astype(x.dtype)

def alibi_slopes(n_heads):
    return 2.0 ** (-8.0 * jnp.arange(1, n_heads + 1, dtype=jnp.float32) / n_heads)

def spatial_gating(z, ln_g, ln_b, w_s, b_s):
    Bn, S, _ = z.shape
    u, v = jnp.split(z, 2, axis=-1)
    v = layer_norm(v, ln_g, ln_b)
    v = v.reshape(Bn, S // CHUNK_2, CHUNK_2, A_HEADS_2, HEAD_DIM)
    causal = jnp.tril(jnp.ones((CHUNK_2, CHUNK_2), dtype=w_s.dtype))
    w = (w_s * causal[None]).astype(v.dtype)
    mixed = jnp.einsum('hts,bcshd->bcthd', w, v) + b_s.T.astype(v.dtype)[None, None, :, :, None]
    return u * mixed.reshape(Bn, S, A_WIDTH_2)

def moba_attention(q, k, v):
    Bn, H, S, Dh = q.shape
    s_pad = -(-S // MOBA_BLOCK) * MOBA_BLOCK
    pad = ((0, 0), (0, 0), (0, s_pad - S), (0, 0))
    q, k, v = jnp.pad(q, pad), jnp.pad(k, pad), jnp.pad(v, pad)
    nb = s_pad // MOBA_BLOCK
    kk = min(MOBA_TOPK, nb)
    n_q = s_pad // Q_BLK
    scale = Dh ** -0.5
    slopes = alibi_slopes(H)
    kb = k.reshape(Bn, H, nb, MOBA_BLOCK, Dh)
    vb = v.reshape(Bn, H, nb, MOBA_BLOCK, Dh)
    kmean = jnp.mean(kb.astype(jnp.float32), axis=3)
    qc = q.reshape(Bn, H, n_q, Q_BLK, Dh).transpose(2, 0, 1, 3, 4)
    bi = jnp.arange(Bn)[:, None, None, None]
    hi = jnp.arange(H)[None, :, None, None]
    offs = jnp.arange(MOBA_BLOCK)

    def one_block(args):
        qi, ci = args
        t = ci * Q_BLK + jnp.arange(Q_BLK)
        own = (ci * Q_BLK) // MOBA_BLOCK
        gate = jnp.einsum('bhqd,bhnd->bhqn', qi.astype(jnp.float32), kmean)
        gate = jnp.where(jnp.arange(nb) < own, gate, -jnp.inf)
        _, idx = lax.top_k(gate, kk)
        valid = idx < own
        ksel = kb[bi, hi, idx]
        vsel = vb[bi, hi, idx]
        s_past = jnp.einsum('bhqd,bhqkld->bhqkl', qi, ksel).astype(jnp.float32) * scale
        kpos = idx[..., None] * MOBA_BLOCK + offs
        dist = (t[None, None, :, None, None] - kpos).astype(jnp.float32)
        s_past = jnp.where(valid[..., None], s_past - slopes[None, :, None, None, None] * dist, -jnp.inf)
        k_own = lax.dynamic_index_in_dim(kb, own, axis=2, keepdims=False)
        v_own = lax.dynamic_index_in_dim(vb, own, axis=2, keepdims=False)
        s_own = jnp.einsum('bhqd,bhld->bhql', qi, k_own).astype(jnp.float32) * scale
        kpos_own = own * MOBA_BLOCK + offs
        dist_own = (t[:, None] - kpos_own[None, :]).astype(jnp.float32)
        s_own = jnp.where((dist_own >= 0)[None, None],
                          s_own - slopes[None, :, None, None] * dist_own[None, None], -jnp.inf)
        s_all = jnp.concatenate([s_past.reshape(Bn, H, Q_BLK, kk * MOBA_BLOCK), s_own], axis=-1)
        p = jax.nn.softmax(s_all, axis=-1).astype(v.dtype)
        p_past = p[..., :kk * MOBA_BLOCK].reshape(Bn, H, Q_BLK, kk, MOBA_BLOCK)
        p_own = p[..., kk * MOBA_BLOCK:]
        return (jnp.einsum('bhqkl,bhqkld->bhqd', p_past, vsel)
                + jnp.einsum('bhql,bhld->bhqd', p_own, v_own))

    out = lax.map(one_block, (qc, jnp.arange(n_q, dtype=jnp.int32)))
    out = out.transpose(1, 0, 3, 2, 4).reshape(Bn, s_pad, H * Dh)
    return out[:, :S]

def conformer_conv(z, w_dw, b_dw, gn_g, gn_b):
    Bn, S, _ = z.shape
    a, g = jnp.split(z, 2, axis=-1)
    y = a * jax.nn.sigmoid(g)
    rhs = w_dw.astype(y.dtype)[:, None, :]
    y = lax.conv_general_dilated(y, rhs, window_strides=(1,), padding=[(CONV_WIDTH_2 - 1, 0)],
                                 dimension_numbers=('NWC', 'WIO', 'NWC'),
                                 feature_group_count=C_WIDTH)
    y = y + b_dw.astype(y.dtype)
    y = y.reshape(Bn, S, C_GROUPS, HEAD_DIM)
    y = layer_norm(y, gn_g.reshape(C_GROUPS, HEAD_DIM), gn_b.reshape(C_GROUPS, HEAD_DIM))
    return jax.nn.silu(y.reshape(Bn, S, C_WIDTH))

def memory_cross_attention(h, m, w_q, w_kv, w_o):
    Bn, S, _ = h.shape
    M = m.shape[1]
    q = (h @ w_q).reshape(Bn, S, X_HEADS, X_HEAD_DIM)
    k, v = jnp.split(m @ w_kv, 2, axis=-1)
    k = k.reshape(Bn, M, X_HEADS, X_HEAD_DIM)
    v = v.reshape(Bn, M, X_HEADS, X_HEAD_DIM)
    s = jnp.einsum('bshd,bmhd->bhsm', q, k).astype(jnp.float32) * (X_HEAD_DIM ** -0.5)
    p = jax.nn.softmax(s, axis=-1).astype(v.dtype)
    o = jnp.einsum('bhsm,bmhd->bshd', p, v).reshape(Bn, S, D_MODEL)
    return o @ w_o

def second_inputs(seed: int = 0) -> dict:
    key = jax.random.key(seed)
    ks = jax.random.split(key, 24)
    f32 = jnp.float32
    L = DEPTH

    def nrm(k, shape, scale):
        return jax.random.normal(k, shape, f32) * scale

    def gain(k, shape):
        return 1.0 + 0.05 * jax.random.normal(k, shape, f32)

    return {
        "x": nrm(ks[0], (BATCH, SEQ, D_MODEL), 1.0),
        "mem": nrm(ks[1], (BATCH, MEM_LEN, D_MODEL), 1.0),
        "pre_mix_g": gain(ks[2], (L, D_MODEL)),
        "w_in": nrm(ks[3], (L, D_MODEL, IN_COLS_2), D_MODEL ** -0.5),
        "gate_ln_g": gain(ks[4], (L, A_WIDTH_2)),
        "gate_ln_b": nrm(ks[5], (L, A_WIDTH_2), 0.02),
        "w_s": nrm(ks[6], (L, A_HEADS_2, CHUNK_2, CHUNK_2), CHUNK_2 ** -0.5),
        "b_s": nrm(ks[7], (L, A_HEADS_2, CHUNK_2), 0.02),
        "w_dw": nrm(ks[8], (L, CONV_WIDTH_2, C_WIDTH), CONV_WIDTH_2 ** -0.5),
        "b_dw": nrm(ks[9], (L, C_WIDTH), 0.02),
        "conv_gn_g": gain(ks[10], (L, C_WIDTH)),
        "conv_gn_b": nrm(ks[11], (L, C_WIDTH), 0.02),
        "w_out": nrm(ks[12], (L, MIX_WIDTH_2, D_MODEL), MIX_WIDTH_2 ** -0.5),
        "post_mix_g": gain(ks[13], (L, D_MODEL)),
        "pre_x_g": gain(ks[14], (L, D_MODEL)),
        "mem_g": gain(ks[15], (L, D_MODEL)),
        "w_xq": nrm(ks[16], (L, D_MODEL, D_MODEL), D_MODEL ** -0.5),
        "w_xkv": nrm(ks[17], (L, D_MODEL, 2 * D_MODEL), D_MODEL ** -0.5),
        "w_xo": nrm(ks[18], (L, D_MODEL, D_MODEL), D_MODEL ** -0.5),
        "post_x_g": gain(ks[19], (L, D_MODEL)),
        "pre_ffn_g": gain(ks[20], (L, D_MODEL)),
        "w_ff1": nrm(ks[21], (L, D_MODEL, D_FF_2), D_MODEL ** -0.5),
        "w_ff2": nrm(ks[22], (L, D_FF_2, D_MODEL), D_FF_2 ** -0.5),
        "post_ffn_g": gain(ks[23], (L, D_MODEL)),
    }

def second_block(x, mem, pre_mix_g, w_in, gate_ln_g, gate_ln_b, w_s, b_s, w_dw, b_dw,
              conv_gn_g, conv_gn_b, w_out, post_mix_g, pre_x_g, mem_g, w_xq, w_xkv,
              w_xo, post_x_g, pre_ffn_g, w_ff1, w_ff2, post_ffn_g):
    Bn, S, _ = x.shape
    split_a = 2 * A_WIDTH_2
    split_b = split_a + 3 * B_WIDTH
    for l in range(DEPTH):
        h = rms_norm(x, pre_mix_g[l])
        z = h @ w_in[l]
        za, zb, zc = z[..., :split_a], z[..., split_a:split_b], z[..., split_b:]
        ya = spatial_gating(jax.nn.gelu(za, approximate=False),
                            gate_ln_g[l], gate_ln_b[l], w_s[l], b_s[l])
        q, k, v = jnp.split(zb, 3, axis=-1)
        q, k, v = (a.reshape(Bn, S, B_HEADS, HEAD_DIM).transpose(0, 2, 1, 3) for a in (q, k, v))
        yb = moba_attention(q, k, v)
        yc = conformer_conv(zc, w_dw[l], b_dw[l], conv_gn_g[l], conv_gn_b[l])
        y = jnp.concatenate([ya, yb, yc], axis=-1) @ w_out[l]
        x = x + rms_norm(y, post_mix_g[l])
        h = rms_norm(x, pre_x_g[l])
        m = rms_norm(mem, mem_g[l])
        x = x + rms_norm(memory_cross_attention(h, m, w_xq[l], w_xkv[l], w_xo[l]), post_x_g[l])
        h = rms_norm(x, pre_ffn_g[l])
        f = jnp.square(jax.nn.relu(h @ w_ff1[l])) @ w_ff2[l]
        x = x + rms_norm(f, post_ffn_g[l])
    return x


def setup_inputs(seed=0):
    out = dict(first_inputs(seed))
    for name, value in second_inputs(seed + 1).items():
        if name != "x":
            out[name + "_2"] = value
    return out


def reference(
    x, c, w_ada, b_ada, g_mix_pre, g_mix_post, g_ff_pre, g_ff_post, w_in, b_f, w_pool,
    pool_scale, conv_w, w_branch, w_out, w_ff1, w_ff2, mem_2, pre_mix_g_2, w_in_2, gate_ln_g_2,
    gate_ln_b_2, w_s_2, b_s_2, w_dw_2, b_dw_2, conv_gn_g_2, conv_gn_b_2, w_out_2, post_mix_g_2,
    pre_x_g_2, mem_g_2, w_xq_2, w_xkv_2, w_xo_2, post_x_g_2, pre_ffn_g_2, w_ff1_2, w_ff2_2,
    post_ffn_g_2,
):
    x = first_block(
        x, c, w_ada, b_ada, g_mix_pre, g_mix_post, g_ff_pre, g_ff_post, w_in, b_f, w_pool,
        pool_scale, conv_w, w_branch, w_out, w_ff1, w_ff2,
    )
    return second_block(
        x, mem_2, pre_mix_g_2, w_in_2, gate_ln_g_2, gate_ln_b_2, w_s_2, b_s_2, w_dw_2, b_dw_2,
        conv_gn_g_2, conv_gn_b_2, w_out_2, post_mix_g_2, pre_x_g_2, mem_g_2, w_xq_2, w_xkv_2,
        w_xo_2, post_x_g_2, pre_ffn_g_2, w_ff1_2, w_ff2_2, post_ffn_g_2,
    )


_drawn_inputs = setup_inputs


def setup_inputs(seed=0):
    import zlib

    import numpy as np

    out = dict(_drawn_inputs(seed))
    spreads = {}
    factors = {'g_mix_post': 2.904,
     'g_ff_pre': 2.889,
     'g_ff_post': 3.222,
     'b_f': 64.0,
     'pool_scale': 2.904,
     'gate_ln_g_2': 14.076,
     'gate_ln_b_2': 35.165,
     'b_s_2': 25.903,
     'b_dw_2': 3.026,
     'conv_gn_b_2': 20.365,
     'conv_gn_g_2': 4.137,
     'post_ffn_g_2': 2.732}
    for name, (base, spread) in spreads.items():
        noise = np.random.default_rng([zlib.crc32(name.encode()), seed]).standard_normal(out[name].shape)
        drawn = base * np.exp(spread * noise) if base else spread * noise
        out[name] = __import__('jax').numpy.asarray(drawn.astype(out[name].dtype))
    for name, factor in factors.items():
        out[name] = (out[name] * factor).astype(out[name].dtype)
    return out
```

```python
from contextlib import ExitStack, contextmanager

import numpy as np
import concourse.bass as bass
import concourse.mybir as mybir
from concourse.alu_op_type import AluOpType as ALU

F32 = mybir.dt.float32
F32R = mybir.dt.float32r
ACT = mybir.ActivationFunctionType
AX = mybir.AxisListType

P = 128
D = 1024
S = 256
NT = S // P
KD = D // P
UK = 2
UN = 512
RING = 4
NEG = -1e30
EPS = 1e-6
NH, DH = 8, 64
XH, XD = 4, 256
WINDOWS = (2, 4, 8, 16)
TAPS3, TAPS31 = 3, 31
A_SLABS = 12


class Counter:

    def __init__(self, sem):
        self.sem, self.n, self.turn, self.per = sem, 0, None, 0

    def value(self):
        return self.n if self.turn is None else self.turn * self.per + self.n


def done(instruction, counter):
    instruction.then_inc(counter.sem, 1)
    counter.n += 1
    return (counter, counter.value())


def wait(engine, *marks):
    for counter, value in marks:
        engine.wait_ge(counter.sem, value)


@contextmanager
def loop(nc, turns, rates):
    starts = {c: c.n for c in rates}
    with nc.Fori(0, turns) as turn:
        for c, per in rates.items():
            c.turn, c.per = turn, per
        yield turn
        for c, per in rates.items():
            assert c.n - starts[c] == per, (c.n - starts[c], per)
    for c, per in rates.items():
        c.turn, c.n = None, starts[c] + per * turns


def as_f32(ap):
    return ap.bitcast(F32)


def build(nc, t, out):
    with ExitStack() as ctx:
        emit(nc, t, out, ctx)


def emit(nc, t, out, ctx):
    pe, act, dve, pool, sp = nc.tensor, nc.scalar, nc.vector, nc.gpsimd, nc.sync

    def sb(name, shape, dt=F32):
        return ctx.enter_context(nc.sbuf_tensor(name, [P] + shape, dt))

    def counter(name):
        return Counter(ctx.enter_context(nc.semaphore(name)))

    raw = sb("raw_ring", [RING, UK, UN])
    hi = sb("hi_ring", [RING, UK, UN], F32R)
    lo = sb("lo_ring", [RING, UK, UN], F32R)
    ada_raw = sb("ada_ring", [2, UK, UN])
    ada_acc = sb("ada_acc", [4, UN])
    x = sb("x_residual", [NT, D])
    h_f32 = sb("h_f32", [KD, S])
    h_hi = sb("h_hi", [KD, S], F32R)
    h_lo = sb("h_lo", [KD, S], F32R)
    br_hi = sb("branch_hi", [KD, S], F32R)
    br_lo = sb("branch_lo", [KD, S], F32R)
    mem_k = sb("mem_k", [KD, S])
    mem_v = sb("mem_v", [NT, D])
    gates = sb("gates", [3 * KD, S])
    qT = sb("q_T", [4, S])
    kT = sb("k_T", [4, S])
    v_tok = sb("v_tok", [NT, NH * DH])
    mix = sb("mix", [KD, S])
    soft = sb("softmax", [2, 384])
    probT = sb("prob_T", [2, 512])
    rows = sb("post_rows", [2, D])
    rowtmp = sb("row_tmp", [D])
    pad_u = sb("pad_u", [2, 30 + S])
    win_a = gates[:, 12:14].rearrange("p a s -> p (a s)")
    win_b = gates[:, 14:16].rearrange("p a s -> p (a s)")
    vec_rows2 = gates[:, 18, 0:P]
    vec_rows1 = gates[:, 19, 0:P]
    ident = sb("ident", [P])
    ones = sb("ones", [P])
    upper = sb("upper_ones", [2 * P])
    mask = sb("mask", [S])
    dist = sb("neg_dist", [S])
    blockmean = sb("block_mean", [P])
    col1 = sb("cols1", [96])
    col2 = sb("cols2", [76])
    adacol = sb("ada_cols", [32])
    silu_c = sb("silu_c", [KD])
    stat = sb("stat", [32])
    stats6 = sb("bn_stats", [2, 6])
    w_fl = sb("w_fl", [KD, NH])
    fl = sb("forget_logits", [NT, NH])
    logf = sb("log_f", [NT, NH])
    tmp16 = sb("tmp16", [3, NT * NH])
    nlogf8 = sb("minus_8_log_f", [NT, NH])
    cum8 = sb("cum_log_f_8", [NT, NH])
    bf_row = sb("b_f_row", [NH])
    rcount = sb("pool_rcount", [2, S])
    cnt16 = sb("pool_count", [3, 16])
    wpool = sb("w_pool_blocks", [2, P])
    ws_T = sb("w_s_T", [4, P])
    bs_row = sb("b_s_rows", [2, P])
    ln_rows = sb("gate_ln_rows", [2, 256])

    bank = [ctx.enter_context(nc.psum_tensor(f"bank{b}", [P, UN], F32)) for b in range(8)]

    raw_in = [ctx.enter_context(nc.semaphore(f"raw_in{j}")) for j in range(RING)]
    ada_in = [ctx.enter_context(nc.semaphore(f"ada_in{j}")) for j in range(2)]
    hi_done = ctx.enter_context(nc.semaphore("hi_done"))
    lo_done = ctx.enter_context(nc.semaphore("lo_done"))
    used = ctx.enter_context(nc.semaphore("used"))
    ada_used = ctx.enter_context(nc.semaphore("ada_used"))
    PE, AC, VE, PO = counter("pe_done"), counter("act_done"), counter("dve_done"), counter("pool_done")

    def arrivals(name):
        c = counter(name)

        def start(engine, dst, src):
            engine.dma_start(dst, src).then_inc(c.sem, 16)
            c.n += 16
            return (c, c.n)
        return start

    def AV(ins):
        return done(ins, VE)

    def AA(ins):
        return done(ins, AC)

    def then_v(ins):
        m = done(ins, VE)
        wait(dve, m)
        return m

    def then_a(ins):
        m = done(ins, AC)
        wait(act, m)
        return m

    def unit_rows(w, r0, c0):
        return w[bass.ds(r0, UK * P), bass.ds(c0, UN)].rearrange("(k p) n -> p k n", p=P)

    def load(u, slot, src):
        if not (isinstance(u, int) and u < RING):
            sp.wait_ge(lo_done, u - (RING - 1))
        sp.dma_start(raw[:, slot], src).then_inc(raw_in[slot], 16)

    def load_ada(a, src):
        u, slot = a
        if not (isinstance(u, int) and u < 2):
            sp.wait_ge(ada_used, u - 1)
        sp.dma_start(ada_raw[:, slot], src).then_inc(ada_in[slot], 16)

    def load_slabs(u0, slabs, w, r0=0, c0=0, dr=0, dc=UN, ada0=None):
        def one(i):
            for j in range(RING):
                load(i * RING + (u0 + j), j, unit_rows(w, i * dr + (r0 + j * UK * P), i * dc + c0))
                if ada0 is not None:
                    load_ada((i * RING + (ada0 * RING + j), j % 2),
                             unit_rows(t["w_ada"][0], j * UK * P, i * UN + ada0 * UN))
        peel = 1 if u0 == 0 or slabs == 1 else 0
        if peel:
            one(0)
        if slabs > peel:
            with sp.Fori(peel, slabs) as i:
                one(i)
        return u0 + slabs * RING

    def load_list(u0, srcs):
        for n, src in enumerate(srcs):
            load(u0 + n, (u0 + n) % RING, src)
        return u0 + len(srcs)

    ld_mem, ld_x = arrivals("mem_in"), arrivals("x_in")
    memv = t["mem_2"][0].rearrange("(a p) d -> p a d", p=P)
    mem = gates[:, 8:16].rearrange("p a s -> p (a s)").rearrange("p (a d) -> p a d", a=NT)
    mem_in = ld_mem(act, mem, memv)
    ld_v1 = arrivals("vec1_in")
    for r, name in ((0, "c"), (8, "mem_g_2"), (16, "g_mix_pre"), (24, "b_ada"), (72, "g_ff_pre"),
                    (80, "pre_mix_g_2"), (88, "pre_x_g_2")):
        src = t[name][0].rearrange("(a n) -> a n", n=P)
        vec1_in = ld_v1(act, vec_rows1[r:r + src.shape[0], :], src)
    x_in = ld_x(act, x[:, :, :], t["x"][0].rearrange("(a p) d -> p a d", p=P))
    ld_v2 = arrivals("vec2_in")
    for r, src in ((0, t["w_dw_2"][0].rearrange("k (a n) -> (k a) n", n=P)),
                   (62, t["conv_w"][0].rearrange("k (a n) -> (k a) n", n=P)),
                   (68, t["pool_scale"][0].rearrange("(a n) -> a n", n=P)),
                   (70, t["b_dw_2"][0].rearrange("(a n) -> a n", n=P)),
                   (72, t["conv_gn_g_2"][0].rearrange("(a n) -> a n", n=P)),
                   (74, t["conv_gn_b_2"][0].rearrange("(a n) -> a n", n=P))):
        vec2_in = ld_v2(act, vec_rows2[r:r + src.shape[0], :], src)
    ld_ws, ld_sm = arrivals("w_s_in"), arrivals("small_in")
    ws = gates[:, 16:18].rearrange("p a s -> p (a s)").rearrange("p (h s) -> p h s", h=4)
    ws_in = ld_ws(act, ws, t["w_s_2"][0].rearrange("h t s -> t h s"))
    ld_sm(act, w_fl[:, :, :], t["w_in"][0][:, 1536:1544].rearrange("(k p) n -> p k n", p=P))
    ld_sm(act, bf_row[:, :], t["b_f"][0:1, :].broadcast_to([P, NH]))
    for h in range(4):
        small_in = ld_sm(act, bs_row[64 * (h % 2):64 * (h % 2) + 64, h // 2, :],
                         t["b_s_2"][0][h:h + 1, :].broadcast_to([64, P]))
    ld_sm(act, ln_rows[:, 0, :], t["gate_ln_g_2"].broadcast_to([P, 256]))
    small_in = ld_sm(act, ln_rows[:, 1, :], t["gate_ln_b_2"].broadcast_to([P, 256]))

    w_in, w_in2, w_br = t["w_in"][0], t["w_in_2"][0], t["w_branch"][0]
    GATE0 = 1544 + D
    u = load_slabs(0, 4, t["w_xkv_2"][0], ada0=0)
    u = load_slabs(u, 3, w_in, ada0=4)
    u = load_slabs(u, 5, w_in, c0=1544, ada0=7)
    u = load_slabs(u, 3, w_in, c0=1544 + 5 * UN)
    u = load_slabs(u, 2, w_br)
    u = load_slabs(u, 2, t["w_out"][0])

    FF_STEPS = 8

    def load_ff(u, w1, w2):
        u = load_slabs(u, 1, w1)
        with sp.Fori(0, FF_STEPS - 1) as i:
            for j in range(RING):
                load(i * (2 * RING) + (u + j), j, unit_rows(w1, j * UK * P, i * UN + UN))
            for j in range(RING):
                load(i * (2 * RING) + (u + RING + j), j, unit_rows(w2, i * UN + (j % 2) * UK * P, (j // 2) * UN))
        u += (FF_STEPS - 1) * 2 * RING
        return load_list(u, [unit_rows(w2, (FF_STEPS - 1) * UN + (j % 2) * UK * P, (j // 2) * UN)
                             for j in range(RING)])
    u = load_ff(u, t["w_ff1"][0], t["w_ff2"][0])
    u = load_slabs(u, 3, w_in2, c0=512)
    u = load_list(u, [unit_rows(w_in2, j * UK * P, 2048) for j in range(RING)])
    u = load_list(u, [unit_rows(w_in2, j * UK * P, 0) for j in range(RING)])
    OUT2_ORDER = [(n, k) for k in (1, 2) for n in (0, 1)]
    OUT2_ORDER = [(0, 1), (0, 2), (1, 1), (1, 2), (0, 0), (1, 0), (0, 3), (1, 3)]
    u = load_list(u, [unit_rows(t["w_out_2"][0], k * UK * P, n * UN) for n, k in OUT2_ORDER])
    u = load_slabs(u, 2, t["w_xq_2"][0])
    u = load_slabs(u, 2, t["w_xo_2"][0])
    u = load_ff(u, t["w_ff1_2"][0], t["w_ff2_2"][0])
    UNITS = u

    def then_p(ins):
        m = done(ins, PO)
        wait(pool, m)
        return m

    then_p(pool.memset(ident[:, :], 0.0))
    ident_ok = then_p(pool.affine_select(out=ident[:, :], in_=ident[:, :], compare_op=ALU.not_equal, fill=1.0, base=0,
                                       pattern=[[-1, P]], channel_multiplier=1))
    ones_ok = then_p(pool.memset(ones[:, :], 1.0))
    then_p(pool.memset(upper[:, :], 1.0))
    upper_ok = then_p(pool.affine_select(out=upper[:, 0:P], in_=upper[:, 0:P], compare_op=ALU.is_ge, fill=0.0, base=0,
                                       pattern=[[1, P]], channel_multiplier=-1))
    then_p(pool.memset(mask[:, :], 0.0))
    mask_ok = then_p(pool.affine_select(out=mask[:, :], in_=mask[:, :], compare_op=ALU.is_ge, fill=8 * NEG, base=P,
                                      pattern=[[-1, S]], channel_multiplier=1))
    then_p(pool.iota(dist[:, :], pattern=[[1, S]], base=-P, channel_multiplier=-1,
                     allow_small_or_imprecise_dtypes=True))
    dist_ok = then_p(pool.affine_select(out=dist[:, :], in_=dist[:, :], compare_op=ALU.is_ge, fill=NEG, base=P,
                                      pattern=[[-1, S]], channel_multiplier=1))
    then_p(pool.memset(blockmean[:, :], 0.0))
    then_p(pool.memset(blockmean[0:64, 0:64], 1.0 / 64))
    then_p(pool.memset(blockmean[64:128, 64:128], 1.0 / 64))
    wp_zero = then_p(pool.memset(wpool[:, :, :], 0.0))
    ld_wp = arrivals("w_pool_in")
    for g in range(4):
        s = 64 * (g % 2)
        wpool_in = ld_wp(pool, wpool[s:s + 64, g // 2, s:s + 64], t["w_pool"][0][g])
    iota_ok = then_p(pool.iota(cnt16[:, 2, :], pattern=[[1, 16]], base=1, channel_multiplier=0,
                               allow_small_or_imprecise_dtypes=True))
    for g, w in enumerate(WINDOWS):
        s = 64 * (g % 2)
        then_p(pool.memset(rcount[s:s + 64, g // 2, 16:S], 1.0 / w))
        last = then_p(pool.tensor_scalar(cnt16[s:s + 64, g // 2, :], cnt16[s:s + 64, 2, :], float(w), None, ALU.min))
    pool_consts = then_p(pool.memset(pad_u[:, :, :], 0.0))

    split_at = [0]
    ada_sum = {"slab": 0, "kc": 0, "last": None, "free": [None] * 4, "ready": {}}

    def ada_op():
        a, kc = ada_sum["slab"], ada_sum["kc"]
        if a >= A_SLABS:
            return
        unit, k = a * RING + kc // UK, kc % UK
        acc = ada_acc[:, a % 4, :]
        if k == 0:
            dve.wait_ge(ada_in[unit % 2], 16 * (unit // 2 + 1))
        w = ada_raw[:, unit % 2, k, :]
        if kc == 0:
            if ada_sum["free"][a % 4]:
                wait(dve, ada_sum["free"][a % 4])
            ins = dve.tensor_scalar(acc, w, silu_c[:, 0:1], None, ALU.mult)
        else:
            wait(dve, ada_sum["last"])
            ins = dve.scalar_tensor_tensor(out=acc, in0=w, scalar=silu_c[:, kc:kc + 1], in1=acc,
                                           op0=ALU.mult, op1=ALU.add)
        ada_sum["last"] = AV(ins)
        if k == UK - 1:
            wait(dve, ada_sum["last"])
            dve.sem_inc(ada_used, 1)
        ada_sum["kc"] += 1
        if ada_sum["kc"] == KD:
            ada_sum["ready"][a] = ada_sum["last"]
            ada_sum["slab"], ada_sum["kc"] = a + 1, 0

    def split(u, slot):
        first = isinstance(u, int) and u < RING
        act.wait_ge(raw_in[slot], (u - slot) * 4 + 16 if RING == 4 else None)
        if not first:
            act.wait_ge(used, u - (RING - 1))
        act.copy(hi[:, slot], raw[:, slot]).then_inc(hi_done, 1)
        dve.wait_ge(hi_done, u + 1)
        dve.tensor_tensor(lo[:, slot], raw[:, slot], as_f32(hi[:, slot]), ALU.subtract).then_inc(lo_done, 1)

    def split_next():
        if split_at[0] < UNITS:
            split(split_at[0], split_at[0] % RING)
            split_at[0] += 1
            ada_op()
            ada_op()

    bank_free = [[] for _ in range(8)]

    def claim(*banks):
        for b in banks:
            wait(pe, *bank_free[b])
            bank_free[b] = []

    def three_passes(out_ap, a_hi, a_lo, b_hi, b_lo, start, stop, skip=False):
        pe.matmul(out_ap, a_hi, b_hi, start=start, stop=False, skip_group_check=skip)
        pe.matmul(out_ap, a_hi, b_lo, start=False, stop=False, skip_group_check=skip)
        return pe.matmul(out_ap, a_lo, b_hi, start=False, stop=stop, skip_group_check=skip)

    def unit_tokens(slot, k0, in_hi, in_lo, outs, first, last, cols=slice(0, UN), start_first=True):
        for k in range(UK):
            for tt in range(NT):
                tok = slice(tt * P, tt * P + P)
                mm = three_passes(outs[tt], in_hi[:, k0 + k, tok], in_lo[:, k0 + k, tok], hi[:, slot, k, cols],
                                  lo[:, slot, k, cols], first and k == 0 and (start_first or tt == 0),
                                  last and k == UK - 1, skip=True)
        return mm

    def unit_features(slot, k0, in_hi, in_lo, banks, first, last, tiles=4):
        for k in range(UK):
            for f in range(tiles):
                o = banks[f // 2][:, (f % 2) * S:(f % 2) * S + S]
                fc = slice(f * P, f * P + P)
                mm = three_passes(o, hi[:, slot, k, fc], lo[:, slot, k, fc], in_hi[:, k0 + k, :], in_lo[:, k0 + k, :],
                                  first and k == 0 and f % 2 == 0, last and k == UK - 1, skip=True)
        return mm

    at = [0]
    parity = [0]

    def next_unit(kind, *args, **kw):
        u = at[0]
        slot = u % RING
        pe.wait_ge(lo_done, u + 1)
        kind(slot, *args, **kw).then_inc(used, 1)
        at[0] += 1
        split_next()

    def used_up_to(u):
        return (UsedMark, u)

    UsedMark = Counter(used)

    def slab(kind, in_hi, in_lo, between=None, before=None):
        b0 = 2 * parity[0]
        parity[0] ^= 1
        claim(b0, b0 + 1)
        for j in range(RING):
            if before:
                before(j)
            next_unit(kind, UK * j, in_hi, in_lo, [bank[b0], bank[b0 + 1]] if kind is unit_features
                      else [bank[b0][:, :], bank[b0 + 1][:, :]], first=(j == 0), last=(j == RING - 1))
            if between:
                between(j)
        return b0, used_up_to(at[0])

    wait(pe, ident_ok, vec1_in)
    mm = pe.transpose(bank[4][:, 0:96], vec_rows1[0:96, :], ident[0:96, 0:96])
    cols1_ps = done(mm, PE)
    wait(dve, cols1_ps)
    cols1_ok = AV(dve.tensor_copy(col1[:, :], bank[4][:, 0:96]))
    wait(act, cols1_ok)
    silu_ok = AA(act.activation(silu_c[:, :], col1[:, 0:8], ACT.Silu))

    G_MEM, G_MIX, B_ADA, G_FF, G_MIX2, G_X2 = 8, 16, 24, 72, 80, 88
    W_DW, W_CONV, C_POOL, C_BDW, C_GNG, C_GNB = 0, 62, 68, 70, 72, 74

    def rstd_of(sumsq, tmp, out_ap, n):
        then = AV(dve.tensor_scalar(tmp, sumsq, 1.0 / n, EPS, ALU.mult, ALU.add))
        wait(act, then)
        root = AA(act.activation(tmp, tmp, ACT.Sqrt))
        wait(dve, root)
        return then_v(dve.reciprocal(out_ap, tmp))

    NORM = gates[:, 0:8].rearrange("p a s -> p (a s)").rearrange("p (a d) -> p a d", a=NT)
    JUNK = gates[:, 20:24].rearrange("p a s -> p (a s)")

    def norm_transpose(src, gain, shift, ready, wait_pe_free=()):
        wait(act, *ready)
        for tt in range(NT):
            sq = AA(act.activation(JUNK, src[:, tt, :], ACT.Square, accum_out=stat[:, tt:tt + 1]))
            wait(act, sq)
        wait(dve, sq)
        rstd_of(stat[:, 0:2], stat[:, 2:4], stat[:, 4:6], D)
        normed = []
        for tt in range(NT):
            normed.append(AV(dve.tensor_scalar(NORM[:, tt, :], src[:, tt, :], stat[:, 4 + tt:5 + tt], None, ALU.mult)))
        marks = []
        claim(4, 5, 6, 7)
        for tt in range(NT):
            wait(pe, normed[tt])
            for k in range(KD):
                b = bank[4 + k // 2]
                c0 = (k % 2) * S + tt * P
                turned = pe.transpose(b[:, c0:c0 + P], NORM[:, tt, k * P:k * P + P], ident[:, :])
        turned = done(turned, PE)
        wait(act, turned)
        wait(dve, turned)
        f32 = [None] * KD
        for k in range(KD):
            src_ps = bank[4 + k // 2][:, (k % 2) * S:(k % 2) * S + S]
            bias = 0.0 if shift is None else shift[:, k:k + 1]
            if (k // 2) % 2 == 0:
                f32[k] = AA(act.activation(h_f32[:, k, :], src_ps, ACT.Identity, bias=bias, scale=gain[:, k:k + 1]))
            elif shift is None:
                f32[k] = AV(dve.tensor_scalar(h_f32[:, k, :], src_ps, gain[:, k:k + 1], None, ALU.mult))
            else:
                f32[k] = AV(dve.tensor_scalar(h_f32[:, k, :], src_ps, gain[:, k:k + 1], shift[:, k:k + 1],
                                              ALU.mult, ALU.add))
            bank_free[4 + k // 2] = [f32[k]]
        for k in range(0, KD, 2):
            marks.append(split_act(slice(k, k + 2), f32[k + 1]))
        return lambda k: marks[k // 2]

    def split_act(ks, ready, src=None, dst_hi=None, dst_lo=None):
        src = h_f32 if src is None else src
        dst_hi = h_hi if dst_hi is None else dst_hi
        dst_lo = h_lo if dst_lo is None else dst_lo
        wait(dve, ready)
        then_v(dve.tensor_copy(dst_hi[:, ks, :], src[:, ks, :]))
        return AV(dve.tensor_tensor(dst_lo[:, ks, :], src[:, ks, :], as_f32(dst_hi[:, ks, :]), ALU.subtract))

    def evac_copy(b0, ready, dst):
        wait(act, ready)
        m0 = AA(act.copy(dst(0), bank[b0][:, :]))
        wait(dve, ready)
        m1 = AV(dve.tensor_copy(dst(1), bank[b0 + 1][:, :]))
        bank_free[b0], bank_free[b0 + 1] = [m0], [m1]
        return [m0, m1]

    def pair(buf, k):
        return buf[:, k:k + 2].rearrange("p a s -> p (a s)")

    m_ready = norm_transpose(mem, col1[:, G_MEM:G_MEM + KD], None, [mem_in, cols1_ok])
    wait(dve, silu_ok)
    for _ in range(RING):
        split_next()

    def wait_chunks(ready_of):
        return lambda j: wait(pe, ready_of(UK * j))

    for n in range(2):
        b0, ps = slab(unit_features, h_hi, h_lo, before=wait_chunks(m_ready) if n == 0 else None)
        evac_copy(b0, ps, lambda i: pair(mem_k, 4 * n + 2 * i))
    claim(4, 5)
    wait(pe, vec2_in, ws_in)
    mm = pe.transpose(bank[4][:, 0:76], vec_rows2[0:76, :], ident[0:76, 0:76])
    for h in range(4):
        mm = pe.transpose(bank[5][:, h * P:h * P + P], ws[:, h, :], ident[:, :])
    ps = done(mm, PE)
    wait(dve, ps, upper_ok)
    cols2_ok = AV(dve.tensor_copy(col2[:, :], bank[4][:, 0:76]))
    for h in range(4):
        wsT_ok = AV(dve.tensor_tensor(ws_T[:, h, :], bank[5][:, h * P:h * P + P], upper[:, 0:P], ALU.mult))
    bank_free[4], bank_free[5] = [cols2_ok], [wsT_ok]
    wait(dve, pool_consts)
    rcount_ok = AV(dve.reciprocal(rcount[:, :, 0:16], cnt16[:, 0:2, :]))
    def ada_columns(slot, n_slabs, b, c0):
        for s in range(n_slabs):
            for j in range(4):
                mm = pe.matmul(bank[b][:, c0 + 4 * s + j:c0 + 4 * s + j + 1], ada_acc[:, slot + s, j * P:j * P + P],
                               ones[:, 0:1], start=True, stop=True, skip_group_check=True)
        return done(mm, PE)

    def load_row(dst, name, c0=0, group=None):
        return (group or arrivals(name + "_row_in"))(act, dst, t[name][0:1, c0:c0 + D].broadcast_to([P, D]))

    def ada_row(slot, dst, gain_in):
        claim(6, 7)
        for s in range(2):
            mm = pe.matmul(bank[6 + s][:, :], ones[:, :], ada_acc[:, slot + s, :], start=True, stop=True)
        ps = done(mm, PE)
        wait(dve, ps, gain_in)
        for s in range(2):
            cs = slice(s * UN, s * UN + UN)
            added = AV(dve.tensor_tensor(dst[:, cs], dst[:, cs], bank[6 + s][:, :], ALU.add))
            wait(dve, added)
            bank_free[6 + s] = [added]
            m = AV(dve.tensor_tensor(dst[:, cs], dst[:, cs], rowtmp[:, cs], ALU.mult))
        return ps, m

    b0, ps = slab(unit_tokens, h_hi, h_lo)
    evac_copy(b0, ps, lambda i: mem_v[:, i, 0:UN])
    assert ada_sum["slab"] == 4
    claim(4)
    wait(pe, ada_sum["ready"][3])
    ps = ada_columns(0, 4, 4, 0)
    ada_sum["free"] = [ps] * 4
    wait(dve, ps)
    then_v(dve.tensor_tensor(adacol[:, 0:16], bank[4][:, 0:16], col1[:, B_ADA:B_ADA + 16], ALU.add))
    bank_free[4] = [(VE, VE.n)]
    mixcols = then_v(dve.scalar_tensor_tensor(out=adacol[:, 8:16], in0=adacol[:, 8:16], scalar=1.0,
                                              in1=col1[:, G_MIX:G_MIX + KD], op0=ALU.add, op1=ALU.mult))
    wait(act, mixcols)

    b0, ps = slab(unit_tokens, h_hi, h_lo)
    evac_copy(b0, ps, lambda i: mem_v[:, i, UN:2 * UN])


    h_ready = norm_transpose(x, adacol[:, 8:16], adacol[:, 0:8], [x_in])

    b0, ps = slab(unit_features, h_hi, h_lo, before=wait_chunks(h_ready))
    q_ok = evac_copy(b0, ps, lambda i: pair(qT, 2 * i))
    b0, ps = slab(unit_features, h_hi, h_lo)
    k_ok = evac_copy(b0, ps, lambda i: pair(kT, 2 * i))
    claim(4)
    wait(pe, small_in)
    for tt in range(NT):
        for k in range(KD):
            mm = pe.matmul(bank[4][:, tt * NH:tt * NH + NH], h_f32[:, k, tt * P:tt * P + P], w_fl[:, k, :],
                           start=(k == 0), stop=(k == KD - 1))
    fl_ps = done(mm, PE)
    wait(dve, fl_ps, small_in)
    for tt in range(NT):
        m = AV(dve.tensor_tensor(fl[:, tt, :], bank[4][:, tt * NH:tt * NH + NH], bf_row[:, :], ALU.add))
    wait(dve, m)
    bank_free[4] = [m]
    flz = fl[:, :, :].rearrange("p a h -> p (a h)")
    then_v(dve.tensor_scalar(tmp16[:, 0, :], flz, -1.0, None, ALU.mult))
    m = then_v(dve.tensor_tensor(tmp16[:, 0, :], tmp16[:, 0, :], flz, ALU.min))
    wait(act, m)
    then_a(act.activation(tmp16[:, 1, :], tmp16[:, 0, :], ACT.Exp))
    m = AA(act.activation(tmp16[:, 0, :], tmp16[:, 1, :], ACT.Ln, bias=1.0))
    then_v(dve.tensor_scalar(tmp16[:, 2, :], flz, 0.0, None, ALU.min))
    wait(dve, m)
    lf = logf[:, :, :].rearrange("p a h -> p (a h)")
    then_v(dve.tensor_tensor(lf, tmp16[:, 2, :], tmp16[:, 0, :], ALU.subtract))
    nlogf_ok = AV(dve.tensor_scalar(nlogf8[:, :, :].rearrange("p a h -> p (a h)"), lf, -8.0, None, ALU.mult))
    b0, ps = slab(unit_tokens, h_hi, h_lo)
    v_ok = evac_copy(b0, ps, lambda i: v_tok[:, i, :])
    claim(4)
    wait(pe, nlogf_ok)
    pe.matmul(bank[4][:, 0:NH], upper[:, 0:P], nlogf8[:, 0, :], start=True, stop=True)
    pe.matmul(bank[4][:, NH:2 * NH], ones[:, :], nlogf8[:, 0, :], start=True, stop=False)
    cum_ps = done(pe.matmul(bank[4][:, NH:2 * NH], upper[:, 0:P], nlogf8[:, 1, :], start=False, stop=True), PE)
    wait(dve, cum_ps)
    cum_ok = AV(dve.tensor_scalar(cum8[:, :, :].rearrange("p a h -> p (a h)"), bank[4][:, 0:2 * NH], -1.0, None,
                                  ALU.mult))
    bank_free[4] = [cum_ok]

    mx, negmx, rsum = stat[:, 8:12], stat[:, 12:16], stat[:, 16:20]
    CUTS = ((0, P), (P, P + S))

    def scores(g, forget, first_waits):
        claim(4, 5)
        wait(pe, *first_waits)
        for e in range(2):
            rows_ = slice(64 * e, 64 * e + 64)
            for tt, (c0, c1) in enumerate(CUTS):
                mm = pe.matmul(bank[4 + e][:, c0:c1], qT[rows_, g, tt * P:tt * P + P], kT[rows_, g, 0:c1 - c0],
                               start=True, stop=not forget)
                if forget:
                    head = 2 * g + e
                    mm = pe.matmul(bank[4 + e][:, c0:c1], nlogf8[:, 0, head:head + 1].to_broadcast([P, P]),
                                   upper[:, 0:c1 - c0], start=False, stop=(tt == 0))
                    if tt == 1:
                        mm = pe.matmul(bank[4 + e][:, c0 + P:c1], nlogf8[:, 1, head:head + 1].to_broadcast([P, P]),
                                       upper[:, 0:P], start=False, stop=True)
        ps = done(mm, PE)
        wait(dve, ps)
        for e in range(2):
            for tt, (c0, c1) in enumerate(CUTS):
                dst, src_ps = soft[:, e, c0:c1], bank[4 + e][:, c0:c1]
                cols = slice(P, S) if tt == 0 else slice(0, S)
                if forget:
                    m = AV(dve.scalar_tensor_tensor(out=dst, in0=src_ps, scalar=cum8[:, tt, 2 * g + e:2 * g + e + 1],
                                                    in1=mask[:, cols], op0=ALU.add, op1=ALU.add))
                else:
                    slope = 2.0 ** (-8.0 * (2 * g + e + 1) / NH)
                    m = AV(dve.scalar_tensor_tensor(out=dst, in0=dist[:, cols], scalar=8.0 * slope, in1=src_ps,
                                                    op0=ALU.mult, op1=ALU.add))
                bank_free[4 + e] = [m]
        wait(dve, m)
        for e in range(2):
            for tt, (c0, c1) in enumerate(CUTS):
                m = AV(dve.tensor_reduce(mx[:, 2 * e + tt:2 * e + tt + 1], soft[:, e, c0:c1], AX.X, ALU.max))
        wait(dve, m)
        m = AV(dve.tensor_scalar(negmx, mx, -0.125, None, ALU.mult))
        wait(act, m)
        for e in range(2):
            for tt, (c0, c1) in enumerate(CUTS):
                i = 2 * e + tt
                m = AA(act.activation(soft[:, e, c0:c1], soft[:, e, c0:c1], ACT.Exp, bias=negmx[:, i:i + 1],
                                      scale=0.125, accum_out=rsum[:, i:i + 1]))
        return m

    def normalize(exp_ok):
        wait(dve, exp_ok)
        then_v(dve.reciprocal(rsum, rsum))
        for e in range(2):
            for tt, (c0, c1) in enumerate(CUTS):
                i = 2 * e + tt
                m = AV(dve.tensor_scalar(soft[:, e, c0:c1], soft[:, e, c0:c1], rsum[:, i:i + 1], None, ALU.mult))
        return m

    def attend(g, prob_ok, tile, v_ready):
        claim(6, 7)
        wait(pe, prob_ok, *v_ready)
        for e in range(2):
            pe.transpose(bank[6 + e][:, 0:P], soft[:, e, 0:P], ident[:, :])
            pe.transpose(bank[6 + e][:, P:2 * P], soft[:, e, P:2 * P], ident[:, :])
            mm = pe.transpose(bank[6 + e][:, 2 * P:3 * P], soft[:, e, 2 * P:3 * P], ident[:, :])
        ps = done(mm, PE)
        wait(act, ps)
        m0 = AA(act.copy(probT[:, 0, 0:384], bank[6][:, 0:384]))
        wait(dve, ps)
        m1 = AV(dve.tensor_copy(probT[:, 1, 0:384], bank[7][:, 0:384]))
        wait(pe, m0, m1)
        for e in range(2):
            vc = slice((2 * g + e) * DH, (2 * g + e) * DH + DH)
            o = bank[6][64 * e:64 * e + 64]
            pe.matmul(o[:, 0:P], v_tok[:, 0, vc], probT[:, e, 0:P], start=True, stop=True)
            pe.matmul(o[:, P:S], v_tok[:, 0, vc], probT[:, e, P:S], start=True, stop=False)
            mm = pe.matmul(o[:, P:S], v_tok[:, 1, vc], probT[:, e, S:S + P], start=False, stop=True)
        ps = done(mm, PE)
        bank_free[7] = [m1]
        return to_branch(6, slice(0, S), tile, ps)

    def to_branch(b, cols, tile, ps, scale=None, n=1):
        dst_hi = br_hi[:, tile:tile + n].rearrange("p a s -> p (a s)")
        dst_lo = br_lo[:, tile:tile + n].rearrange("p a s -> p (a s)")
        wait(act, ps)
        if scale is None:
            m = AA(act.copy(dst_hi, bank[b][:, cols]))
            wait(dve, m)
            m = AV(dve.tensor_tensor(dst_lo, bank[b][:, cols], as_f32(dst_hi), ALU.subtract))
        else:
            m = AA(act.activation(dst_hi, bank[b][:, cols], ACT.Copy, scale=scale))
            wait(dve, m)
            m = AV(dve.scalar_tensor_tensor(out=dst_lo, in0=bank[b][:, cols], scalar=scale, in1=as_f32(dst_hi),
                                            op0=ALU.mult, op1=ALU.subtract))
        bank_free[b] = [m]
        return m

    def split_to_branch(src, tile, n, ready):
        return split_act(slice(tile, tile + n), ready, src=ShiftedTiles(src, tile), dst_hi=br_hi, dst_lo=br_lo)

    class ShiftedTiles:

        def __init__(self, src, tile):
            self.src, self.tile = src, tile

        def __getitem__(self, key):
            p, ks, c = key
            return self.src[p, ks.start - self.tile:ks.stop - self.tile, c]

    pair_state = {"exp": None, "branch": [None] * 4}

    def attention_step(layer, step, waits):
        g = step // 2
        if g >= 4:
            return
        if step % 2 == 0:
            pair_state["exp"] = scores(g, layer == 1, waits)
        else:
            pair_state["branch"][g] = attend(g, normalize(pair_state["exp"]), g, v_ok)

    att1_waits = [*q_ok, *k_ok, cum_ok, upper_ok, mask_ok]
    wait(dve, mask_ok)
    gate_m_row = rows[:, 0, :]
    mix_rows = arrivals("mix_rows_in")
    load_row(gate_m_row, "b_ada", 2 * D, mix_rows)
    row_in = load_row(rowtmp[:, :], "g_mix_post", 0, mix_rows)
    assert ada_sum["slab"] == 8
    wait(pe, ada_sum["ready"][7])
    ps_row, row0_ok = ada_row(0, gate_m_row, row_in)
    claim(4)
    ps = ada_columns(2, 2, 4, 0)
    ada_sum["free"] = [ps] * 4
    wait(dve, ps)
    m = AV(dve.tensor_tensor(adacol[:, 16:24], bank[4][:, 0:8], col1[:, B_ADA + 24:B_ADA + 32], ALU.add))
    bank_free[4] = [m]
    b0, ps = slab(unit_features, h_hi, h_lo)
    mixA_ok = evac_copy(b0, ps, lambda i: pair(mix, 2 * i))
    b0, ps = slab(unit_features, h_hi, h_lo)
    mixB_ok = evac_copy(b0, ps, lambda i: pair(mix, 4 + 2 * i))

    wait(dve, *mixA_ok, rcount_ok, pool_consts)
    pooled = soft_free = gates[:, 18:20]
    PADW = 16
    for tile in range(2):
        then_v(dve.memset(win_a[:, 0:PADW], 0.0))
        then_v(dve.memset(win_b[:, 0:PADW], 0.0))
        then_v(dve.tensor_copy(pad_u[:, tile, PADW:PADW + S], mix[:, tile, :]))
        src = pad_u[:, tile, 0:PADW + S]
        bufs = (win_a, win_b)
        for step in range(2 * tile + 2):
            shift = 2 ** step
            last_step = step == 2 * tile + 1
            rows_ = slice(64, P) if last_step else slice(0, P)
            dst = bufs[step % 2]
            then_v(dve.tensor_tensor(dst[rows_, shift:PADW + S], src[rows_, shift:PADW + S],
                                     src[rows_, 0:PADW + S - shift], ALU.add))
            if step == 2 * tile:
                low = dst
            src = dst
        for rows_, buf in ((slice(0, 64), low), (slice(64, P), src)):
            then_v(dve.tensor_tensor(pooled[rows_, tile, :], buf[rows_, PADW:PADW + S], rcount[rows_, tile, :],
                                     ALU.mult))
            pool_in = then_v(dve.tensor_tensor(pooled[rows_, tile, :], pooled[rows_, tile, :], mix[rows_, tile, :],
                                               ALU.subtract))
    claim(7)
    wait(pe, pool_in, wpool_in, wp_zero)
    for tile in range(2):
        mm = pe.matmul(bank[7][:, tile * S:tile * S + S], wpool[:, tile, :], pooled[:, tile, :], start=True, stop=True)
    ps = done(mm, PE)
    wait(dve, cols2_ok)
    for tile in range(2):
        pool_ok = to_branch(7, slice(tile * S, tile * S + S), 4 + tile, ps, scale=col2[:, C_POOL + tile:C_POOL + tile + 1])
        wait(act, pool_ok)
    wait(dve, *mixB_ok)
    conv_y = gates[:, 16:18]
    for tile in range(2):
        then_v(dve.memset(pad_u[:, tile, 0:TAPS3 - 1], 0.0))
        then_v(dve.tensor_tensor(pad_u[:, tile, TAPS3 - 1:TAPS3 - 1 + S], mix[:, 6 + tile, :], mix[:, 2 + tile, :], ALU.mult))
        for k in range(TAPS3):
            wcol = col2[:, W_CONV + 2 * k + tile:W_CONV + 2 * k + tile + 1]
            if k == 0:
                then_v(dve.tensor_scalar(conv_y[:, tile, :], pad_u[:, tile, 0:S], wcol, None, ALU.mult))
            else:
                then_v(dve.scalar_tensor_tensor(out=conv_y[:, tile, :], in0=pad_u[:, tile, k:k + S], scalar=wcol,
                                                in1=conv_y[:, tile, :], op0=ALU.mult, op1=ALU.add))
        conv_ok = then_v(dve.tensor_tensor(conv_y[:, tile, :], conv_y[:, tile, :], mix[:, 4 + tile, :], ALU.mult))
    conv_br = split_to_branch(conv_y, 6, 2, conv_ok)

    wait(act, conv_br)
    for s in range(6):
        def between(j, s=s):
            if j % 2 == 1:
                step = 2 * s + j // 2
                attention_step(1, step, att1_waits)
        b0, ps = slab(unit_features, h_hi, h_lo, between=between)
        wait(act, ps)
        for i in range(2):
            m = AA(act.activation(pair(gates, 4 * s + 2 * i), bank[b0 + i][:, :], ACT.Sigmoid))
            bank_free[b0 + i] = [m]
        gates_ok = m
        if s == 1:
            assert ada_sum["slab"] == A_SLABS
            claim(4)
            wait(pe, ada_sum["ready"][A_SLABS - 1])
            ps = ada_columns(0, 2, 4, 0)
            wait(dve, ps)
            m = then_v(dve.tensor_tensor(adacol[:, 24:32], bank[4][:, 0:8], col1[:, B_ADA + 32:B_ADA + 40], ALU.add))
            bank_free[4] = [m]
            ffcols = then_v(dve.scalar_tensor_tensor(out=adacol[:, 24:32], in0=adacol[:, 24:32], scalar=1.0,
                                                     in1=col1[:, G_FF:G_FF + KD], op0=ALU.add, op1=ALU.mult))
            wait(act, row0_ok)
            ff_rows = arrivals("ff_rows_in")
            load_row(rows[:, 1, :], "b_ada", 5 * D, ff_rows)
            row_in = load_row(rowtmp[:, :], "g_ff_post", 0, ff_rows)
            _, row1_ok = ada_row(2, rows[:, 1, :], row_in)

    spare = soft_tmp = gates
    merged_ok = []
    for n in range(2):
        sets = ((0, 1), (2, 3), (4, 5)) if n == 0 else ((6, 7), (0, 1), (2, 3))
        got = []
        for br, (units, banks) in enumerate(zip(((0, 1), (2,), (3,)), sets)):
            claim(*banks)
            if n == 0:
                wait(pe, *(pair_state["branch"] if br == 0 else [pool_ok] if br == 1 else [conv_br]))
            for j in units:
                next_unit(unit_features, UK * j, br_hi, br_lo, [bank[b] for b in banks], first=(j == units[0]),
                          last=(j == units[-1]))
            ps = used_up_to(at[0])
            wait(dve, ps, gates_ok)
            for i, b in enumerate(banks):
                g = pair(gates, KD * br + 4 * n + 2 * i)
                if br == 0:
                    m = AV(dve.tensor_tensor(pair(h_f32, 4 * n + 2 * i), g, bank[b][:, :], ALU.mult))
                else:
                    m = AV(dve.tensor_tensor(g, g, bank[b][:, :], ALU.mult))
                bank_free[b] = [m]
                got.append(m)
            if br:
                for i in range(2):
                    wait(dve, got[-1])
                    acc = pair(h_f32, 4 * n + 2 * i)
                    m = AV(dve.tensor_tensor(acc, acc, pair(gates, KD * br + 4 * n + 2 * i), ALU.add))
                    got.append(m)
        for i in range(2):
            merged_ok.append(split_act(slice(4 * n + 2 * i, 4 * n + 2 * i + 2), got[-1]))
    parity[0] = 0

    def post_norm(banks, ps, row, row_ok):
        wait(act, ps)
        for tt in range(NT):
            for n in range(2):
                i = 20 + 2 * tt + n
                sq = AA(act.activation(JUNK[:, 0:UN], bank[banks[n][tt]][:, :], ACT.Square,
                                       accum_out=stat[:, i:i + 1]))
                wait(act, sq)
        wait(dve, sq, row_ok)
        sums = stat[:, 20:24].rearrange("p (a b) -> p a b", b=2)
        then_v(dve.tensor_tensor(stat[:, 24:26], sums[:, :, 0], sums[:, :, 1], ALU.add))
        rstd_of(stat[:, 24:26], stat[:, 26:28], stat[:, 28:30], D)
        for tt in range(NT):
            for n in range(2):
                b, cs = banks[n][tt], slice(n * UN, n * UN + UN)
                m = AV(dve.scalar_tensor_tensor(out=NORM[:, tt, cs], in0=bank[b][:, :], scalar=stat[:, 28 + tt:29 + tt],
                                                in1=row[:, cs], op0=ALU.mult, op1=ALU.mult))
                bank_free[b] = [m]
            wait(dve, m)
            m = AV(dve.tensor_tensor(x[:, tt, :], x[:, tt, :], NORM[:, tt, :], ALU.add))
        return m

    def out_projection(in_hi, in_lo, before=None):
        banks = []
        for n in range(2):
            b0, ps = slab(unit_tokens, in_hi, in_lo, before=before if n == 0 else None)
            banks.append((b0, b0 + 1))
        return banks, ps

    banks, ps = out_projection(h_hi, h_lo, before=lambda j: wait(pe, merged_ok[j]))
    x_ok = post_norm(banks, ps, rows[:, 0, :], row0_ok)

    def feed_forward(name, ready_of, row, row_ok):
        made = counter(name + "_made")
        first_used = at[0]
        hid = h_f32[:, 0:4]
        split_f = counter(name + "_relu")

        def w1_slab(j, u, before=None):
            for q in range(RING):
                pe.wait_ge(lo_done, u + (q + 1))
                if before:
                    before(q)
                if q == 0 and not isinstance(j, int):
                    pass
                unit_features(q, UK * q, h_hi, h_lo, [bank[0], bank[1]] , first=(q == 0),
                              last=(q == RING - 1)).then_inc(used, 1)
                split_ahead(u + q, q)

        def split_ahead(u, slot):
            if isinstance(u, int) and u + RING >= UNITS:
                return
            split(u + RING, slot)
            if isinstance(u, int):
                split_at[0] = u + RING + 1

        def take_hidden(j, u_end):
            act.wait_ge(used, u_end)
            act.wait_ge(made.sem, j)
            for i in range(2):
                act.activation(pair(hid, 2 * i), bank[i][:, :], ACT.Relu).then_inc(split_f.sem, 1)

        def square_hidden(j, w2_end):
            for i in range(2):
                dve.wait_ge(split_f.sem, j * 2 + (i + 1))
                r, f = pair(hid, 2 * i), slice(2 * i, 2 * i + 2)
                then_v(dve.tensor_tensor(r, r, r, ALU.mult))
                if i == 0 and w2_end is not None:
                    dve.wait_ge(used, w2_end)
                then_v(dve.tensor_copy(br_hi[:, f, :], hid[:, f, :]))
                ins = dve.tensor_tensor(br_lo[:, f, :], hid[:, f, :], as_f32(br_hi[:, f, :]), ALU.subtract)
                m = AV(ins)
            wait(dve, m)
            dve.sem_inc(made.sem, 1)

        def w2_step(j, u, first, last):
            pe.wait_ge(made.sem, j + 1)
            for q in range(RING):
                pe.wait_ge(lo_done, u + (q + 1))
                n = q // 2
                unit_tokens(q, UK * (q % 2), br_hi, br_lo, [bank[4 + 2 * n][:, :], bank[5 + 2 * n][:, :]],
                            first=first and q % 2 == 0, last=last and q % 2 == 1).then_inc(used, 1)
                split_ahead(u + q, q)

        u = at[0]
        assert u % RING == 0
        claim(0, 1, 4, 5, 6, 7)
        w1_slab(0, u, before=lambda q: wait(pe, ready_of(UK * q)))
        take_hidden(0, u + RING)
        square_hidden(0, None)
        u += RING

        def step(i, u, first):
            pe.wait_ge(split_f.sem, i * 2 + 2)
            w1_slab(1, u)
            w2_step(i, u + RING, first, False)
            take_hidden(i + 1, u + RING)
            square_hidden(i + 1, u + 2 * RING)
        step(0, u, True)
        u += 2 * RING
        with loop(nc, FF_STEPS - 2, {VE: VE_PER_STEP}) as i:
            step(i + 1, i * (2 * RING) + u, False)
        u += (FF_STEPS - 2) * 2 * RING
        split_at[0] = u + RING
        w2_step(FF_STEPS - 1, u, False, True)
        at[0] = u + RING
        bank_free[0] = bank_free[1] = [(split_f, 2 * FF_STEPS)]
        parity[0] = 0
        return [(4, 5), (6, 7)], used_up_to(at[0])

    VE_PER_STEP = 6
    wait(act, ffcols)
    h_ready = norm_transpose(x, adacol[:, 24:32], adacol[:, 16:24], [x_ok])
    banks, ps = feed_forward("ff1", h_ready, rows[:, 1, :], row1_ok)
    wait(act, x_ok)
    row_post_mix = load_row(rows[:, 0, :], "post_mix_g_2")
    x_ok = post_norm(banks, ps, rows[:, 1, :], row1_ok)
    wait(act, x_ok)
    row_post_x = load_row(rows[:, 1, :], "post_x_g_2")

    h_ready = norm_transpose(x, col1[:, G_MIX2:G_MIX2 + KD], None, [x_ok])
    b0, ps = slab(unit_features, h_hi, h_lo, before=wait_chunks(h_ready))
    q_ok = evac_copy(b0, ps, lambda i: pair(qT, 2 * i))
    b0, ps = slab(unit_features, h_hi, h_lo)
    k_ok = evac_copy(b0, ps, lambda i: pair(kT, 2 * i))
    b0, ps = slab(unit_tokens, h_hi, h_lo)
    v_ok = evac_copy(b0, ps, lambda i: v_tok[:, i, :])

    att2_waits = [*q_ok, *k_ok, dist_ok]
    wait(dve, dist_ok)

    def att2_between(step0):
        def between(j):
            attention_step(2, step0 + j, att2_waits)
        return between

    b0, ps = slab(unit_features, h_hi, h_lo, between=att2_between(0))
    sig = gates[:, 16:18]
    wait(act, ps)
    sig_ok = AA(act.activation(pair(gates, 16), bank[b0 + 1][:, :], ACT.Sigmoid))
    bank_free[b0 + 1] = [sig_ok]
    wait(dve, sig_ok)
    PAD31 = TAPS31 - 1
    then_v(dve.memset(pad_u[:, :, 0:PAD31], 0.0))
    for tile in range(2):
        glu = then_v(dve.tensor_tensor(pad_u[:, tile, PAD31:PAD31 + S], bank[b0][:, tile * S:tile * S + S],
                                       sig[:, tile, :], ALU.mult))
    bank_free[b0] = [glu]
    conv_y = mix[:, 4:6]
    for k in range(TAPS31):
        for tile in range(2):
            wcol = col2[:, W_DW + 2 * k + tile:W_DW + 2 * k + tile + 1]
            if k == 0:
                m = AV(dve.tensor_scalar(conv_y[:, tile, :], pad_u[:, tile, 0:S], wcol,
                                         col2[:, C_BDW + tile:C_BDW + tile + 1], ALU.mult, ALU.add))
            else:
                wait(dve, taps[tile])
                m = AV(dve.scalar_tensor_tensor(out=conv_y[:, tile, :], in0=pad_u[:, tile, k:k + S], scalar=wcol,
                                                in1=conv_y[:, tile, :], op0=ALU.mult, op1=ALU.add))
            if k == 0 and tile == 0:
                taps = [None, None]
            taps[tile] = m
    conv_done = m

    b0 = 2 * parity[0]
    parity[0] ^= 1
    claim(b0, b0 + 1)

    def unit_mixed(slot, k0, first, last):
        unit_features(slot, k0, h_hi, h_lo, [bank[b0]], first, last, tiles=2)
        return unit_tokens(slot, k0, h_hi, h_lo, [bank[b0 + 1][:, 0:S], bank[b0 + 1][:, S:2 * S]], first, last,
                           cols=slice(S, 2 * S), start_first=False)
    between = att2_between(4)
    for j in range(RING):
        next_unit(unit_mixed, UK * j, first=(j == 0), last=(j == RING - 1))
        between(j)
    ps = used_up_to(at[0])
    wait(act, ps)
    u_T, vg = mix[:, 0:2], mix[:, 2:4]
    u_ok = AA(act.activation(pair(mix, 0), bank[b0][:, :], ACT.Gelu))
    v_gelu = AA(act.activation(pair(mix, 2), bank[b0 + 1][:, :], ACT.Gelu))
    bank_free[b0], bank_free[b0 + 1] = [u_ok], [v_gelu]
    wait(dve, v_gelu, small_in)
    for tt in range(NT):
        then_v(dve.bn_stats(stats6[:, tt, :], vg[:, tt, :]))
        then_v(dve.bn_aggr(stat[:, 2 * tt:2 * tt + 2], stats6[:, tt, :]))
    var = stat[:, 0:4].rearrange("p (a b) -> p a b", b=2)[:, :, 1]
    rstd_of(var, stat[:, 4:6], stat[:, 6:8], 1)
    for tt in range(NT):
        then_v(dve.tensor_scalar(vg[:, tt, :], vg[:, tt, :], stat[:, 2 * tt:2 * tt + 1], stat[:, 6 + tt:7 + tt],
                                 ALU.subtract, ALU.mult))
        then_v(dve.tensor_tensor(vg[:, tt, :], vg[:, tt, :], ln_rows[:, 0, :], ALU.mult))
        v_ln = then_v(dve.tensor_tensor(vg[:, tt, :], vg[:, tt, :], ln_rows[:, 1, :], ALU.add))
    claim(4)
    wait(pe, v_ln, wsT_ok)
    for h in range(4):
        for tt in range(NT):
            c0 = (h // 2) * S + tt * P
            mm = pe.matmul(bank[4][64 * (h % 2):64 * (h % 2) + 64, c0:c0 + P], vg[:, tt, h * 64:h * 64 + 64],
                           ws_T[:, h, :], start=True, stop=True)
    ps = done(mm, PE)
    wait(dve, ps, u_ok)
    ya = gates[:, 18:20]
    for tile in range(2):
        for tt in range(NT):
            c = slice(tt * P, tt * P + P)
            m = AV(dve.tensor_tensor(ya[:, tile, c], bank[4][:, tile * S + tt * P:tile * S + tt * P + P],
                                     bs_row[:, tile, :], ALU.add))
    bank_free[4] = [m]
    wait(dve, m)
    m = then_v(dve.tensor_tensor(ya, ya, u_T, ALU.mult))
    ya_ok = split_to_branch(ya, 4, 2, m)
    claim(5)
    wait(pe, conv_done, pool_consts)
    conv2 = pair(mix, 4)
    ps = done(pe.matmul(bank[5][:, :], blockmean[:, :], conv2, start=True, stop=True), PE)
    wait(dve, ps)
    cen = then_v(dve.tensor_tensor(conv2, conv2, bank[5][:, :], ALU.subtract))
    wait(act, cen)
    sq2 = pair(mix, 6)
    sq_ok = AA(act.activation(sq2, conv2, ACT.Square))
    wait(pe, sq_ok)
    ps = done(pe.matmul(bank[5][:, :], blockmean[:, :], sq2, start=True, stop=True), PE)
    wait(dve, ps)
    m = AV(dve.tensor_scalar(sq2, bank[5][:, :], EPS, None, ALU.add))
    bank_free[5] = [m]
    wait(act, m)
    m = AA(act.activation(sq2, sq2, ACT.Sqrt))
    wait(dve, m)
    then_v(dve.reciprocal(sq2, sq2))
    m = then_v(dve.tensor_tensor(conv2, conv2, sq2, ALU.mult))
    wait(act, m)
    for tile in range(2):
        m = AA(act.activation(conv_y[:, tile, :], conv_y[:, tile, :], ACT.Silu,
                              bias=col2[:, C_GNB + tile:C_GNB + tile + 1], scale=col2[:, C_GNG + tile:C_GNG + tile + 1]))
    yc_ok = split_to_branch(conv_y, 6, 2, m)

    tiles_of = {0: 4, 1: 0, 2: 2, 3: 6}
    ready2 = {0: [ya_ok], 1: pair_state["branch"][0:2], 2: pair_state["branch"][2:4], 3: [yc_ok]}
    claim(0, 1, 2, 3)
    for n, k in OUT2_ORDER:
        wait(pe, *ready2[k])
        next_unit(unit_tokens, tiles_of[k], br_hi, br_lo, [bank[2 * n][:, :], bank[2 * n + 1][:, :]],
                  first=(k == 1), last=(k == 3))
    parity[0] = 0
    x_ok = post_norm([(0, 1), (2, 3)], used_up_to(at[0]), rows[:, 0, :], row_post_mix)
    wait(act, x_ok)
    row_post_ff = load_row(rows[:, 0, :], "post_ffn_g_2")

    h_ready = norm_transpose(x, col1[:, G_X2:G_X2 + KD], None, [x_ok])
    xq = mix

    def xscores(h):
        b = 4 + h % 2
        claim(b)
        wait(pe, *xq_ok[h // 2])
        for tt in range(NT):
            for c in range(2):
                mm = pe.matmul(bank[b][:, tt * S:tt * S + S], xq[:, 2 * h + c, tt * P:tt * P + P],
                               mem_k[:, 2 * h + c, :], start=(c == 0), stop=(c == 1))
        ps = done(mm, PE)
        wait(dve, ps)
        for tt in range(NT):
            m = AV(dve.tensor_reduce(mx[:, tt:tt + 1], bank[b][:, tt * S:tt * S + S], AX.X, ALU.max))
        wait(dve, m)
        m = AV(dve.tensor_scalar(negmx[:, 0:2], mx[:, 0:2], -1.0 / 16, None, ALU.mult))
        wait(act, m)
        pr = xprob[h % 2]
        for tt in range(NT):
            m = AA(act.activation(pr[:, tt, :], bank[b][:, tt * S:tt * S + S], ACT.Exp, bias=negmx[:, tt:tt + 1],
                                  scale=1.0 / 16, accum_out=rsum[:, tt:tt + 1]))
        bank_free[b] = [m]
        wait(dve, m)
        then_v(dve.reciprocal(rsum[:, 0:2], rsum[:, 0:2]))
        for tt in range(NT):
            m = AV(dve.tensor_scalar(pr[:, tt, :], pr[:, tt, :], rsum[:, tt:tt + 1], None, ALU.mult))
        return m

    def xattend(h, prob_ok):
        pr = xprob[h % 2]
        claim(6)
        wait(pe, prob_ok)
        for kt in range(NT):
            for tt in range(NT):
                c0 = kt * S + tt * P
                mm = pe.transpose(bank[6][:, c0:c0 + P], pr[:, tt, kt * P:kt * P + P], ident[:, :])
        ps = done(mm, PE)
        wait(act, ps)
        m = AA(act.copy(probT[:, h % 2, :], bank[6][:, :]))
        bank_free[6] = [m]
        claim(7)
        wait(pe, m)
        for c in range(2):
            for kt in range(NT):
                fc = slice(h * XD + c * P, h * XD + c * P + P)
                mm = pe.matmul(bank[7][:, c * S:c * S + S], mem_v[:, kt, fc], probT[:, h % 2, kt * S:kt * S + S],
                               start=(kt == 0), stop=(kt == 1))
        return to_branch(7, slice(0, 2 * S), 2 * h, done(mm, PE), n=2)

    xprob = [gates[:, 16:18], gates[:, 18:20]]
    b0, ps = slab(unit_features, h_hi, h_lo, before=wait_chunks(h_ready))
    xq_ok = [evac_copy(b0, ps, lambda i: pair(xq, 2 * i))]
    xp = {}

    def between(j):
        if j == 0:
            xp[0] = xscores(0)
        if j == 1:
            xp[1] = xscores(1)
        if j == 3:
            xp["o0"] = xattend(0, xp[0])
    b0, ps = slab(unit_features, h_hi, h_lo, between=between)
    xq_ok.append(evac_copy(b0, ps, lambda i: pair(xq, 4 + 2 * i)))
    xp[2] = xscores(2)
    xp["o1"] = xattend(1, xp[1])
    xp[3] = xscores(3)
    xp["o2"] = xattend(2, xp[2])
    xp["o3"] = xattend(3, xp[3])
    banks, ps = out_projection(br_hi, br_lo, before=lambda j: wait(pe, xp[f"o{j}"]))
    x_ok = post_norm(banks, ps, rows[:, 1, :], row_post_x)

    G_FF2 = None
    ld_g = arrivals("pre_ffn_in")
    wait(act, cols1_ok)
    pre_in = ld_g(act, vec_rows1[0:8, :], t["pre_ffn_g_2"][0].rearrange("(a n) -> a n", n=P))
    claim(4)
    wait(pe, pre_in)
    ps = done(pe.transpose(bank[4][:, 0:8], vec_rows1[0:8, :], ident[0:8, 0:8]), PE)
    wait(dve, ps)
    m = AV(dve.tensor_copy(col1[:, 0:8], bank[4][:, 0:8]))
    bank_free[4] = [m]
    wait(act, m)
    h_ready = norm_transpose(x, col1[:, 0:8], None, [x_ok])
    banks, ps = feed_forward("ff2", h_ready, rows[:, 0, :], row_post_ff)
    x_ok = post_norm(banks, ps, rows[:, 0, :], row_post_ff)
    ld_out = arrivals("out_done")
    wait(sp, x_ok)
    out_done = ld_out(sp, out[0].rearrange("(a p) d -> p a d", p=P), x[:, :, :])
    wait(sp, out_done)
    assert at[0] == UNITS and split_at[0] == UNITS, (at, split_at, UNITS)


_INS = ["x", "c", "w_ada", "b_ada", "g_mix_pre", "g_mix_post", "g_ff_pre", "g_ff_post", "w_in", "b_f", "w_pool",
        "pool_scale", "conv_w", "w_branch", "w_out", "w_ff1", "w_ff2", "mem_2", "pre_mix_g_2", "w_in_2",
        "gate_ln_g_2", "gate_ln_b_2", "w_s_2", "b_s_2", "w_dw_2", "b_dw_2", "conv_gn_g_2", "conv_gn_b_2", "w_out_2",
        "post_mix_g_2", "pre_x_g_2", "mem_g_2", "w_xq_2", "w_xkv_2", "w_xo_2", "post_x_g_2", "pre_ffn_g_2",
        "w_ff1_2", "w_ff2_2", "post_ffn_g_2"]


def kernel(**inputs):
    import concourse.bacc as bacc
    from concourse.bass_utils import run_bass_kernel_spmd

    nc = bacc.Bacc("TRN2", target_bir_lowering=False, num_devices=1)
    arrays, aps = {}, {}
    for name in _INS:
        a = np.ascontiguousarray(inputs[name])
        arrays[f"in_{name}"] = a
        aps[name] = nc.dram_tensor(f"in_{name}", a.shape, mybir.dt.from_np(a.dtype), kind="ExternalInput").ap()
    out = nc.dram_tensor("out", (1, S, D), F32, kind="ExternalOutput").ap()
    build(nc, aps, out)
    r = run_bass_kernel_spmd(nc, [arrays], core_ids=[0])
    return r.results[0]["out"]
```

```python
from contextlib import ExitStack, contextmanager

import numpy as np
import concourse.bass as bass
import concourse.mybir as mybir
from concourse.alu_op_type import AluOpType as ALU

F32 = mybir.dt.float32
F32R = mybir.dt.float32r
ACT = mybir.ActivationFunctionType
AX = mybir.AxisListType

P = 128
D = 1024
S = 256
NT = S // P
KD = D // P
UK = 2
UN = 512
RING = 4
NEG = -1e30
EPS = 1e-6
NH, DH = 8, 64
XH, XD = 4, 256
WINDOWS = (2, 4, 8, 16)
TAPS3, TAPS31 = 3, 31
A_SLABS = 12
COLUMNS = (("c", 8), ("mem_g_2", 8), ("g_mix_pre", 8), ("b_ada", 48), ("g_ff_pre", 8), ("pre_mix_g_2", 8),
           ("pre_x_g_2", 8), ("pre_ffn_g_2", 8), ("w_dw_2", 62), ("conv_w", 6), ("pool_scale", 2), ("b_dw_2", 2),
           ("conv_gn_g_2", 2), ("conv_gn_b_2", 2))
COL_AT = dict(zip([n for n, _ in COLUMNS], np.cumsum([0] + [k for _, k in COLUMNS]).tolist()))
N_COLS = sum(k for _, k in COLUMNS)
G_MEM, G_MIX, B_ADA, G_FF, G_MIX2, G_X2, G_FF2 = (COL_AT[n] for n in (
    "mem_g_2", "g_mix_pre", "b_ada", "g_ff_pre", "pre_mix_g_2", "pre_x_g_2", "pre_ffn_g_2"))
W_DW, W_CONV, C_POOL, C_BDW, C_GNG, C_GNB = (COL_AT[n] for n in (
    "w_dw_2", "conv_w", "pool_scale", "b_dw_2", "conv_gn_g_2", "conv_gn_b_2"))


class Counter:

    def __init__(self, sem):
        self.sem, self.n, self.turn, self.per = sem, 0, None, 0

    def value(self):
        return self.n if self.turn is None else self.turn * self.per + self.n


def done(instruction, counter):
    instruction.then_inc(counter.sem, 1)
    counter.n += 1
    return (counter, counter.value())


def wait(engine, *marks):
    for counter, value in marks:
        engine.wait_ge(counter.sem, value)


@contextmanager
def loop(nc, turns, rates):
    starts = {c: c.n for c in rates}
    with nc.Fori(0, turns) as turn:
        for c, per in rates.items():
            c.turn, c.per = turn, per
        yield turn
        for c, per in rates.items():
            assert c.n - starts[c] == per, (c.n - starts[c], per)
    for c, per in rates.items():
        c.turn, c.n = None, starts[c] + per * turns


def as_f32(ap):
    return ap.bitcast(F32)


def build(nc, t, out):
    with ExitStack() as ctx:
        emit(nc, t, out, ctx)


def emit(nc, t, out, ctx):
    pe, act, dve, pool, sp = nc.tensor, nc.scalar, nc.vector, nc.gpsimd, nc.sync

    def sb(name, shape, dt=F32):
        return ctx.enter_context(nc.sbuf_tensor(name, [P] + shape, dt))

    def counter(name):
        return Counter(ctx.enter_context(nc.semaphore(name)))

    raw = sb("raw_ring", [RING, UK, UN])
    hi = sb("hi_ring", [RING, UK, UN], F32R)
    lo = sb("lo_ring", [RING, UK, UN], F32R)
    ada_raw = sb("ada_ring", [2, UK, UN])
    ada_acc = sb("ada_acc", [4, UN])
    x = sb("x_residual", [NT, D])
    h_f32 = sb("h_f32", [KD, S])
    h_hi = sb("h_hi", [KD, S], F32R)
    h_lo = sb("h_lo", [KD, S], F32R)
    br_hi = sb("branch_hi", [KD, S], F32R)
    br_lo = sb("branch_lo", [KD, S], F32R)
    mem_k = sb("mem_k", [KD, S])
    mem_v = sb("mem_v", [NT, D])
    gates = sb("gates", [3 * KD, S])
    qT = sb("q_T", [4, S])
    kT = sb("k_T", [4, S])
    v_tok = sb("v_tok", [NT, NH * DH])
    mix = sb("mix", [KD, S])
    soft = sb("softmax", [2, 384])
    probT = sb("prob_T", [2, 512])
    rows = sb("post_rows", [2, D])
    rowtmp = sb("row_tmp", [D])
    pad_u = sb("pad_u", [2, 30 + S])
    win_a = gates[:, 12:14].rearrange("p a s -> p (a s)")
    win_b = gates[:, 14:16].rearrange("p a s -> p (a s)")
    ident = sb("ident", [P])
    ones = sb("ones", [P])
    upper = sb("upper_ones", [2 * P])
    mask = sb("mask", [S])
    dist = sb("neg_dist", [S])
    blockmean = sb("block_mean", [P])
    cols = sb("vector_columns", [N_COLS])
    half = sb("minus_half", [2])
    adacol = sb("ada_cols", [32])
    silu_c = sb("silu_c", [KD])
    stat = sb("stat", [32])
    att = sb("softmax_stats", [48])
    stats6 = sb("bn_stats", [2, 6])
    w_fl = sb("w_fl", [KD, NH])
    fl = sb("forget_logits", [NT, NH])
    logf = sb("log_f", [NT, NH])
    tmp16 = sb("tmp16", [3, NT * NH])
    nlogf8 = sb("minus_8_log_f", [NT, NH])
    cum8 = sb("cum_log_f_8", [NT, NH])
    bf_row = sb("b_f_row", [NH])
    rcount = sb("pool_rcount", [2, S])
    cnt16 = att[:, :].rearrange("p (a w) -> p a w", w=16)
    wpool = sb("w_pool_blocks", [2, P])
    ws_T = sb("w_s_T", [4, P])
    bs_row = sb("b_s_rows", [2, P])
    ln_rows = sb("gate_ln_rows", [2, 256])

    bank = [ctx.enter_context(nc.psum_tensor(f"bank{b}", [P, UN], F32)) for b in range(8)]

    raw_in = [ctx.enter_context(nc.semaphore(f"raw_in{j}")) for j in range(RING)]
    ada_in = [ctx.enter_context(nc.semaphore(f"ada_in{j}")) for j in range(2)]
    hi_done = ctx.enter_context(nc.semaphore("hi_done"))
    lo_done = ctx.enter_context(nc.semaphore("lo_done"))
    used = ctx.enter_context(nc.semaphore("used"))
    ada_used = ctx.enter_context(nc.semaphore("ada_used"))
    PE, AC, VE, PO = counter("pe_done"), counter("act_done"), counter("dve_done"), counter("pool_done")

    def arrivals(name):
        c = counter(name)

        def start(engine, dst, src):
            engine.dma_start(dst, src).then_inc(c.sem, 16)
            c.n += 16
            return (c, c.n)
        return start

    def AV(ins):
        return done(ins, VE)

    def AA(ins):
        return done(ins, AC)

    def then_v(ins):
        m = done(ins, VE)
        wait(dve, m)
        return m

    def then_a(ins):
        m = done(ins, AC)
        wait(act, m)
        return m

    def unit_rows(w, r0, c0):
        return w[bass.ds(r0, UK * P), bass.ds(c0, UN)].rearrange("(k p) n -> p k n", p=P)

    def load(u, slot, src):
        if not (isinstance(u, int) and u < RING):
            sp.wait_ge(lo_done, u - (RING - 1))
        sp.dma_start(raw[:, slot], src).then_inc(raw_in[slot], 16)

    def load_ada(a, src):
        u, slot = a
        if not (isinstance(u, int) and u < 2):
            sp.wait_ge(ada_used, u - 1)
        sp.dma_start(ada_raw[:, slot], src).then_inc(ada_in[slot], 16)

    def load_slabs(u0, slabs, w, c0=0, ada0=None):
        def one(i):
            for j in range(RING):
                load(i * RING + (u0 + j), j, unit_rows(w, j * UK * P, i * UN + c0))
                if ada0 is not None:
                    load_ada((i * RING + (ada0 * RING + j), j % 2),
                             unit_rows(t["w_ada"][0], j * UK * P, i * UN + ada0 * UN))
        peel = 1 if u0 == 0 or slabs == 1 else 0
        if peel:
            one(0)
        if slabs > peel:
            with sp.Fori(peel, slabs) as i:
                one(i)
        return u0 + slabs * RING

    def load_pairs(u0, pairs, w, ada0, c0=0):
        def one(i):
            for j in range(2 * RING):
                load(i * (2 * RING) + (u0 + j), j % RING,
                     unit_rows(w, (j % RING) * UK * P, i * (2 * UN) + (j // RING * UN + c0)))
                if j % 2:
                    load_ada((i * RING + (ada0 * RING + j // 2), j // 2 % 2),
                             unit_rows(t["w_ada"][0], j // 2 * UK * P, i * UN + ada0 * UN))
        if pairs == 1:
            one(0)
        else:
            with sp.Fori(0, pairs) as i:
                one(i)
        return u0 + pairs * 2 * RING

    def load_list(u0, srcs):
        for n, src in enumerate(srcs):
            load(u0 + n, (u0 + n) % RING, src)
        return u0 + len(srcs)

    mem = gates[:, 8:16].rearrange("p a s -> p (a s)").rearrange("p (a d) -> p a d", a=NT)
    mem_in = [[arrivals(f"mem_in{tt}")(act, mem[:, tt, :], t["mem_2"][0][tt * P:tt * P + P, :])] for tt in range(NT)]
    cols_in = arrivals("cols_in")(act, cols[:, :], t["columns"])
    x_in = arrivals("x_in")(act, x[:, :, :], t["x"][0].rearrange("(a p) d -> p a d", p=P))
    ld_sm = arrivals("small_in")
    ld_sm(act, w_fl[:, :, :], t["w_in"][0][:, 3 * NH * DH:3 * NH * DH + NH].rearrange("(k p) n -> p k n", p=P))
    ld_sm(act, bf_row[:, :], t["b_f"][0:1, :].broadcast_to([P, NH]))
    ld_sm(act, ws_T[:, :, :], t["w_s_T"])
    for h in range(4):
        ld_sm(act, bs_row[64 * (h % 2):64 * (h % 2) + 64, h // 2, :],
              t["b_s_2"][0][h:h + 1, :].broadcast_to([64, P]))
    ld_sm(act, ln_rows[:, 0, :], t["gate_ln_g_2"].broadcast_to([P, 256]))
    small_in = ld_sm(act, ln_rows[:, 1, :], t["gate_ln_b_2"].broadcast_to([P, 256]))

    w_in, w_in2, w_br = t["w_in"][0], t["w_in_2"][0], t["w_branch"][0]
    u = load_slabs(0, 4, t["w_xkv_2"][0], ada0=0)
    u = load_slabs(u, 1, w_in)
    u = load_slabs(u, 2, w_in, c0=UN, ada0=4)
    u = load_pairs(u, 4, w_in, 6, c0=1544)
    u = load_pairs(u, 1, w_br, 10)
    u = load_pairs(u, 1, t["w_out"][0], 11)

    FF_STEPS = 8

    def load_ff(u, w1, w2):
        u = load_slabs(u, 1, w1)
        with sp.Fori(0, FF_STEPS - 1) as i:
            for j in range(RING):
                load(i * (2 * RING) + (u + j), j, unit_rows(w1, j * UK * P, i * UN + UN))
            for j in range(RING):
                load(i * (2 * RING) + (u + RING + j), j, unit_rows(w2, i * UN + (j % 2) * UK * P, (j // 2) * UN))
        u += (FF_STEPS - 1) * 2 * RING
        return load_list(u, [unit_rows(w2, (FF_STEPS - 1) * UN + (j % 2) * UK * P, (j // 2) * UN)
                             for j in range(RING)])
    u = load_ff(u, t["w_ff1"][0], t["w_ff2"][0])
    for c0 in (2048, 512, 1024, 0, 1536):
        u = load_slabs(u, 1, w_in2, c0=c0)
    OUT2_ORDER = [(n, k) for k in (0, 1, 2, 3) for n in (0, 1)]
    u = load_list(u, [unit_rows(t["w_out_2"][0], k * UK * P, n * UN) for n, k in OUT2_ORDER])
    u = load_slabs(u, 2, t["w_xq_2"][0])
    u = load_slabs(u, 2, t["w_xo_2"][0])
    u = load_ff(u, t["w_ff1_2"][0], t["w_ff2_2"][0])
    UNITS = u

    def then_p(ins):
        m = done(ins, PO)
        wait(pool, m)
        return m

    then_p(pool.memset(ident[:, :], 0.0))
    ident_ok = then_p(pool.affine_select(out=ident[:, :], in_=ident[:, :], compare_op=ALU.not_equal, fill=1.0, base=0,
                                       pattern=[[-1, P]], channel_multiplier=1))
    then_p(pool.memset(half[:, :], -0.5))

    split_at = [0]
    ada_sum = {"slab": 0, "kc": 0, "last": None, "free": [None] * 4, "ready": {}}

    def ada_op():
        a, kc = ada_sum["slab"], ada_sum["kc"]
        if a >= A_SLABS:
            return
        unit, k = a * RING + kc // UK, kc % UK
        acc = ada_acc[:, a % 4, :]
        if k == 0:
            dve.wait_ge(ada_in[unit % 2], 16 * (unit // 2 + 1))
        w = ada_raw[:, unit % 2, k, :]
        if kc == 0:
            if ada_sum["free"][a % 4]:
                wait(dve, ada_sum["free"][a % 4])
            ins = dve.tensor_scalar(acc, w, silu_c[:, 0:1], None, ALU.mult)
        else:
            wait(dve, ada_sum["last"])
            ins = dve.scalar_tensor_tensor(out=acc, in0=w, scalar=silu_c[:, kc:kc + 1], in1=acc,
                                           op0=ALU.mult, op1=ALU.add)
        ada_sum["last"] = AV(ins)
        if k == UK - 1:
            wait(dve, ada_sum["last"])
            dve.sem_inc(ada_used, 1)
        ada_sum["kc"] += 1
        if ada_sum["kc"] == KD:
            ada_sum["ready"][a] = ada_sum["last"]
            ada_sum["slab"], ada_sum["kc"] = a + 1, 0

    def split(u, slot):
        first = isinstance(u, int) and u < RING
        act.wait_ge(raw_in[slot], (u - slot) * (16 // RING) + 16)
        if not first:
            act.wait_ge(used, u - (RING - 1))
        act.copy(hi[:, slot], raw[:, slot]).then_inc(hi_done, 1)
        dve.wait_ge(hi_done, u + 1)
        dve.tensor_tensor(lo[:, slot], raw[:, slot], as_f32(hi[:, slot]), ALU.subtract).then_inc(lo_done, 1)

    def split_next():
        if split_at[0] < UNITS:
            split(split_at[0], split_at[0] % RING)
            n = split_at[0] // RING
            for _ in range(2 if n < 4 or n in (5, 6) else 0 if n == 4 else 1):
                ada_op()
            split_at[0] += 1
            for _ in range(min(len(background), 3)):
                background.pop(0)()

    background = []

    bank_free = [[] for _ in range(8)]

    def claim(*banks):
        for b in banks:
            wait(pe, *bank_free[b])
            bank_free[b] = []

    def three_passes(out_ap, a_hi, a_lo, b_hi, b_lo, start, stop, skip=False):
        pe.matmul(out_ap, a_hi, b_hi, start=start, stop=False, skip_group_check=skip)
        pe.matmul(out_ap, a_hi, b_lo, start=False, stop=False, skip_group_check=skip)
        return pe.matmul(out_ap, a_lo, b_hi, start=False, stop=stop, skip_group_check=skip)

    def unit_tokens(slot, k0, in_hi, in_lo, outs, first, last, cols=slice(0, UN), start_first=True):
        for k in range(UK):
            for tt in range(NT):
                tok = slice(tt * P, tt * P + P)
                mm = three_passes(outs[tt], in_hi[:, k0 + k, tok], in_lo[:, k0 + k, tok], hi[:, slot, k, cols],
                                  lo[:, slot, k, cols], first and k == 0 and (start_first or tt == 0),
                                  last and k == UK - 1, skip=True)
        return mm

    def unit_features(slot, k0, in_hi, in_lo, banks, first, last, tiles=4):
        for k in range(UK):
            for f in range(tiles):
                o = banks[f // 2][:, (f % 2) * S:(f % 2) * S + S]
                fc = slice(f * P, f * P + P)
                mm = three_passes(o, hi[:, slot, k, fc], lo[:, slot, k, fc], in_hi[:, k0 + k, :], in_lo[:, k0 + k, :],
                                  first and k == 0 and f % 2 == 0, last and k == UK - 1, skip=True)
        return mm

    at = [0]
    parity = [0]

    def next_unit(kind, *args, finish=None, **kw):
        u = at[0]
        slot = u % RING
        pe.wait_ge(lo_done, u + 1)
        kind(slot, *args, **kw).then_inc(used, 1)
        at[0] += 1
        result = finish(used_up_to(at[0])) if finish else None
        split_next()
        return result

    def used_up_to(u):
        return (UsedMark, u)

    UsedMark = Counter(used)

    def slab(kind, in_hi, in_lo, between=None, before=None, finish=None):
        b0 = 2 * parity[0]
        parity[0] ^= 1
        claim(b0, b0 + 1)
        for j in range(RING):
            if before:
                before(j)
            result = next_unit(kind, UK * j, in_hi, in_lo, [bank[b0], bank[b0 + 1]] if kind is unit_features
                      else [bank[b0][:, :], bank[b0 + 1][:, :]], first=(j == 0), last=(j == RING - 1),
                      finish=(lambda ps: finish(b0, ps)) if j == RING - 1 else None)
            if between:
                between(j)
        return result

    wait(act, cols_in)
    silu_ok = AA(act.activation(silu_c[:, :], cols[:, 0:KD], ACT.Silu))

    def rstd_of(sumsq, tmp, out_ap, n, ready):
        wait(pool, *ready)
        then_p(pool.tensor_scalar(tmp, sumsq, 1.0 / n, EPS, ALU.mult, ALU.add))
        return then_p(pool.tensor_tensor(out_ap, tmp, half[:, 0:out_ap.shape[1]], ALU.pow))

    NORM = gates[:, 0:8].rearrange("p a s -> p (a s)").rearrange("p (a d) -> p a d", a=NT)
    JUNK = gates[:, 20:24].rearrange("p a s -> p (a s)")

    def pre_norm(src, ready):
        normed = []
        for tt in range(NT):
            wait(act, *ready[tt])
            sq = AA(act.activation(JUNK, src[:, tt, :], ACT.Square, accum_out=stat[:, tt:tt + 1]))
            wait(act, sq)
            rs = rstd_of(stat[:, tt:tt + 1], stat[:, 2 + tt:3 + tt], stat[:, 4 + tt:5 + tt], D, [sq])
            wait(dve, *ready[tt], rs)
            normed.append(AV(dve.tensor_scalar(NORM[:, tt, :], src[:, tt, :], stat[:, 4 + tt:5 + tt], None, ALU.mult)))
        return normed

    def turn(normed):
        claim(4, 5, 6, 7)
        for tt in range(NT):
            wait(pe, normed[tt])
            for k in range(KD):
                c0 = (k % 2) * S + tt * P
                turned = pe.transpose(bank[4 + k // 2][:, c0:c0 + P], NORM[:, tt, k * P:k * P + P], ident[:, :])
        return done(turned, PE)

    def chunk_ps(k):
        return bank[4 + k // 2][:, (k % 2) * S:(k % 2) * S + S]

    def gain_and_split(turned, gain, dst_hi, dst_lo):
        marks = []
        wait(act, turned)
        for b in range(KD // 2):
            for k in (2 * b, 2 * b + 1):
                m = AA(act.activation(dst_hi[:, k, :], chunk_ps(k), ACT.Copy, scale=gain[:, k:k + 1]))
            wait(dve, m)
            for k in (2 * b, 2 * b + 1):
                m = AV(dve.scalar_tensor_tensor(out=dst_lo[:, k, :], in0=chunk_ps(k), scalar=gain[:, k:k + 1],
                                                in1=as_f32(dst_hi[:, k, :]), op0=ALU.mult, op1=ALU.subtract))
            bank_free[4 + b] = [m]
            marks.append(m)
        return lambda k: marks[k // 2]

    def affine_and_split(turned, gain, shift, hi_free=()):
        wait(act, turned)
        wait(dve, turned)
        f32 = []
        for k in range(KD):
            if (k // 2) % 2 == 0:
                f32.append(AA(act.activation(h_f32[:, k, :], chunk_ps(k), ACT.Identity, bias=shift[:, k:k + 1],
                                             scale=gain[:, k:k + 1])))
            else:
                f32.append(AV(dve.tensor_scalar(h_f32[:, k, :], chunk_ps(k), gain[:, k:k + 1], shift[:, k:k + 1],
                                                ALU.mult, ALU.add)))
            bank_free[4 + k // 2] = [f32[k]]
        marks = [split_act(slice(k, k + 2), f32[k + 1]) for k in range(0, KD, 2)]
        return lambda k: marks[k // 2]

    def split_act(ks, ready, src=None, dst_hi=None, dst_lo=None):
        src = h_f32 if src is None else src
        dst_hi = h_hi if dst_hi is None else dst_hi
        dst_lo = h_lo if dst_lo is None else dst_lo
        wait(dve, ready)
        then_v(dve.tensor_copy(dst_hi[:, ks, :], src[:, ks, :]))
        return AV(dve.tensor_tensor(dst_lo[:, ks, :], src[:, ks, :], as_f32(dst_hi[:, ks, :]), ALU.subtract))

    def evac_to(dst):
        return lambda b0, ready: evac_copy(b0, ready, dst)

    def evac_copy(b0, ready, dst):
        wait(act, ready)
        m0 = AA(act.copy(dst(0), bank[b0][:, :]))
        wait(dve, ready)
        m1 = AV(dve.tensor_copy(dst(1), bank[b0 + 1][:, :]))
        bank_free[b0], bank_free[b0 + 1] = [m0], [m1]
        return [m0, m1]

    def pair(buf, k):
        return buf[:, k:k + 2].rearrange("p a s -> p (a s)")

    wait(act, cols_in)
    wait(dve, cols_in)
    wait(pe, ident_ok)
    turned = turn(pre_norm(mem, mem_in))
    wait(dve, silu_ok)
    split_next()
    m_ready = gain_and_split(turned, cols[:, G_MEM:G_MEM + KD], br_hi, br_lo)
    for _ in range(RING - 1):
        split_next()

    then_p(pool.memset(ones[:, :], 1.0))
    then_p(pool.memset(upper[:, :], 1.0))
    upper_ok = then_p(pool.affine_select(out=upper[:, 0:P], in_=upper[:, 0:P], compare_op=ALU.is_ge, fill=0.0, base=0,
                                       pattern=[[1, P]], channel_multiplier=-1))
    then_p(pool.memset(mask[:, :], 0.0))
    mask_ok = then_p(pool.affine_select(out=mask[:, :], in_=mask[:, :], compare_op=ALU.is_ge, fill=8 * NEG, base=P,
                                      pattern=[[-1, S]], channel_multiplier=1))
    then_p(pool.iota(dist[:, :], pattern=[[1, S]], base=-P, channel_multiplier=-1,
                     allow_small_or_imprecise_dtypes=True))
    dist_ok = then_p(pool.affine_select(out=dist[:, :], in_=dist[:, :], compare_op=ALU.is_ge, fill=NEG, base=P,
                                      pattern=[[-1, S]], channel_multiplier=1))
    then_p(pool.memset(blockmean[:, :], 0.0))
    then_p(pool.memset(blockmean[0:64, 0:64], 1.0 / 64))
    then_p(pool.memset(blockmean[64:128, 64:128], 1.0 / 64))
    wp_zero = then_p(pool.memset(wpool[:, :, :], 0.0))
    ld_wp = arrivals("w_pool_in")
    for g in range(4):
        s = 64 * (g % 2)
        wpool_in = ld_wp(pool, wpool[s:s + 64, g // 2, s:s + 64], t["w_pool"][0][g])
    then_p(pool.iota(cnt16[:, 2, :], pattern=[[1, 16]], base=1, channel_multiplier=0,
                               allow_small_or_imprecise_dtypes=True))
    for g, w in enumerate(WINDOWS):
        s = 64 * (g % 2)
        then_p(pool.memset(rcount[s:s + 64, g // 2, 16:S], 1.0 / w))
        then_p(pool.tensor_scalar(cnt16[s:s + 64, g // 2, :], cnt16[s:s + 64, 2, :], float(w), None, ALU.min))
    pool_consts = then_p(pool.memset(pad_u[:, :, :], 0.0))
    wait(pool, small_in)
    wsT_ok = then_p(pool.affine_select(out=ws_T[:, :, :], in_=ws_T[:, :, :], compare_op=ALU.is_ge, fill=0.0, base=0,
                                       pattern=[[0, 4], [1, P]], channel_multiplier=-1))


    def wait_chunks(ready_of):
        return lambda j: wait(pe, ready_of(UK * j))

    x_normed = None
    for n in range(2):
        slab(unit_features, br_hi, br_lo, before=wait_chunks(m_ready) if n == 0 else None,
             finish=evac_to(lambda i: pair(mem_k, 4 * n + 2 * i)))
        if n == 0:
            x_normed = pre_norm(x, [[x_in], [x_in]])
        else:
            x_turned = turn(x_normed)
    wait(dve, pool_consts)
    rcount_ok = AV(dve.reciprocal(rcount[:, :, 0:16], cnt16[:, 0:2, :]))
    def ada_columns(slot, n_slabs, b, c0):
        for s in range(n_slabs):
            for j in range(4):
                mm = pe.matmul(bank[b][:, c0 + 4 * s + j:c0 + 4 * s + j + 1], ada_acc[:, slot + s, j * P:j * P + P],
                               ones[:, 0:1], start=True, stop=True, skip_group_check=True)
        return done(mm, PE)

    def load_row(dst, name, c0=0, group=None):
        return (group or arrivals(name + "_row_in"))(act, dst, t[name][0:1, c0:c0 + D].broadcast_to([P, D]))

    def ada_row(slot, dst, gain_in, b0):
        claim(b0, b0 + 1)
        for s in range(2):
            mm = pe.matmul(bank[b0 + s][:, :], ones[:, :], ada_acc[:, slot + s, :], start=True, stop=True)
        ps = done(mm, PE)
        wait(dve, ps, gain_in)
        for s in range(2):
            cs = slice(s * UN, s * UN + UN)
            added = AV(dve.tensor_tensor(dst[:, cs], dst[:, cs], bank[b0 + s][:, :], ALU.add))
            wait(dve, added)
            bank_free[b0 + s] = [added]
            m = AV(dve.tensor_tensor(dst[:, cs], dst[:, cs], rowtmp[:, cs], ALU.mult))
        return ps, m

    slab(unit_tokens, br_hi, br_lo,
         finish=evac_to(lambda i: mem_v[:, i, 0:UN]))

    def mixer_columns(j):
        if j != 1:
            return
        assert ada_sum["slab"] == 4
        wait(pe, ada_sum["ready"][3])
        b = 2 * parity[0]
        claim(b)
        ps = ada_columns(0, 4, b, 0)
        ada_sum["free"] = [ps] * 4
        wait(dve, ps)
        m = then_v(dve.tensor_tensor(adacol[:, 0:16], bank[b][:, 0:16], cols[:, B_ADA:B_ADA + 16], ALU.add))
        bank_free[b] = [m]
        m = then_v(dve.scalar_tensor_tensor(out=adacol[:, 8:16], in0=adacol[:, 8:16], scalar=1.0,
                                            in1=cols[:, G_MIX:G_MIX + KD], op0=ALU.add, op1=ALU.mult))
        wait(act, m)
        mixer_input.append(affine_and_split(x_turned, adacol[:, 8:16], adacol[:, 0:8]))

    mixer_input = []
    slab(unit_tokens, br_hi, br_lo, between=mixer_columns,
         finish=evac_to(lambda i: mem_v[:, i, UN:2 * UN]))
    h_ready = mixer_input[0]

    q_ok = slab(unit_features, h_hi, h_lo, before=wait_chunks(h_ready),
         finish=evac_to(lambda i: pair(qT, 2 * i)))
    k_ok = slab(unit_features, h_hi, h_lo,
         finish=evac_to(lambda i: pair(kT, 2 * i)))
    claim(4)
    wait(pe, small_in)
    for tt in range(NT):
        for k in range(KD):
            mm = pe.matmul(bank[4][:, tt * NH:tt * NH + NH], h_f32[:, k, tt * P:tt * P + P], w_fl[:, k, :],
                           start=(k == 0), stop=(k == KD - 1))
    fl_ps = done(mm, PE)
    wait(dve, fl_ps, small_in)
    for tt in range(NT):
        m = AV(dve.tensor_tensor(fl[:, tt, :], bank[4][:, tt * NH:tt * NH + NH], bf_row[:, :], ALU.add))
    wait(dve, m)
    bank_free[4] = [m]
    flz = fl[:, :, :].rearrange("p a h -> p (a h)")
    then_v(dve.tensor_scalar(tmp16[:, 0, :], flz, -1.0, None, ALU.mult))
    m = then_v(dve.tensor_tensor(tmp16[:, 0, :], tmp16[:, 0, :], flz, ALU.min))
    wait(act, m)
    then_a(act.activation(tmp16[:, 1, :], tmp16[:, 0, :], ACT.Exp))
    m = AA(act.activation(tmp16[:, 0, :], tmp16[:, 1, :], ACT.Ln, bias=1.0))
    then_v(dve.tensor_scalar(tmp16[:, 2, :], flz, 0.0, None, ALU.min))
    wait(dve, m)
    lf = logf[:, :, :].rearrange("p a h -> p (a h)")
    then_v(dve.tensor_tensor(lf, tmp16[:, 2, :], tmp16[:, 0, :], ALU.subtract))
    nlogf_ok = AV(dve.tensor_scalar(nlogf8[:, :, :].rearrange("p a h -> p (a h)"), lf, -8.0, None, ALU.mult))
    v_ok = slab(unit_tokens, h_hi, h_lo,
         finish=evac_to(lambda i: v_tok[:, i, :]))
    claim(4)
    wait(pe, nlogf_ok)
    pe.matmul(bank[4][:, 0:NH], upper[:, 0:P], nlogf8[:, 0, :], start=True, stop=True)
    pe.matmul(bank[4][:, NH:2 * NH], ones[:, :], nlogf8[:, 0, :], start=True, stop=False)
    cum_ps = done(pe.matmul(bank[4][:, NH:2 * NH], upper[:, 0:P], nlogf8[:, 1, :], start=False, stop=True), PE)
    wait(dve, cum_ps)
    cum_ok = AV(dve.tensor_scalar(cum8[:, :, :].rearrange("p a h -> p (a h)"), bank[4][:, 0:2 * NH], -1.0, None,
                                  ALU.mult))
    bank_free[4] = [cum_ok]

    CUTS = ((0, P), (P, P + S))

    class HeadPair:

        def __init__(self, g, soft, turned, forget, logit_banks, banks):
            self.g, self.soft, self.turned, self.forget = g, soft, turned, forget
            self.logit_banks, self.banks = logit_banks, banks
            c = 12 * g
            self.mx, self.negmx, self.rsum = att[:, c:c + 4], att[:, c + 4:c + 8], att[:, c + 8:c + 12]

        def parts(self):
            for e in range(2):
                for tt, (c0, c1) in enumerate(CUTS):
                    yield e, tt, c0, c1

        def scores(self, first_waits):
            g, soft = self.g, self.soft
            claim(*self.logit_banks)
            wait(pe, *first_waits)
            for e, tt, c0, c1 in self.parts():
                rows_ = slice(64 * e, 64 * e + 64)
                b = bank[self.logit_banks[e]]
                mm = pe.matmul(b[:, c0:c1], qT[rows_, g, tt * P:tt * P + P], kT[rows_, g, 0:c1 - c0],
                               start=True, stop=not self.forget)
                if self.forget:
                    head = 2 * g + e
                    mm = pe.matmul(b[:, c0:c1], nlogf8[:, 0, head:head + 1].to_broadcast([P, P]),
                                   upper[:, 0:c1 - c0], start=False, stop=(tt == 0))
                    if tt == 1:
                        mm = pe.matmul(b[:, c0 + P:c1], nlogf8[:, 1, head:head + 1].to_broadcast([P, P]),
                                       upper[:, 0:P], start=False, stop=True)
            ps = done(mm, PE)
            wait(dve, ps)
            for e, tt, c0, c1 in self.parts():
                dst, src_ps = soft[:, e, c0:c1], bank[self.logit_banks[e]][:, c0:c1]
                keys = slice(P, S) if tt == 0 else slice(0, S)
                if self.forget:
                    m = AV(dve.scalar_tensor_tensor(out=dst, in0=src_ps, scalar=cum8[:, tt, 2 * g + e:2 * g + e + 1],
                                                    in1=mask[:, keys], op0=ALU.add, op1=ALU.add))
                else:
                    slope = 2.0 ** (-8.0 * (2 * g + e + 1) / NH)
                    m = AV(dve.scalar_tensor_tensor(out=dst, in0=dist[:, keys], scalar=8.0 * slope, in1=src_ps,
                                                    op0=ALU.mult, op1=ALU.add))
                bank_free[self.logit_banks[e]] = [m]
            wait(dve, m)
            for e, tt, c0, c1 in self.parts():
                i = 2 * e + tt
                m = AV(dve.tensor_reduce(self.mx[:, i:i + 1], soft[:, e, c0:c1], AX.X, ALU.max))
            wait(dve, m)
            m = AV(dve.tensor_scalar(self.negmx, self.mx, -0.125, None, ALU.mult))
            wait(act, m)
            for e, tt, c0, c1 in self.parts():
                i = 2 * e + tt
                m = AA(act.activation(soft[:, e, c0:c1], soft[:, e, c0:c1], ACT.Exp, bias=self.negmx[:, i:i + 1],
                                      scale=0.125, accum_out=self.rsum[:, i:i + 1]))
            self.exp_ok = m

        def normalize(self):
            wait(dve, self.exp_ok)
            m = AV(dve.reciprocal(self.rsum, self.rsum))
            wait(act, m)
            for e, tt, c0, c1 in self.parts():
                i = 2 * e + tt
                m = AA(act.activation(self.soft[:, e, c0:c1], self.soft[:, e, c0:c1], ACT.Copy,
                                      scale=self.rsum[:, i:i + 1]))
            self.prob_ok = m

        def turn(self):
            claim(*self.banks)
            wait(pe, self.prob_ok)
            for e in range(2):
                for c in range(0, 3 * P, P):
                    mm = pe.transpose(bank[self.banks[e]][:, c:c + P], self.soft[:, e, c:c + P], ident[:, :])
            ps = done(mm, PE)
            wait(act, ps)
            m0 = AA(act.copy(self.turned[:, 0, :], bank[self.banks[0]][:, 0:384]))
            wait(dve, ps)
            m1 = AV(dve.tensor_copy(self.turned[:, 1, :], bank[self.banks[1]][:, 0:384]))
            bank_free[self.banks[1]] = [m1]
            self.turned_ok = [m0, m1]

        def attend(self, v_ready):
            wait(pe, *self.turned_ok, *v_ready)
            for e in range(2):
                vc = slice((2 * self.g + e) * DH, (2 * self.g + e) * DH + DH)
                o = bank[self.banks[0]][64 * e:64 * e + 64]
                pT = self.turned[:, e, :]
                pe.matmul(o[:, 0:P], v_tok[:, 0, vc], pT[:, 0:P], start=True, stop=True)
                pe.matmul(o[:, P:S], v_tok[:, 0, vc], pT[:, P:S], start=True, stop=False)
                mm = pe.matmul(o[:, P:S], v_tok[:, 1, vc], pT[:, S:S + P], start=False, stop=True)
            self.branch_ok = to_branch(self.banks[0], slice(0, S), self.g, done(mm, PE))

    def to_branch(b, cols, tile, ps, scale=None, n=1):
        dst_hi = br_hi[:, tile:tile + n].rearrange("p a s -> p (a s)")
        dst_lo = br_lo[:, tile:tile + n].rearrange("p a s -> p (a s)")
        wait(act, ps)
        if scale is None:
            m = AA(act.copy(dst_hi, bank[b][:, cols]))
            wait(dve, m)
            m = AV(dve.tensor_tensor(dst_lo, bank[b][:, cols], as_f32(dst_hi), ALU.subtract))
        else:
            m = AA(act.activation(dst_hi, bank[b][:, cols], ACT.Copy, scale=scale))
            wait(dve, m)
            m = AV(dve.scalar_tensor_tensor(out=dst_lo, in0=bank[b][:, cols], scalar=scale, in1=as_f32(dst_hi),
                                            op0=ALU.mult, op1=ALU.subtract))
        bank_free[b] = [m]
        return m

    def split_to_branch(src, tile, n, ready):
        return split_act(slice(tile, tile + n), ready, src=ShiftedTiles(src, tile), dst_hi=br_hi, dst_lo=br_lo)

    class ShiftedTiles:

        def __init__(self, src, tile):
            self.src, self.tile = src, tile

        def __getitem__(self, key):
            p, ks, c = key
            return self.src[p, ks.start - self.tile:ks.stop - self.tile, c]

    probT_pair = probT[:, :, 0:384]
    pairs1 = [HeadPair(g, soft, probT_pair, True, (4, 5), (6, 7)) for g in range(4)]
    att1_waits = [*q_ok, *k_ok, cum_ok, upper_ok, mask_ok]
    wait(dve, mask_ok)
    gate_m_row = rows[:, 0, :]
    mix_rows = arrivals("mix_rows_in")
    load_row(gate_m_row, "b_ada", 2 * D, mix_rows)
    row_in = load_row(rowtmp[:, :], "g_mix_post", 0, mix_rows)
    gate_rows = []

    def make_gate_m_row(j):
        if j == 1:
            assert ada_sum["slab"] >= 6
            wait(pe, ada_sum["ready"][5])
            gate_rows.append(ada_row(0, gate_m_row, row_in, 2 * parity[0]))
            ada_sum["free"][0:2] = [gate_rows[0][0]] * 2

    mixA_ok = slab(unit_features, h_hi, h_lo, between=make_gate_m_row, finish=evac_to(lambda i: pair(mix, 2 * i)))
    mixB_ok = slab(unit_features, h_hi, h_lo, finish=evac_to(lambda i: pair(mix, 4 + 2 * i)))
    _, row0_ok = gate_rows[0]

    wait(pool, *mixA_ok, rcount_ok)
    pooled = gates[:, 18:20]
    PADW = 16
    for tile in range(2):
        then_p(pool.memset(win_a[:, 0:PADW], 0.0))
        then_p(pool.memset(win_b[:, 0:PADW], 0.0))
        then_p(pool.tensor_copy(pad_u[:, tile, PADW:PADW + S], mix[:, tile, :]))
        src = pad_u[:, tile, 0:PADW + S]
        bufs = (win_a, win_b)
        for step in range(2 * tile + 2):
            shift = 2 ** step
            last_step = step == 2 * tile + 1
            rows_ = slice(64, P) if last_step else slice(0, P)
            dst = bufs[step % 2]
            then_p(pool.tensor_tensor(dst[rows_, shift:PADW + S], src[rows_, shift:PADW + S],
                                      src[rows_, 0:PADW + S - shift], ALU.add))
            if step == 2 * tile:
                low = dst
            src = dst
        for rows_, buf in ((slice(0, 64), low), (slice(64, P), src)):
            then_p(pool.tensor_tensor(pooled[rows_, tile, :], buf[rows_, PADW:PADW + S], rcount[rows_, tile, :],
                                      ALU.mult))
            pool_in = then_p(pool.tensor_tensor(pooled[rows_, tile, :], pooled[rows_, tile, :], mix[rows_, tile, :],
                                                ALU.subtract))
    wait(pool, *mixB_ok)
    conv_y = gates[:, 16:18]
    for tile in range(2):
        tap = gates[:, 12 + tile, :]
        then_p(pool.memset(pad_u[:, tile, 0:TAPS3 - 1], 0.0))
        then_p(pool.tensor_tensor(pad_u[:, tile, TAPS3 - 1:TAPS3 - 1 + S], mix[:, 6 + tile, :], mix[:, 2 + tile, :],
                                  ALU.mult))
        for k in range(TAPS3):
            wcol = cols[:, W_CONV + 2 * k + tile:W_CONV + 2 * k + tile + 1].to_broadcast([P, S])
            then_p(pool.tensor_tensor(tap if k else conv_y[:, tile, :], pad_u[:, tile, k:k + S], wcol, ALU.mult))
            if k:
                then_p(pool.tensor_tensor(conv_y[:, tile, :], conv_y[:, tile, :], tap, ALU.add))
        conv_ok = then_p(pool.tensor_tensor(conv_y[:, tile, :], conv_y[:, tile, :], mix[:, 4 + tile, :], ALU.mult))

    def gate_tiles(s):
        def take(b0, ps):
            wait(act, ps)
            if s == 3:
                wait(act, conv_br)
            for i in range(2):
                m = AA(act.activation(pair(gates, 4 * s + 2 * i), bank[b0 + i][:, :], ACT.Sigmoid))
                bank_free[b0 + i] = [m]
            return m
        return take

    def attention1(unit):
        pr, stage = pairs1[unit // 6], unit % 6
        if stage == 0:
            pr.scores(att1_waits)
        if stage == 2:
            pr.normalize()
        if stage == 3:
            pr.turn()
        if stage == 4:
            pr.attend(v_ok)

    for s in range(6):
        gates_ok = slab(unit_features, h_hi, h_lo, between=lambda j: attention1(4 * s + j), finish=gate_tiles(s))
        if s == 1:
            assert ada_sum["slab"] >= 8
            b = 2 * parity[0]
            claim(b)
            wait(pe, ada_sum["ready"][7])
            ps = ada_columns(2, 2, b, 0)
            ada_sum["free"][2:4] = [ps] * 2
            wait(dve, ps)
            m = AV(dve.tensor_tensor(adacol[:, 16:24], bank[b][:, 0:8], cols[:, B_ADA + 24:B_ADA + 32], ALU.add))
            bank_free[b] = [m]
        if s == 2:
            claim(7)
            wait(pe, pool_in, wpool_in, wp_zero)
            for tile in range(2):
                mm = pe.matmul(bank[7][:, tile * S:tile * S + S], wpool[:, tile, :], pooled[:, tile, :],
                               start=True, stop=True)
            ps = done(mm, PE)
            for tile in range(2):
                pool_ok = to_branch(7, slice(tile * S, tile * S + S), 4 + tile, ps,
                                    scale=cols[:, C_POOL + tile:C_POOL + tile + 1])
                wait(act, pool_ok)
            conv_br = split_to_branch(conv_y, 6, 2, conv_ok)
        if s == 3:
            wait(act, row0_ok)
            ff_rows = arrivals("ff_rows_in")
            load_row(rows[:, 1, :], "b_ada", 5 * D, ff_rows)
            row1_in = load_row(rowtmp[:, :], "g_ff_post", 0, ff_rows)

    merged_ok = []
    for n in range(2):
        sets = ((0, 1), (2, 3), (4, 5)) if n == 0 else ((6, 7), (0, 1), (2, 3))
        got = []
        for br, (units, banks) in enumerate(zip(((0, 1), (2,), (3,)), sets)):
            claim(*banks)
            if n == 0:
                wait(pe, *([pr.branch_ok for pr in pairs1] if br == 0 else [pool_ok] if br == 1 else [conv_br]))
            for j in units:
                next_unit(unit_features, UK * j, br_hi, br_lo, [bank[b] for b in banks], first=(j == units[0]),
                          last=(j == units[-1]))
            ps = used_up_to(at[0])
            wait(dve, ps, gates_ok)
            for i, b in enumerate(banks):
                g = pair(gates, KD * br + 4 * n + 2 * i)
                if br == 0:
                    m = AV(dve.tensor_tensor(pair(h_f32, 4 * n + 2 * i), g, bank[b][:, :], ALU.mult))
                else:
                    m = AV(dve.tensor_tensor(g, g, bank[b][:, :], ALU.mult))
                bank_free[b] = [m]
                got.append(m)
            if br:
                for i in range(2):
                    wait(dve, got[-1])
                    acc = pair(h_f32, 4 * n + 2 * i)
                    m = AV(dve.tensor_tensor(acc, acc, pair(gates, KD * br + 4 * n + 2 * i), ALU.add))
                    got.append(m)
        for i in range(2):
            merged_ok.append(split_act(slice(4 * n + 2 * i, 4 * n + 2 * i + 2), got[-1]))
    parity[0] = 0

    assert ada_sum["slab"] >= 10
    claim(4)
    wait(pe, ada_sum["ready"][9])
    ps = ada_columns(0, 2, 4, 0)
    wait(dve, ps)
    m = then_v(dve.tensor_tensor(adacol[:, 24:32], bank[4][:, 0:8], cols[:, B_ADA + 32:B_ADA + 40], ALU.add))
    bank_free[4] = [m]
    ffcols = then_v(dve.scalar_tensor_tensor(out=adacol[:, 24:32], in0=adacol[:, 24:32], scalar=1.0,
                                             in1=cols[:, G_FF:G_FF + KD], op0=ALU.add, op1=ALU.mult))

    def post_half(n, banks, ps, row, row_ok):
        wait(act, ps)
        wait(dve, row_ok)
        for tt in range(NT):
            i = 20 + 2 * tt + n
            sq = AA(act.activation(JUNK[:, tt * UN:tt * UN + UN], bank[banks[tt]][:, :], ACT.Square,
                                   accum_out=stat[:, i:i + 1]))
            wait(act, sq)
            wait(dve, sq)
            cs = slice(n * UN, n * UN + UN)
            m = AV(dve.tensor_tensor(NORM[:, tt, cs], bank[banks[tt]][:, :], row[:, cs], ALU.mult))
            bank_free[banks[tt]] = [m]
        return sq, m

    def post_sum(sq, scaled):
        sums = stat[:, 20:24].rearrange("p (a b) -> p a b", b=2)
        wait(pool, sq)
        then_p(pool.tensor_tensor(stat[:, 24:26], sums[:, :, 0], sums[:, :, 1], ALU.add))
        rs = rstd_of(stat[:, 24:26], stat[:, 26:28], stat[:, 28:30], D, [])
        wait(dve, scaled, rs)
        return [[AV(dve.scalar_tensor_tensor(out=x[:, tt, :], in0=NORM[:, tt, :], scalar=stat[:, 28 + tt:29 + tt],
                                             in1=x[:, tt, :], op0=ALU.mult, op1=ALU.add))] for tt in range(NT)]

    def out_projection(in_hi, in_lo, row, row_ok, before=None):
        for n in range(2):
            half_done = slab(unit_tokens, in_hi, in_lo, before=before if n == 0 else None,
                             finish=lambda b0, ps: post_half(n, (b0, b0 + 1), ps, row, row_ok))
        return post_sum(*half_done)

    x_ok = out_projection(h_hi, h_lo, rows[:, 0, :], row0_ok, before=lambda j: wait(pe, merged_ok[j]))

    def feed_forward(name, ready_of, row, row_ok):
        made = counter(name + "_made")
        first_used = at[0]
        hid = h_f32[:, 0:4]
        split_f = counter(name + "_relu")

        def w1_slab(u, before=None):
            for q in range(RING):
                pe.wait_ge(lo_done, u + (q + 1))
                if before:
                    before(q)
                unit_features(q, UK * q, h_hi, h_lo, [bank[0], bank[1]], first=(q == 0),
                              last=(q == RING - 1)).then_inc(used, 1)
                split_ahead(u + q, q)

        def split_ahead(u, slot):
            if isinstance(u, int) and u + RING >= UNITS:
                return
            split(u + RING, slot)
            if isinstance(u, int):
                split_at[0] = u + RING + 1

        def take_hidden(j, u_end):
            act.wait_ge(used, u_end)
            if not (isinstance(j, int) and j == 0):
                act.wait_ge(made.sem, j)
            for i in range(2):
                act.activation(pair(hid, 2 * i), bank[i][:, :], ACT.Relu).then_inc(split_f.sem, 1)
            for i in range(2):
                dve.wait_ge(split_f.sem, j * 2 + (i + 1))
                r = pair(hid, 2 * i)
                m = AV(dve.tensor_tensor(r, r, r, ALU.mult))
            wait(dve, m)

        def split_hidden(w2_end):
            for i in range(2):
                f = slice(2 * i, 2 * i + 2)
                if i == 0 and w2_end is not None:
                    dve.wait_ge(used, w2_end)
                then_v(dve.tensor_copy(br_hi[:, f, :], hid[:, f, :]))
                ins = dve.tensor_tensor(br_lo[:, f, :], hid[:, f, :], as_f32(br_hi[:, f, :]), ALU.subtract)
                m = AV(ins)
            wait(dve, m)
            dve.sem_inc(made.sem, 1)

        def w2_step(j, u, first, last, after=None):
            pe.wait_ge(made.sem, j + 1)
            for q in range(RING):
                pe.wait_ge(lo_done, u + (q + 1))
                n = q // 2
                unit_tokens(q, UK * (q % 2), br_hi, br_lo, [bank[4 + 2 * n][:, :], bank[5 + 2 * n][:, :]],
                            first=first and q % 2 == 0, last=last and q % 2 == 1).then_inc(used, 1)
                split_ahead(u + q, q)
                if after:
                    after(q)

        u = at[0]
        assert u % RING == 0
        claim(0, 1, 4, 5, 6, 7)
        w1_slab(u, before=lambda q: wait(pe, ready_of(UK * q)))
        take_hidden(0, u + RING)
        split_hidden(None)
        u += RING

        def step(i, u, first):
            pe.wait_ge(split_f.sem, i * 2 + 2)
            w1_slab(u)
            take_hidden(i + 1, u + RING)
            w2_step(i, u + RING, first, False)
            split_hidden(u + 2 * RING)
        step(0, u, True)
        u += 2 * RING
        with loop(nc, FF_STEPS - 2, {VE: VE_PER_STEP}) as i:
            step(i + 1, i * (2 * RING) + u, False)
        u += (FF_STEPS - 2) * 2 * RING
        split_at[0] = u + RING
        half_done = []

        def after(q):
            if q % 2:
                n = q // 2
                half_done.append(post_half(n, (4 + 2 * n, 5 + 2 * n), used_up_to(u + q + 1), row, row_ok))
        w2_step(FF_STEPS - 1, u, False, True, after)
        at[0] = u + RING
        bank_free[0] = bank_free[1] = [(split_f, 2 * FF_STEPS)]
        parity[0] = 0
        return post_sum(*half_done[1])

    VE_PER_STEP = 6
    wait(act, ffcols)
    h_ready = affine_and_split(turn(pre_norm(x, x_ok)), adacol[:, 24:32], adacol[:, 16:24])
    row_post_mix = load_row(rows[:, 0, :], "post_mix_g_2")
    assert ada_sum["slab"] == A_SLABS
    wait(pe, ada_sum["ready"][A_SLABS - 1])
    _, row1_ok = ada_row(2, rows[:, 1, :], row1_in, 2)
    x_ok = feed_forward("ff1", h_ready, rows[:, 1, :], row1_ok)
    wait(act, *x_ok[1])
    row_post_x = load_row(rows[:, 1, :], "post_x_g_2")

    h_ready = gain_and_split(turn(pre_norm(x, x_ok)), cols[:, G_MIX2:G_MIX2 + KD], h_hi, h_lo)
    pad_zero = then_p(pool.memset(pad_u[:, :, 0:TAPS31 - 1], 0.0))

    def take_glu(b0, ps):
        sig = gates[:, 16:18]
        wait(act, ps)
        sig_ok = AA(act.activation(pair(gates, 16), bank[b0 + 1][:, :], ACT.Sigmoid))
        bank_free[b0 + 1] = [sig_ok]
        wait(dve, sig_ok, pad_zero)
        for tile in range(2):
            m = AV(dve.tensor_tensor(pad_u[:, tile, TAPS31 - 1:], bank[b0][:, tile * S:tile * S + S],
                                     sig[:, tile, :], ALU.mult))
        bank_free[b0] = [m]
        return m
    glu_ok = slab(unit_features, h_hi, h_lo, before=wait_chunks(h_ready), finish=take_glu)

    conv_y = mix[:, 4:6]
    tap_marks = [glu_ok]

    def tap_column(k, tile):
        return cols[:, W_DW + 2 * k + tile:W_DW + 2 * k + tile + 1]

    def vector_tap(k):
        def emit_tap():
            wait(dve, tap_marks[-1])
            if k == 0:
                ins = dve.tensor_scalar(conv_y[:, 0, :], pad_u[:, 0, 0:S], tap_column(0, 0), cols[:, C_BDW:C_BDW + 1],
                                        ALU.mult, ALU.add)
            else:
                ins = dve.scalar_tensor_tensor(out=conv_y[:, 0, :], in0=pad_u[:, 0, k:k + S], scalar=tap_column(k, 0),
                                               in1=conv_y[:, 0, :], op0=ALU.mult, op1=ALU.add)
            tap_marks.append(AV(ins))
        return emit_tap
    background.extend(vector_tap(k) for k in range(TAPS31))
    wait(pool, glu_ok)
    tap = gates[:, 15, :]
    for k in range(TAPS31):
        dst = tap if k else conv_y[:, 1, :]
        then_p(pool.tensor_tensor(dst, pad_u[:, 1, k:k + S], tap_column(k, 1).to_broadcast([P, S]), ALU.mult))
        other = tap if k else cols[:, C_BDW + 1:C_BDW + 2].to_broadcast([P, S])
        conv1_ok = then_p(pool.tensor_tensor(conv_y[:, 1, :], conv_y[:, 1, :], other, ALU.add))

    q_ok = slab(unit_features, h_hi, h_lo, finish=evac_to(lambda i: pair(qT, 2 * i)))
    k_ok = slab(unit_features, h_hi, h_lo, finish=evac_to(lambda i: pair(kT, 2 * i)))
    att2_waits = [*q_ok, *k_ok]
    wait(dve, dist_ok)

    def floats(a, b):
        return gates[:, a:b].rearrange("p a s -> p (a s)").rearrange("p (e c) -> p e c", e=2)
    pairs2 = [HeadPair(g, floats(3 * g, 3 * g + 3), probT_pair if g % 2 == 0 else floats(12, 15), False,
                       *[(4, 5) if g % 2 == 0 else (6, 7)] * 2) for g in range(4)]
    ya = gates[:, 18:20]
    u_T, vg = mix[:, 0:2], mix[:, 2:4]
    late = {}

    def take_gelu(b0, ps):
        wait(act, ps)
        u_ok = AA(act.activation(pair(mix, 0), bank[b0][:, :], ACT.Gelu))
        v_gelu = AA(act.activation(pair(mix, 2), bank[b0 + 1][:, :], ACT.Gelu))
        bank_free[b0], bank_free[b0 + 1] = [u_ok], [v_gelu]
        return u_ok, v_gelu

    def gate_norm():
        wait(dve, late["gelu"][1], small_in)
        for tt in range(NT):
            then_v(dve.bn_stats(stats6[:, tt, :], vg[:, tt, :]))
            m = then_v(dve.bn_aggr(stat[:, 2 * tt:2 * tt + 2], stats6[:, tt, :]))
        var = stat[:, 0:4].rearrange("p (a b) -> p a b", b=2)[:, :, 1]
        late["var"] = AV(dve.tensor_scalar(stat[:, 4:6], var, EPS, None, ALU.add))
        wait(act, late["var"])
        late["std"] = AA(act.activation(stat[:, 6:8], stat[:, 4:6], ACT.Sqrt))

    def gate_scale():
        wait(dve, late["std"])
        then_v(dve.reciprocal(stat[:, 6:8], stat[:, 6:8]))
        for tt in range(NT):
            then_v(dve.tensor_scalar(vg[:, tt, :], vg[:, tt, :], stat[:, 2 * tt:2 * tt + 1], stat[:, 6 + tt:7 + tt],
                                     ALU.subtract, ALU.mult))
            then_v(dve.tensor_tensor(vg[:, tt, :], vg[:, tt, :], ln_rows[:, 0, :], ALU.mult))
            late["v"] = then_v(dve.tensor_tensor(vg[:, tt, :], vg[:, tt, :], ln_rows[:, 1, :], ALU.add))

    def gate_mix():
        b = 2 * parity[0]
        claim(b)
        wait(pe, late["v"], wsT_ok)
        for h in range(4):
            for tt in range(NT):
                c0 = (h // 2) * S + tt * P
                mm = pe.matmul(bank[b][64 * (h % 2):64 * (h % 2) + 64, c0:c0 + P], vg[:, tt, h * 64:h * 64 + 64],
                               ws_T[:, h, :], start=True, stop=True)
        ps = done(mm, PE)
        wait(dve, ps, late["gelu"][0])
        for tile in range(2):
            for tt in range(NT):
                c = slice(tt * P, tt * P + P)
                m = AV(dve.tensor_tensor(ya[:, tile, c], bank[b][:, tile * S + tt * P:tile * S + tt * P + P],
                                         bs_row[:, tile, :], ALU.add))
        bank_free[b] = [m]
        wait(dve, m)
        m = then_v(dve.tensor_tensor(ya, ya, u_T, ALU.mult))
        late["ya"] = split_to_branch(ya, 4, 2, m)

    conv2, sq2 = pair(mix, 4), pair(mix, 6)
    NORM_BANK = 4

    def conv_center():
        assert not background
        claim(NORM_BANK)
        wait(pe, tap_marks[-1], conv1_ok, pool_consts)
        ps = done(pe.matmul(bank[NORM_BANK][:, :], blockmean[:, :], conv2, start=True, stop=True), PE)
        wait(dve, ps, tap_marks[-1], conv1_ok)
        cen = then_v(dve.tensor_tensor(conv2, conv2, bank[NORM_BANK][:, :], ALU.subtract))
        wait(act, cen)
        late["squares"] = AA(act.activation(sq2, conv2, ACT.Square))

    def conv_norm():
        wait(pe, late["squares"])
        ps = done(pe.matmul(bank[NORM_BANK][:, :], blockmean[:, :], sq2, start=True, stop=True), PE)
        wait(dve, ps)
        m = AV(dve.tensor_scalar(sq2, bank[NORM_BANK][:, :], EPS, None, ALU.add))
        bank_free[NORM_BANK] = [m]
        wait(act, m)
        m = AA(act.activation(sq2, sq2, ACT.Sqrt))
        wait(dve, m)
        then_v(dve.reciprocal(sq2, sq2))
        m = then_v(dve.tensor_tensor(conv2, conv2, sq2, ALU.mult))
        wait(act, m)
        for tile in range(2):
            m = AA(act.activation(conv_y[:, tile, :], conv_y[:, tile, :], ACT.Silu,
                                  bias=cols[:, C_GNB + tile:C_GNB + tile + 1],
                                  scale=cols[:, C_GNG + tile:C_GNG + tile + 1]))
        late["yc"] = split_to_branch(conv_y, 6, 2, m)

    p0, p1, p2, p3 = pairs2

    def start_pair(pr):
        return lambda: pr.scores(att2_waits)

    def finish_pair(pr):
        return lambda: pr.attend(v_ok)
    plan = {0: [start_pair(p0)], 1: [start_pair(p1)], 2: [p0.normalize], 3: [gate_norm, start_pair(p2), p1.normalize],
            4: [gate_scale], 5: [start_pair(p3), gate_mix, p2.normalize], 6: [p0.turn], 7: [p1.turn, p3.normalize],
            8: [finish_pair(p0), finish_pair(p1)], 9: [p2.turn, p3.turn], 10: [finish_pair(p2), finish_pair(p3)],
            12: [conv_center], 13: [conv_norm]}

    def follow(unit):
        for step in plan.get(unit, ()):
            step()

    b0 = 2 * parity[0]
    parity[0] ^= 1
    claim(b0, b0 + 1)

    def unit_mixed(slot, k0, first, last):
        unit_features(slot, k0, h_hi, h_lo, [bank[b0]], first, last, tiles=2)
        return unit_tokens(slot, k0, h_hi, h_lo, [bank[b0 + 1][:, 0:S], bank[b0 + 1][:, S:2 * S]], first, last,
                           cols=slice(S, 2 * S), start_first=False)
    for j in range(RING):
        late["gelu"] = next_unit(unit_mixed, UK * j, first=(j == 0), last=(j == RING - 1),
                                 finish=(lambda ps: take_gelu(b0, ps)) if j == RING - 1 else None)
        follow(j)
    v_ok = slab(unit_tokens, h_hi, h_lo, between=lambda j: follow(RING + j), finish=evac_to(lambda i: v_tok[:, i, :]))

    tiles_of = {0: 4, 1: 0, 2: 2, 3: 6}
    claim(0, 1, 2, 3)
    for i, (n, k) in enumerate(OUT2_ORDER):
        if k == 0:
            wait(pe, late["ya"])
        elif k == 3:
            wait(pe, late["yc"])
        else:
            wait(pe, pairs2[2 * k - 2].branch_ok, pairs2[2 * k - 1].branch_ok)
        half_done = next_unit(unit_tokens, tiles_of[k], br_hi, br_lo, [bank[2 * n][:, :], bank[2 * n + 1][:, :]],
                              first=(k == 0), last=(k == 3), finish=(lambda ps: post_half(
                                  n, (2 * n, 2 * n + 1), ps, rows[:, 0, :], row_post_mix)) if k == 3 else None)
        follow(2 * RING + i)
    parity[0] = 0
    x_ok = post_sum(*half_done)
    wait(act, *x_ok[1])
    row_post_ff = load_row(rows[:, 0, :], "post_ffn_g_2")

    h_ready = gain_and_split(turn(pre_norm(x, x_ok)), cols[:, G_X2:G_X2 + KD], h_hi, h_lo)
    xq = mix

    mx, negmx, rsum = att[:, 0:2], att[:, 2:4], att[:, 4:6]

    def xscores(h):
        b = 4 + h % 2
        claim(b)
        wait(pe, *xq_ok[h // 2])
        for tt in range(NT):
            for c in range(2):
                mm = pe.matmul(bank[b][:, tt * S:tt * S + S], xq[:, 2 * h + c, tt * P:tt * P + P],
                               mem_k[:, 2 * h + c, :], start=(c == 0), stop=(c == 1))
        ps = done(mm, PE)
        wait(dve, ps)
        for tt in range(NT):
            m = AV(dve.tensor_reduce(mx[:, tt:tt + 1], bank[b][:, tt * S:tt * S + S], AX.X, ALU.max))
        wait(dve, m)
        m = AV(dve.tensor_scalar(negmx[:, 0:2], mx[:, 0:2], -1.0 / 16, None, ALU.mult))
        wait(act, m)
        pr = xprob[h % 2]
        for tt in range(NT):
            m = AA(act.activation(pr[:, tt, :], bank[b][:, tt * S:tt * S + S], ACT.Exp, bias=negmx[:, tt:tt + 1],
                                  scale=1.0 / 16, accum_out=rsum[:, tt:tt + 1]))
        bank_free[b] = [m]
        wait(dve, m)
        then_v(dve.reciprocal(rsum[:, 0:2], rsum[:, 0:2]))
        for tt in range(NT):
            m = AV(dve.tensor_scalar(pr[:, tt, :], pr[:, tt, :], rsum[:, tt:tt + 1], None, ALU.mult))
        return m

    def xattend(h, prob_ok):
        pr = xprob[h % 2]
        claim(6)
        wait(pe, prob_ok)
        for kt in range(NT):
            for tt in range(NT):
                c0 = kt * S + tt * P
                mm = pe.transpose(bank[6][:, c0:c0 + P], pr[:, tt, kt * P:kt * P + P], ident[:, :])
        ps = done(mm, PE)
        wait(act, ps)
        m = AA(act.copy(probT[:, h % 2, :], bank[6][:, :]))
        bank_free[6] = [m]
        claim(7)
        wait(pe, m)
        for c in range(2):
            for kt in range(NT):
                fc = slice(h * XD + c * P, h * XD + c * P + P)
                mm = pe.matmul(bank[7][:, c * S:c * S + S], mem_v[:, kt, fc], probT[:, h % 2, kt * S:kt * S + S],
                               start=(kt == 0), stop=(kt == 1))
        return to_branch(7, slice(0, 2 * S), 2 * h, done(mm, PE), n=2)

    xprob = [gates[:, 16:18], gates[:, 18:20]]
    xq_ok = [slab(unit_features, h_hi, h_lo, before=wait_chunks(h_ready), finish=evac_to(lambda i: pair(xq, 2 * i)))]
    xp = {}

    def between(j):
        if j == 0:
            xp[0] = xscores(0)
        if j == 1:
            xp[1] = xscores(1)
        if j == 3:
            xp["o0"] = xattend(0, xp[0])
    xq_ok.append(slab(unit_features, h_hi, h_lo, between=between, finish=evac_to(lambda i: pair(xq, 4 + 2 * i))))
    xp[2] = xscores(2)
    xp["o1"] = xattend(1, xp[1])
    xp[3] = xscores(3)
    xp["o2"] = xattend(2, xp[2])
    xp["o3"] = xattend(3, xp[3])
    x_ok = out_projection(br_hi, br_lo, rows[:, 1, :], row_post_x, before=lambda j: wait(pe, xp[f"o{j}"]))

    h_ready = gain_and_split(turn(pre_norm(x, x_ok)), cols[:, G_FF2:G_FF2 + KD], h_hi, h_lo)
    x_ok = feed_forward("ff2", h_ready, rows[:, 0, :], row_post_ff)
    ld_out = arrivals("out_done")
    for tt in range(NT):
        wait(sp, *x_ok[tt])
        out_done = ld_out(sp, out[0][tt * P:tt * P + P, :], x[:, tt, :])
    wait(sp, out_done)
    assert at[0] == UNITS and split_at[0] == UNITS, (at, split_at, UNITS)


_INS = ["x", "c", "w_ada", "b_ada", "g_mix_pre", "g_mix_post", "g_ff_pre", "g_ff_post", "w_in", "b_f", "w_pool",
        "pool_scale", "conv_w", "w_branch", "w_out", "w_ff1", "w_ff2", "mem_2", "pre_mix_g_2", "w_in_2",
        "gate_ln_g_2", "gate_ln_b_2", "w_s_2", "b_s_2", "w_dw_2", "b_dw_2", "conv_gn_g_2", "conv_gn_b_2", "w_out_2",
        "post_mix_g_2", "pre_x_g_2", "mem_g_2", "w_xq_2", "w_xkv_2", "w_xo_2", "post_x_g_2", "pre_ffn_g_2",
        "w_ff1_2", "w_ff2_2", "post_ffn_g_2"]


def kernel(**inputs):
    import concourse.bacc as bacc
    from concourse.bass_utils import run_bass_kernel_spmd

    nc = bacc.Bacc("TRN2", target_bir_lowering=False, num_devices=1)
    arrays, aps = {}, {}
    for name in _INS:
        a = np.ascontiguousarray(inputs[name])
        arrays[f"in_{name}"] = a
        aps[name] = nc.dram_tensor(f"in_{name}", a.shape, mybir.dt.from_np(a.dtype), kind="ExternalInput").ap()
    out = nc.dram_tensor("out", (1, S, D), F32, kind="ExternalOutput").ap()
    packed = {"columns": np.ascontiguousarray(np.concatenate([np.asarray(inputs[n]).reshape(-1, P)
                                                              for n, _ in COLUMNS]).T),
              "w_s_T": np.ascontiguousarray(np.asarray(inputs["w_s_2"])[0].transpose(2, 0, 1))}
    for name, a in packed.items():
        arrays[f"in_{name}"] = a
        aps[name] = nc.dram_tensor(f"in_{name}", a.shape, F32, kind="ExternalInput").ap()
    build(nc, aps, out)
    r = run_bass_kernel_spmd(nc, [arrays], core_ids=[0])
    return r.results[0]["out"]
```

```python
from contextlib import ExitStack, contextmanager

import numpy as np
import concourse.bass as bass
import concourse.mybir as mybir
from concourse.alu_op_type import AluOpType as ALU

F32 = mybir.dt.float32
F32R = mybir.dt.float32r
ACT = mybir.ActivationFunctionType
AX = mybir.AxisListType

P = 128
D = 1024
S = 256
NT = S // P
KD = D // P
UK = 2
UN = 512
RING = 4
NEG = -1e30
EPS = 1e-6
NH, DH = 8, 64
XH, XD = 4, 256
WINDOWS = (2, 4, 8, 16)
TAPS3, TAPS31 = 3, 31
A_SLABS = 12
COLUMNS = (("c", 8), ("mem_g_2", 8), ("g_mix_pre", 8), ("b_ada", 48), ("g_ff_pre", 8), ("pre_mix_g_2", 8),
           ("pre_x_g_2", 8), ("pre_ffn_g_2", 8), ("w_dw_2", 62), ("conv_w", 6), ("pool_scale", 2), ("b_dw_2", 2),
           ("conv_gn_g_2", 2), ("conv_gn_b_2", 2))
COL_AT = dict(zip([n for n, _ in COLUMNS], np.cumsum([0] + [k for _, k in COLUMNS]).tolist()))
N_COLS = sum(k for _, k in COLUMNS)
G_MEM, G_MIX, B_ADA, G_FF, G_MIX2, G_X2, G_FF2 = (COL_AT[n] for n in (
    "mem_g_2", "g_mix_pre", "b_ada", "g_ff_pre", "pre_mix_g_2", "pre_x_g_2", "pre_ffn_g_2"))
W_DW, W_CONV, C_POOL, C_BDW, C_GNG, C_GNB = (COL_AT[n] for n in (
    "w_dw_2", "conv_w", "pool_scale", "b_dw_2", "conv_gn_g_2", "conv_gn_b_2"))


class Counter:

    def __init__(self, sem):
        self.sem, self.n, self.turn, self.per = sem, 0, None, 0

    def value(self):
        return self.n if self.turn is None else self.turn * self.per + self.n


def done(instruction, counter):
    instruction.then_inc(counter.sem, 1)
    counter.n += 1
    return (counter, counter.value())


def wait(engine, *marks):
    for counter, value in marks:
        engine.wait_ge(counter.sem, value)


@contextmanager
def loop(nc, turns, rates):
    starts = {c: c.n for c in rates}
    with nc.Fori(0, turns) as turn:
        for c, per in rates.items():
            c.turn, c.per = turn, per
        yield turn
        for c, per in rates.items():
            assert c.n - starts[c] == per, (c.n - starts[c], per)
    for c, per in rates.items():
        c.turn, c.n = None, starts[c] + per * turns


def as_f32(ap):
    return ap.bitcast(F32)


def build(nc, t, out):
    with ExitStack() as ctx:
        emit(nc, t, out, ctx)


def emit(nc, t, out, ctx):
    pe, act, dve, pool, sp = nc.tensor, nc.scalar, nc.vector, nc.gpsimd, nc.sync

    def sb(name, shape, dt=F32):
        return ctx.enter_context(nc.sbuf_tensor(name, [P] + shape, dt))

    def counter(name):
        return Counter(ctx.enter_context(nc.semaphore(name)))

    raw = sb("raw_ring", [RING, UK, UN])
    hi = sb("hi_ring", [RING, UK, UN], F32R)
    lo = sb("lo_ring", [RING, UK, UN], F32R)
    ada_raw = sb("ada_ring", [2, UK, UN])
    ada_acc = sb("ada_acc", [4, UN])
    x = sb("x_residual", [NT, D])
    h_f32 = sb("h_f32", [KD, S])
    h_hi = sb("h_hi", [KD, S], F32R)
    h_lo = sb("h_lo", [KD, S], F32R)
    br_hi = sb("branch_hi", [KD, S], F32R)
    br_lo = sb("branch_lo", [KD, S], F32R)
    mem_k = sb("mem_k", [KD, S])
    mem_v = sb("mem_v", [NT, D])
    gates = sb("gates", [3 * KD, S])
    qT = sb("q_T", [4, S])
    kT = sb("k_T", [4, S])
    v_tok = sb("v_tok", [NT, NH * DH])
    mix = sb("mix", [KD, S])
    soft = sb("softmax", [2, 384])
    probT = sb("prob_T", [2, 512])
    rows = sb("post_rows", [2, D])
    rowtmp = sb("row_tmp", [D])
    pad_u = sb("pad_u", [2, 30 + S])
    win_a = gates[:, 12:14].rearrange("p a s -> p (a s)")
    win_b = gates[:, 14:16].rearrange("p a s -> p (a s)")
    ident = sb("ident", [P])
    ones = sb("ones", [P])
    upper = sb("upper_ones", [2 * P])
    mask = sb("mask", [S])
    dist = sb("neg_dist", [S])
    blockmean = sb("block_mean", [P])
    cols = sb("vector_columns", [N_COLS])
    half = sb("minus_half", [KD])
    adacol = sb("ada_cols", [32])
    silu_c = sb("silu_c", [KD])
    stat = sb("stat", [32])
    att = sb("softmax_stats", [48])
    stats6 = sb("bn_stats", [2, 6])
    w_fl = sb("w_fl", [KD, NH])
    fl = sb("forget_logits", [NT, NH])
    logf = sb("log_f", [NT, NH])
    tmp16 = sb("tmp16", [3, NT * NH])
    nlogf8 = sb("minus_8_log_f", [NT, NH])
    cum8 = sb("cum_log_f_8", [NT, NH])
    bf_row = sb("b_f_row", [NH])
    rcount = sb("pool_rcount", [2, S])
    cnt16 = att[:, :].rearrange("p (a w) -> p a w", w=16)
    wpool = sb("w_pool_blocks", [2, P])
    ws_T = sb("w_s_T", [4, P])
    bs_row = sb("b_s_rows", [2, P])
    ln_rows = sb("gate_ln_rows", [2, 256])

    bank = [ctx.enter_context(nc.psum_tensor(f"bank{b}", [P, UN], F32)) for b in range(8)]

    raw_in = [ctx.enter_context(nc.semaphore(f"raw_in{j}")) for j in range(RING)]
    ada_in = [ctx.enter_context(nc.semaphore(f"ada_in{j}")) for j in range(2)]
    hi_done = ctx.enter_context(nc.semaphore("hi_done"))
    lo_done = ctx.enter_context(nc.semaphore("lo_done"))
    used = ctx.enter_context(nc.semaphore("used"))
    ada_used = ctx.enter_context(nc.semaphore("ada_used"))
    PE, AC, VE, PO = counter("pe_done"), counter("act_done"), counter("dve_done"), counter("pool_done")

    def arrivals(name):
        c = counter(name)

        def start(engine, dst, src):
            engine.dma_start(dst, src).then_inc(c.sem, 16)
            c.n += 16
            return (c, c.n)
        return start

    def AV(ins):
        return done(ins, VE)

    def AA(ins):
        return done(ins, AC)

    def then_v(ins):
        m = done(ins, VE)
        wait(dve, m)
        return m

    def then_a(ins):
        m = done(ins, AC)
        wait(act, m)
        return m

    def unit_rows(w, r0, c0):
        return w[bass.ds(r0, UK * P), bass.ds(c0, UN)].rearrange("(k p) n -> p k n", p=P)

    def load(u, slot, src):
        if not (isinstance(u, int) and u < RING):
            sp.wait_ge(lo_done, u - (RING - 1))
        sp.dma_start(raw[:, slot], src).then_inc(raw_in[slot], 16)

    def load_ada(a, src):
        u, slot = a
        if not (isinstance(u, int) and u < 2):
            sp.wait_ge(ada_used, u - 1)
        sp.dma_start(ada_raw[:, slot], src).then_inc(ada_in[slot], 16)

    def load_slabs(u0, slabs, w, c0=0, ada0=None):
        def one(i):
            for j in range(RING):
                load(i * RING + (u0 + j), j, unit_rows(w, j * UK * P, i * UN + c0))
                if ada0 is not None:
                    load_ada((i * RING + (ada0 * RING + j), j % 2),
                             unit_rows(t["w_ada"][0], j * UK * P, i * UN + ada0 * UN))
        peel = 1 if u0 == 0 or slabs == 1 else 0
        if peel:
            one(0)
        if slabs > peel:
            with sp.Fori(peel, slabs) as i:
                one(i)
        return u0 + slabs * RING

    def load_pairs(u0, pairs, w, ada0, c0=0):
        def one(i):
            for j in range(2 * RING):
                load(i * (2 * RING) + (u0 + j), j % RING,
                     unit_rows(w, (j % RING) * UK * P, i * (2 * UN) + (j // RING * UN + c0)))
                if j % 2:
                    load_ada((i * RING + (ada0 * RING + j // 2), j // 2 % 2),
                             unit_rows(t["w_ada"][0], j // 2 * UK * P, i * UN + ada0 * UN))
        if pairs == 1:
            one(0)
        else:
            with sp.Fori(0, pairs) as i:
                one(i)
        return u0 + pairs * 2 * RING

    def load_list(u0, srcs):
        for n, src in enumerate(srcs):
            load(u0 + n, (u0 + n) % RING, src)
        return u0 + len(srcs)

    mem = gates[:, 8:16].rearrange("p a s -> p (a s)").rearrange("p (a d) -> p a d", a=NT)
    mem_in = [[arrivals(f"mem_in{tt}")(act, mem[:, tt, :], t["mem_2"][0][tt * P:tt * P + P, :])] for tt in range(NT)]
    cols_in = arrivals("cols_in")(act, cols[:, :], t["columns"])
    x_in = arrivals("x_in")(act, x[:, :, :], t["x"][0].rearrange("(a p) d -> p a d", p=P))
    ld_sm = arrivals("small_in")
    ld_sm(act, w_fl[:, :, :], t["w_in"][0][:, 3 * NH * DH:3 * NH * DH + NH].rearrange("(k p) n -> p k n", p=P))
    ld_sm(act, bf_row[:, :], t["b_f"][0:1, :].broadcast_to([P, NH]))
    ld_sm(act, ws_T[:, :, :], t["w_s_T"])
    for h in range(4):
        ld_sm(act, bs_row[64 * (h % 2):64 * (h % 2) + 64, h // 2, :],
              t["b_s_2"][0][h:h + 1, :].broadcast_to([64, P]))
    ld_sm(act, ln_rows[:, 0, :], t["gate_ln_g_2"].broadcast_to([P, 256]))
    small_in = ld_sm(act, ln_rows[:, 1, :], t["gate_ln_b_2"].broadcast_to([P, 256]))

    w_in, w_in2, w_br = t["w_in"][0], t["w_in_2"][0], t["w_branch"][0]
    u = load_slabs(0, 4, t["w_xkv_2"][0], ada0=0)
    u = load_slabs(u, 1, w_in)
    u = load_slabs(u, 2, w_in, c0=UN, ada0=4)
    u = load_pairs(u, 4, w_in, 6, c0=1544)
    u = load_pairs(u, 1, w_br, 10)
    u = load_pairs(u, 1, t["w_out"][0], 11)

    FF_STEPS = 8

    def load_ff(u, w1, w2):
        u = load_slabs(u, 1, w1)
        with sp.Fori(0, FF_STEPS - 1) as i:
            for j in range(RING):
                load(i * (2 * RING) + (u + j), j, unit_rows(w1, j * UK * P, i * UN + UN))
            for j in range(RING):
                load(i * (2 * RING) + (u + RING + j), j, unit_rows(w2, i * UN + (j % 2) * UK * P, (j // 2) * UN))
        u += (FF_STEPS - 1) * 2 * RING
        return load_list(u, [unit_rows(w2, (FF_STEPS - 1) * UN + (j % 2) * UK * P, (j // 2) * UN)
                             for j in range(RING)])
    u = load_ff(u, t["w_ff1"][0], t["w_ff2"][0])
    for c0 in (2048, 512, 1024, 0, 1536):
        u = load_slabs(u, 1, w_in2, c0=c0)
    OUT2_ORDER = [(n, k) for k in (1, 0, 2, 3) for n in (0, 1)]
    u = load_list(u, [unit_rows(t["w_out_2"][0], k * UK * P, n * UN) for n, k in OUT2_ORDER])
    u = load_slabs(u, 2, t["w_xq_2"][0])
    XO_ORDER = [(n, k) for k in range(4) for n in (0, 1)]
    u = load_list(u, [unit_rows(t["w_xo_2"][0], k * UK * P, n * UN) for n, k in XO_ORDER])
    u = load_ff(u, t["w_ff1_2"][0], t["w_ff2_2"][0])
    UNITS = u

    def then_p(ins):
        m = done(ins, PO)
        wait(pool, m)
        return m

    then_p(pool.memset(ident[:, :], 0.0))
    ident_ok = then_p(pool.affine_select(out=ident[:, :], in_=ident[:, :], compare_op=ALU.not_equal, fill=1.0, base=0,
                                       pattern=[[-1, P]], channel_multiplier=1))
    then_p(pool.memset(half[:, :], -0.5))

    split_at = [0]
    ada_sum = {"slab": 0, "kc": 0, "last": None, "free": [None] * 4, "ready": {}}

    def ada_op():
        a, kc = ada_sum["slab"], ada_sum["kc"]
        if a >= A_SLABS:
            return
        unit, k = a * RING + kc // UK, kc % UK
        acc = ada_acc[:, a % 4, :]
        if k == 0:
            dve.wait_ge(ada_in[unit % 2], 16 * (unit // 2 + 1))
        w = ada_raw[:, unit % 2, k, :]
        if kc == 0:
            if ada_sum["free"][a % 4]:
                wait(dve, ada_sum["free"][a % 4])
            ins = dve.tensor_scalar(acc, w, silu_c[:, 0:1], None, ALU.mult)
        else:
            wait(dve, ada_sum["last"])
            ins = dve.scalar_tensor_tensor(out=acc, in0=w, scalar=silu_c[:, kc:kc + 1], in1=acc,
                                           op0=ALU.mult, op1=ALU.add)
        ada_sum["last"] = AV(ins)
        if k == UK - 1:
            wait(dve, ada_sum["last"])
            dve.sem_inc(ada_used, 1)
        ada_sum["kc"] += 1
        if ada_sum["kc"] == KD:
            ada_sum["ready"][a] = ada_sum["last"]
            ada_sum["slab"], ada_sum["kc"] = a + 1, 0

    def split(u, slot):
        first = isinstance(u, int) and u < RING
        act.wait_ge(raw_in[slot], (u - slot) * (16 // RING) + 16)
        if not first:
            act.wait_ge(used, u - (RING - 1))
        act.copy(hi[:, slot], raw[:, slot]).then_inc(hi_done, 1)
        dve.wait_ge(hi_done, u + 1)
        dve.tensor_tensor(lo[:, slot], raw[:, slot], as_f32(hi[:, slot]), ALU.subtract).then_inc(lo_done, 1)

    def split_next():
        if split_at[0] < UNITS:
            split(split_at[0], split_at[0] % RING)
            n = split_at[0] // RING
            for _ in range(2 if n < 4 or n in (5, 6) else 0 if n == 4 else 1):
                ada_op()
            split_at[0] += 1
            for queue, n in ((background, 3), (pool_background, 2)):
                for _ in range(min(len(queue), n)):
                    queue.pop(0)()

    background, pool_background = [], []

    bank_free = [[] for _ in range(8)]

    def claim(*banks):
        for b in banks:
            wait(pe, *bank_free[b])
            bank_free[b] = []

    def three_passes(out_ap, a_hi, a_lo, b_hi, b_lo, start, stop, skip=False):
        pe.matmul(out_ap, a_hi, b_hi, start=start, stop=False, skip_group_check=skip)
        pe.matmul(out_ap, a_hi, b_lo, start=False, stop=False, skip_group_check=skip)
        return pe.matmul(out_ap, a_lo, b_hi, start=False, stop=stop, skip_group_check=skip)

    def unit_tokens(slot, k0, in_hi, in_lo, outs, first, last, cols=slice(0, UN), start_first=True):
        for k in range(UK):
            for tt in range(NT):
                tok = slice(tt * P, tt * P + P)
                mm = three_passes(outs[tt], in_hi[:, k0 + k, tok], in_lo[:, k0 + k, tok], hi[:, slot, k, cols],
                                  lo[:, slot, k, cols], first and k == 0 and (start_first or tt == 0),
                                  last and k == UK - 1, skip=True)
        return mm

    def unit_features(slot, k0, in_hi, in_lo, banks, first, last, tiles=4):
        for k in range(UK):
            for f in range(tiles):
                o = banks[f // 2][:, (f % 2) * S:(f % 2) * S + S]
                fc = slice(f * P, f * P + P)
                mm = three_passes(o, hi[:, slot, k, fc], lo[:, slot, k, fc], in_hi[:, k0 + k, :], in_lo[:, k0 + k, :],
                                  first and k == 0 and f % 2 == 0, last and k == UK - 1, skip=True)
        return mm

    at = [0]
    parity = [0]

    def next_unit(kind, *args, finish=None, last_of_all=False, **kw):
        u = at[0]
        slot = u % RING
        pe.wait_ge(lo_done, u + 1)
        kind(slot, *args, **kw).then_inc(used, 1)
        at[0] += 1
        result = finish(used_up_to(at[0])) if finish else None
        if not last_of_all:
            split_next()
        return result

    def used_up_to(u):
        return (UsedMark, u)

    UsedMark = Counter(used)

    def slab(kind, in_hi, in_lo, between=None, before=None, finish=None, last_of_all=False):
        b0 = 2 * parity[0]
        parity[0] ^= 1
        claim(b0, b0 + 1)
        for j in range(RING):
            if before:
                before(j)
            result = next_unit(kind, UK * j, in_hi, in_lo, [bank[b0], bank[b0 + 1]] if kind is unit_features
                      else [bank[b0][:, :], bank[b0 + 1][:, :]], first=(j == 0), last=(j == RING - 1),
                      finish=(lambda ps: finish(b0, ps)) if j == RING - 1 else None,
                      last_of_all=last_of_all and j == RING - 1)
            if between:
                between(j)
        return result

    wait(act, cols_in)
    silu_ok = AA(act.activation(silu_c[:, :], cols[:, 0:KD], ACT.Silu))

    def rstd_of(sumsq, tmp, out_ap, n, ready):
        wait(pool, *ready)
        then_p(pool.tensor_scalar(tmp, sumsq, 1.0 / n, EPS, ALU.mult, ALU.add))
        return then_p(pool.tensor_tensor(out_ap, tmp, half[:, 0:out_ap.shape[1]], ALU.pow))

    NORM = gates[:, 0:8].rearrange("p a s -> p (a s)").rearrange("p (a d) -> p a d", a=NT)
    JUNK = gates[:, 20:24].rearrange("p a s -> p (a s)")

    def pre_norm(src, ready):
        normed = []
        for tt in range(NT):
            wait(act, *ready[tt])
            sq = AA(act.activation(JUNK, src[:, tt, :], ACT.Square, accum_out=stat[:, tt:tt + 1]))
            wait(act, sq)
            rs = rstd_of(stat[:, tt:tt + 1], stat[:, 2 + tt:3 + tt], stat[:, 4 + tt:5 + tt], D, [sq])
            wait(dve, *ready[tt], rs)
            normed.append(AV(dve.tensor_scalar(NORM[:, tt, :], src[:, tt, :], stat[:, 4 + tt:5 + tt], None, ALU.mult)))
        return normed

    def sums_to_rstd(src, ready):
        for tt in range(NT):
            wait(act, *ready[tt])
            sq = AA(act.activation(JUNK, src[:, tt, :], ACT.Square, accum_out=stat[:, tt:tt + 1]))
            wait(act, sq)
        return rstd_of(stat[:, 0:2], stat[:, 2:4], R_TOKEN, D, [sq])

    R_TOKEN = stat[:, 4:6]

    def turn(normed, src=None):
        src = NORM if src is None else src
        claim(4, 5, 6, 7)
        turned = []
        for tt in range(NT):
            wait(pe, *(normed[tt] if isinstance(normed[tt], list) else [normed[tt]]))
            for k in range(KD):
                c0 = (k % 2) * S + tt * P
                mm = pe.transpose(bank[4 + k // 2][:, c0:c0 + P], src[:, tt, k * P:k * P + P], ident[:, :])
                if tt == NT - 1 and k % 2:
                    turned.append(done(mm, PE))
        return turned

    def chunk_ps(k):
        return bank[4 + k // 2][:, (k % 2) * S:(k % 2) * S + S]

    def gain_and_split(turned, gain, dst_hi, dst_lo):
        marks = []
        for b in range(KD // 2):
            wait(act, turned[b])
            for k in (2 * b, 2 * b + 1):
                m = AA(act.activation(dst_hi[:, k, :], chunk_ps(k), ACT.Copy, scale=gain[:, k:k + 1]))
            wait(dve, m)
            for k in (2 * b, 2 * b + 1):
                m = AV(dve.scalar_tensor_tensor(out=dst_lo[:, k, :], in0=chunk_ps(k), scalar=gain[:, k:k + 1],
                                                in1=as_f32(dst_hi[:, k, :]), op0=ALU.mult, op1=ALU.subtract))
            bank_free[4 + b] = [m]
            marks.append(m)
        return lambda k: marks[k // 2]

    def affine_and_split(turned, gain, shift):
        f32 = []
        for k in range(KD):
            wait(act if (k // 2) % 2 == 0 else dve, turned[k // 2])
            if (k // 2) % 2 == 0:
                f32.append(AA(act.activation(h_f32[:, k, :], chunk_ps(k), ACT.Identity, bias=shift[:, k:k + 1],
                                             scale=gain[:, k:k + 1])))
            else:
                f32.append(AV(dve.tensor_scalar(h_f32[:, k, :], chunk_ps(k), gain[:, k:k + 1], shift[:, k:k + 1],
                                                ALU.mult, ALU.add)))
            bank_free[4 + k // 2] = [f32[k]]
        marks = [split_act(slice(k, k + 2), f32[k + 1]) for k in range(0, KD, 2)]
        return lambda k: marks[k // 2]

    def split_act(ks, ready, src=None, dst_hi=None, dst_lo=None):
        src = h_f32 if src is None else src
        dst_hi = h_hi if dst_hi is None else dst_hi
        dst_lo = h_lo if dst_lo is None else dst_lo
        wait(dve, ready)
        then_v(dve.tensor_copy(dst_hi[:, ks, :], src[:, ks, :]))
        return AV(dve.tensor_tensor(dst_lo[:, ks, :], src[:, ks, :], as_f32(dst_hi[:, ks, :]), ALU.subtract))

    def evac_to(dst, scalar_only=False):
        return lambda b0, ready: evac_copy(b0, ready, dst, scalar_only)

    def evac_copy(b0, ready, dst, scalar_only=False):
        wait(act, ready)
        m0 = AA(act.copy(dst(0), bank[b0][:, :]))
        if scalar_only:
            m1 = AA(act.copy(dst(1), bank[b0 + 1][:, :]))
        else:
            wait(dve, ready)
            m1 = AV(dve.tensor_copy(dst(1), bank[b0 + 1][:, :]))
        bank_free[b0], bank_free[b0 + 1] = [m0], [m1]
        return [m0, m1]

    def pair(buf, k):
        return buf[:, k:k + 2].rearrange("p a s -> p (a s)")

    wait(act, cols_in)
    wait(dve, cols_in)
    wait(pe, ident_ok)
    turned = turn(pre_norm(mem, mem_in))
    wait(dve, silu_ok)
    split_next()
    m_ready = gain_and_split(turned, cols[:, G_MEM:G_MEM + KD], br_hi, br_lo)
    for _ in range(RING - 1):
        split_next()

    then_p(pool.memset(ones[:, :], 1.0))
    then_p(pool.memset(upper[:, :], 1.0))
    upper_ok = then_p(pool.affine_select(out=upper[:, 0:P], in_=upper[:, 0:P], compare_op=ALU.is_ge, fill=0.0, base=0,
                                       pattern=[[1, P]], channel_multiplier=-1))
    then_p(pool.memset(mask[:, :], 0.0))
    mask_ok = then_p(pool.affine_select(out=mask[:, :], in_=mask[:, :], compare_op=ALU.is_ge, fill=8 * NEG, base=P,
                                      pattern=[[-1, S]], channel_multiplier=1))
    then_p(pool.iota(dist[:, :], pattern=[[1, S]], base=-P, channel_multiplier=-1,
                     allow_small_or_imprecise_dtypes=True))
    dist_ok = then_p(pool.affine_select(out=dist[:, :], in_=dist[:, :], compare_op=ALU.is_ge, fill=NEG, base=P,
                                      pattern=[[-1, S]], channel_multiplier=1))
    then_p(pool.memset(blockmean[:, :], 0.0))
    then_p(pool.memset(blockmean[0:64, 0:64], 1.0 / 64))
    then_p(pool.memset(blockmean[64:128, 64:128], 1.0 / 64))
    wp_zero = then_p(pool.memset(wpool[:, :, :], 0.0))
    ld_wp = arrivals("w_pool_in")
    for g in range(4):
        s = 64 * (g % 2)
        wpool_in = ld_wp(pool, wpool[s:s + 64, g // 2, s:s + 64], t["w_pool"][0][g])
    then_p(pool.iota(cnt16[:, 2, :], pattern=[[1, 16]], base=1, channel_multiplier=0,
                               allow_small_or_imprecise_dtypes=True))
    for g, w in enumerate(WINDOWS):
        s = 64 * (g % 2)
        then_p(pool.memset(rcount[s:s + 64, g // 2, 16:S], 1.0 / w))
        then_p(pool.tensor_scalar(cnt16[s:s + 64, g // 2, :], cnt16[s:s + 64, 2, :], float(w), None, ALU.min))
    pool_consts = then_p(pool.memset(pad_u[:, :, :], 0.0))
    wait(pool, small_in)
    wsT_ok = then_p(pool.affine_select(out=ws_T[:, :, :], in_=ws_T[:, :, :], compare_op=ALU.is_ge, fill=0.0, base=0,
                                       pattern=[[0, 4], [1, P]], channel_multiplier=-1))


    def wait_chunks(ready_of):
        return lambda j: wait(pe, ready_of(UK * j))

    x_normed = None
    for n in range(2):
        slab(unit_features, br_hi, br_lo, before=wait_chunks(m_ready) if n == 0 else None,
             finish=evac_to(lambda i: pair(mem_k, 4 * n + 2 * i), scalar_only=True))
        if n == 0:
            x_normed = pre_norm(x, [[x_in], [x_in]])
        else:
            x_turned = turn(x_normed)
    wait(dve, pool_consts)
    rcount_ok = AV(dve.reciprocal(rcount[:, :, 0:16], cnt16[:, 0:2, :]))
    def ada_columns(slot, n_slabs, b, c0):
        for s in range(n_slabs):
            for j in range(4):
                mm = pe.matmul(bank[b][:, c0 + 4 * s + j:c0 + 4 * s + j + 1], ada_acc[:, slot + s, j * P:j * P + P],
                               ones[:, 0:1], start=True, stop=True, skip_group_check=True)
        return done(mm, PE)

    def load_row(dst, name, c0=0, group=None):
        return (group or arrivals(name + "_row_in"))(act, dst, t[name][0:1, c0:c0 + D].broadcast_to([P, D]))

    def ada_row(slot, dst, gain_in, b0):
        claim(b0, b0 + 1)
        for s in range(2):
            mm = pe.matmul(bank[b0 + s][:, :], ones[:, :], ada_acc[:, slot + s, :], start=True, stop=True)
        ps = done(mm, PE)
        wait(dve, ps, gain_in)
        for s in range(2):
            cs = slice(s * UN, s * UN + UN)
            added = AV(dve.tensor_tensor(dst[:, cs], dst[:, cs], bank[b0 + s][:, :], ALU.add))
            wait(dve, added)
            bank_free[b0 + s] = [added]
            m = AV(dve.tensor_tensor(dst[:, cs], dst[:, cs], rowtmp[:, cs], ALU.mult))
        return ps, m

    slab(unit_tokens, br_hi, br_lo,
         finish=evac_to(lambda i: mem_v[:, i, 0:UN], scalar_only=True))

    def mixer_columns(j):
        if j != 1:
            return
        assert ada_sum["slab"] == 4
        wait(pe, ada_sum["ready"][3])
        b = 2 * parity[0]
        claim(b)
        ps = ada_columns(0, 4, b, 0)
        ada_sum["free"] = [ps] * 4
        wait(dve, ps)
        m = then_v(dve.tensor_tensor(adacol[:, 0:16], bank[b][:, 0:16], cols[:, B_ADA:B_ADA + 16], ALU.add))
        bank_free[b] = [m]
        m = then_v(dve.scalar_tensor_tensor(out=adacol[:, 8:16], in0=adacol[:, 8:16], scalar=1.0,
                                            in1=cols[:, G_MIX:G_MIX + KD], op0=ALU.add, op1=ALU.mult))
        wait(act, m)
        mixer_input.append(affine_and_split(x_turned, adacol[:, 8:16], adacol[:, 0:8]))

    mixer_input = []
    slab(unit_tokens, br_hi, br_lo, between=mixer_columns,
         finish=evac_to(lambda i: mem_v[:, i, UN:2 * UN], scalar_only=True))
    h_ready = mixer_input[0]

    q_ok = slab(unit_features, h_hi, h_lo, before=wait_chunks(h_ready),
         finish=evac_to(lambda i: pair(qT, 2 * i)))
    k_ok = slab(unit_features, h_hi, h_lo,
         finish=evac_to(lambda i: pair(kT, 2 * i)))
    claim(4)
    wait(pe, small_in)
    for tt in range(NT):
        for k in range(KD):
            mm = pe.matmul(bank[4][:, tt * NH:tt * NH + NH], h_f32[:, k, tt * P:tt * P + P], w_fl[:, k, :],
                           start=(k == 0), stop=(k == KD - 1))
    fl_ps = done(mm, PE)
    wait(dve, fl_ps, small_in)
    for tt in range(NT):
        m = AV(dve.tensor_tensor(fl[:, tt, :], bank[4][:, tt * NH:tt * NH + NH], bf_row[:, :], ALU.add))
    wait(dve, m)
    bank_free[4] = [m]
    flz = fl[:, :, :].rearrange("p a h -> p (a h)")
    then_v(dve.tensor_scalar(tmp16[:, 0, :], flz, -1.0, None, ALU.mult))
    m = then_v(dve.tensor_tensor(tmp16[:, 0, :], tmp16[:, 0, :], flz, ALU.min))
    wait(act, m)
    then_a(act.activation(tmp16[:, 1, :], tmp16[:, 0, :], ACT.Exp))
    m = AA(act.activation(tmp16[:, 0, :], tmp16[:, 1, :], ACT.Ln, bias=1.0))
    then_v(dve.tensor_scalar(tmp16[:, 2, :], flz, 0.0, None, ALU.min))
    wait(dve, m)
    lf = logf[:, :, :].rearrange("p a h -> p (a h)")
    then_v(dve.tensor_tensor(lf, tmp16[:, 2, :], tmp16[:, 0, :], ALU.subtract))
    nlogf_ok = AV(dve.tensor_scalar(nlogf8[:, :, :].rearrange("p a h -> p (a h)"), lf, -8.0, None, ALU.mult))
    v_ok = slab(unit_tokens, h_hi, h_lo,
         finish=evac_to(lambda i: v_tok[:, i, :]))
    claim(4)
    wait(pe, nlogf_ok)
    pe.matmul(bank[4][:, 0:NH], upper[:, 0:P], nlogf8[:, 0, :], start=True, stop=True)
    pe.matmul(bank[4][:, NH:2 * NH], ones[:, :], nlogf8[:, 0, :], start=True, stop=False)
    cum_ps = done(pe.matmul(bank[4][:, NH:2 * NH], upper[:, 0:P], nlogf8[:, 1, :], start=False, stop=True), PE)
    wait(dve, cum_ps)
    cum_ok = AV(dve.tensor_scalar(cum8[:, :, :].rearrange("p a h -> p (a h)"), bank[4][:, 0:2 * NH], -1.0, None,
                                  ALU.mult))
    bank_free[4] = [cum_ok]

    CUTS = ((0, P), (P, P + S))

    class HeadPair:

        def __init__(self, g, soft, turned, forget, logit_banks, banks):
            self.g, self.soft, self.turned, self.forget = g, soft, turned, forget
            self.logit_banks, self.banks = logit_banks, banks
            c = 12 * g
            self.mx, self.negmx, self.rsum = att[:, c:c + 4], att[:, c + 4:c + 8], att[:, c + 8:c + 12]

        def parts(self):
            for e in range(2):
                for tt, (c0, c1) in enumerate(CUTS):
                    yield e, tt, c0, c1

        def scores(self, first_waits):
            g, soft = self.g, self.soft
            claim(*self.logit_banks)
            wait(pe, *first_waits)
            for e, tt, c0, c1 in self.parts():
                rows_ = slice(64 * e, 64 * e + 64)
                b = bank[self.logit_banks[e]]
                mm = pe.matmul(b[:, c0:c1], qT[rows_, g, tt * P:tt * P + P], kT[rows_, g, 0:c1 - c0],
                               start=True, stop=not self.forget)
                if self.forget:
                    head = 2 * g + e
                    mm = pe.matmul(b[:, c0:c1], nlogf8[:, 0, head:head + 1].to_broadcast([P, P]),
                                   upper[:, 0:c1 - c0], start=False, stop=(tt == 0))
                    if tt == 1:
                        mm = pe.matmul(b[:, c0 + P:c1], nlogf8[:, 1, head:head + 1].to_broadcast([P, P]),
                                       upper[:, 0:P], start=False, stop=True)
            ps = done(mm, PE)
            wait(dve, ps)
            for e, tt, c0, c1 in self.parts():
                dst, src_ps = soft[:, e, c0:c1], bank[self.logit_banks[e]][:, c0:c1]
                keys = slice(P, S) if tt == 0 else slice(0, S)
                if self.forget:
                    m = AV(dve.scalar_tensor_tensor(out=dst, in0=src_ps, scalar=cum8[:, tt, 2 * g + e:2 * g + e + 1],
                                                    in1=mask[:, keys], op0=ALU.add, op1=ALU.add))
                else:
                    slope = 2.0 ** (-8.0 * (2 * g + e + 1) / NH)
                    m = AV(dve.scalar_tensor_tensor(out=dst, in0=dist[:, keys], scalar=8.0 * slope, in1=src_ps,
                                                    op0=ALU.mult, op1=ALU.add))
                bank_free[self.logit_banks[e]] = [m]
            wait(dve, m)
            for e, tt, c0, c1 in self.parts():
                i = 2 * e + tt
                m = AV(dve.tensor_reduce(self.mx[:, i:i + 1], soft[:, e, c0:c1], AX.X, ALU.max))
            wait(dve, m)
            self.max_ok = AV(dve.tensor_scalar(self.negmx, self.mx, -0.125, None, ALU.mult))

        def exponentials(self):
            wait(act, self.max_ok)
            for e, tt, c0, c1 in self.parts():
                i = 2 * e + tt
                m = AA(act.activation(self.soft[:, e, c0:c1], self.soft[:, e, c0:c1], ACT.Exp, bias=self.negmx[:, i:i + 1],
                                      scale=0.125, accum_out=self.rsum[:, i:i + 1]))
            self.exp_ok = m

        def reciprocals(self):
            wait(dve, self.exp_ok)
            self.rsum_ok = AV(dve.reciprocal(self.rsum, self.rsum))

        def normalize(self):
            wait(act, self.rsum_ok)
            for e, tt, c0, c1 in self.parts():
                i = 2 * e + tt
                m = AA(act.activation(self.soft[:, e, c0:c1], self.soft[:, e, c0:c1], ACT.Copy,
                                      scale=self.rsum[:, i:i + 1]))
            self.prob_ok = m

        def turn(self):
            claim(*self.banks)
            wait(pe, self.prob_ok)
            for e in range(2):
                for c in range(0, 3 * P, P):
                    mm = pe.transpose(bank[self.banks[e]][:, c:c + P], self.soft[:, e, c:c + P], ident[:, :])
            ps = done(mm, PE)
            wait(act, ps)
            m0 = AA(act.copy(self.turned[:, 0, :], bank[self.banks[0]][:, 0:384]))
            wait(dve, ps)
            m1 = AV(dve.tensor_copy(self.turned[:, 1, :], bank[self.banks[1]][:, 0:384]))
            bank_free[self.banks[1]] = [m1]
            self.turned_ok = [m0, m1]

        def attend(self, v_ready):
            wait(pe, *self.turned_ok, *v_ready)
            for e in range(2):
                vc = slice((2 * self.g + e) * DH, (2 * self.g + e) * DH + DH)
                o = bank[self.banks[0]][64 * e:64 * e + 64]
                pT = self.turned[:, e, :]
                pe.matmul(o[:, 0:P], v_tok[:, 0, vc], pT[:, 0:P], start=True, stop=True)
                pe.matmul(o[:, P:S], v_tok[:, 0, vc], pT[:, P:S], start=True, stop=False)
                mm = pe.matmul(o[:, P:S], v_tok[:, 1, vc], pT[:, S:S + P], start=False, stop=True)
            self.branch_ok = to_branch(self.banks[0], slice(0, S), self.g, done(mm, PE))

    def to_branch(b, cols, tile, ps, scale=None, n=1):
        dst_hi = br_hi[:, tile:tile + n].rearrange("p a s -> p (a s)")
        dst_lo = br_lo[:, tile:tile + n].rearrange("p a s -> p (a s)")
        wait(act, ps)
        if scale is None:
            m = AA(act.copy(dst_hi, bank[b][:, cols]))
            wait(dve, m)
            m = AV(dve.tensor_tensor(dst_lo, bank[b][:, cols], as_f32(dst_hi), ALU.subtract))
        else:
            m = AA(act.activation(dst_hi, bank[b][:, cols], ACT.Copy, scale=scale))
            wait(dve, m)
            m = AV(dve.scalar_tensor_tensor(out=dst_lo, in0=bank[b][:, cols], scalar=scale, in1=as_f32(dst_hi),
                                            op0=ALU.mult, op1=ALU.subtract))
        bank_free[b] = [m]
        return m

    def split_to_branch(src, tile, n, ready):
        return split_act(slice(tile, tile + n), ready, src=ShiftedTiles(src, tile), dst_hi=br_hi, dst_lo=br_lo)

    class ShiftedTiles:

        def __init__(self, src, tile):
            self.src, self.tile = src, tile

        def __getitem__(self, key):
            p, ks, c = key
            return self.src[p, ks.start - self.tile:ks.stop - self.tile, c]

    probT_pair = probT[:, :, 0:384]
    pairs1 = [HeadPair(g, soft, probT_pair, True, (4, 5), (6, 7)) for g in range(4)]
    att1_waits = [*q_ok, *k_ok, cum_ok, upper_ok, mask_ok]
    wait(dve, mask_ok)
    gate_m_row = rows[:, 0, :]
    mix_rows = arrivals("mix_rows_in")
    load_row(gate_m_row, "b_ada", 2 * D, mix_rows)
    row_in = load_row(rowtmp[:, :], "g_mix_post", 0, mix_rows)
    gate_rows = []

    def make_gate_m_row(j):
        if j == 1:
            assert ada_sum["slab"] >= 6
            wait(pe, ada_sum["ready"][5])
            gate_rows.append(ada_row(0, gate_m_row, row_in, 2 * parity[0]))
            ada_sum["free"][0:2] = [gate_rows[0][0]] * 2

    def attention1(unit):
        g, stage = unit // 6, unit % 6
        if g >= 4:
            return
        pr = pairs1[g]
        if stage == 0:
            pr.scores(att1_waits)
        if stage == 1:
            pr.exponentials()
        if stage == 2:
            pr.reciprocals()
        if stage == 3:
            pr.normalize()
        if stage == 4:
            pr.turn()
        if stage == 5:
            pr.attend(v_ok)

    mixA_ok = slab(unit_features, h_hi, h_lo, between=make_gate_m_row, finish=evac_to(lambda i: pair(mix, 2 * i)))
    mixB_ok = slab(unit_features, h_hi, h_lo, between=attention1, finish=evac_to(lambda i: pair(mix, 4 + 2 * i)))
    _, row0_ok = gate_rows[0]

    wait(pool, *mixA_ok, rcount_ok)
    pooled = gates[:, 18:20]
    PADW = 16
    for tile in range(2):
        then_p(pool.memset(win_a[:, 0:PADW], 0.0))
        then_p(pool.memset(win_b[:, 0:PADW], 0.0))
        then_p(pool.tensor_copy(pad_u[:, tile, PADW:PADW + S], mix[:, tile, :]))
        src = pad_u[:, tile, 0:PADW + S]
        bufs = (win_a, win_b)
        for step in range(2 * tile + 2):
            shift = 2 ** step
            last_step = step == 2 * tile + 1
            rows_ = slice(64, P) if last_step else slice(0, P)
            dst = bufs[step % 2]
            then_p(pool.tensor_tensor(dst[rows_, shift:PADW + S], src[rows_, shift:PADW + S],
                                      src[rows_, 0:PADW + S - shift], ALU.add))
            if step == 2 * tile:
                low = dst
            src = dst
        for rows_, buf in ((slice(0, 64), low), (slice(64, P), src)):
            then_p(pool.tensor_tensor(pooled[rows_, tile, :], buf[rows_, PADW:PADW + S], rcount[rows_, tile, :],
                                      ALU.mult))
            pool_in = then_p(pool.tensor_tensor(pooled[rows_, tile, :], pooled[rows_, tile, :], mix[rows_, tile, :],
                                                ALU.subtract))
    wait(pool, *mixB_ok)
    conv_y = gates[:, 16:18]
    for tile in range(2):
        tap = gates[:, 12 + tile, :]
        then_p(pool.memset(pad_u[:, tile, 0:TAPS3 - 1], 0.0))
        then_p(pool.tensor_tensor(pad_u[:, tile, TAPS3 - 1:TAPS3 - 1 + S], mix[:, 6 + tile, :], mix[:, 2 + tile, :],
                                  ALU.mult))
        for k in range(TAPS3):
            wcol = cols[:, W_CONV + 2 * k + tile:W_CONV + 2 * k + tile + 1].to_broadcast([P, S])
            then_p(pool.tensor_tensor(tap if k else conv_y[:, tile, :], pad_u[:, tile, k:k + S], wcol, ALU.mult))
            if k:
                then_p(pool.tensor_tensor(conv_y[:, tile, :], conv_y[:, tile, :], tap, ALU.add))
        conv_ok = then_p(pool.tensor_tensor(conv_y[:, tile, :], conv_y[:, tile, :], mix[:, 4 + tile, :], ALU.mult))

    def gate_tiles(s):
        def take(b0, ps):
            wait(act, ps)
            if s == 3:
                wait(act, conv_br)
            for i in range(2):
                m = AA(act.activation(pair(gates, 4 * s + 2 * i), bank[b0 + i][:, :], ACT.Sigmoid))
                bank_free[b0 + i] = [m]
            return m
        return take


    for s in range(6):
        gates_ok = slab(unit_features, h_hi, h_lo, between=lambda j: attention1(RING + 4 * s + j), finish=gate_tiles(s))
        if s == 1:
            assert ada_sum["slab"] >= 8
            b = 2 * parity[0]
            claim(b)
            wait(pe, ada_sum["ready"][7])
            ps = ada_columns(2, 2, b, 0)
            ada_sum["free"][2:4] = [ps] * 2
            wait(dve, ps)
            m = AV(dve.tensor_tensor(adacol[:, 16:24], bank[b][:, 0:8], cols[:, B_ADA + 24:B_ADA + 32], ALU.add))
            bank_free[b] = [m]
        if s == 2:
            claim(7)
            wait(pe, pool_in, wpool_in, wp_zero)
            for tile in range(2):
                mm = pe.matmul(bank[7][:, tile * S:tile * S + S], wpool[:, tile, :], pooled[:, tile, :],
                               start=True, stop=True)
            ps = done(mm, PE)
            for tile in range(2):
                pool_ok = to_branch(7, slice(tile * S, tile * S + S), 4 + tile, ps,
                                    scale=cols[:, C_POOL + tile:C_POOL + tile + 1])
                wait(act, pool_ok)
            conv_br = split_to_branch(conv_y, 6, 2, conv_ok)
        if s == 3:
            wait(act, row0_ok)
            ff_rows = arrivals("ff_rows_in")
            load_row(rows[:, 1, :], "b_ada", 5 * D, ff_rows)
            row1_in = load_row(rowtmp[:, :], "g_ff_post", 0, ff_rows)

    merged_ok = []
    for n in range(2):
        sets = ((0, 1), (2, 3), (4, 5)) if n == 0 else ((6, 7), (0, 1), (2, 3))
        got, added = [], [None, None]
        for br, (units, banks) in enumerate(zip(((0, 1), (2,), (3,)), sets)):
            claim(*banks)
            if n == 0:
                wait(pe, *([pr.branch_ok for pr in pairs1] if br == 0 else [pool_ok] if br == 1 else [conv_br]))

            def take_gated(ps):
                wait(dve, ps, gates_ok)
                for i, b in enumerate(banks):
                    g = pair(gates, KD * br + 4 * n + 2 * i)
                    m = AV(dve.tensor_tensor(g if br else pair(h_f32, 4 * n + 2 * i), g, bank[b][:, :], ALU.mult))
                    bank_free[b] = [m]
                    got.append(m)
            for j in units:
                next_unit(unit_features, UK * j, br_hi, br_lo, [bank[b] for b in banks], first=(j == units[0]),
                          last=(j == units[-1]), finish=take_gated if j == units[-1] else None)
            if br:
                for i in range(2):
                    wait(pool, got[len(got) - 2 + i])
                    acc = pair(h_f32, 4 * n + 2 * i)
                    added[i] = then_p(pool.tensor_tensor(acc, acc, pair(gates, KD * br + 4 * n + 2 * i), ALU.add))
        for i in range(2):
            k = 4 * n + 2 * i
            wait(act, added[i])
            m = AA(act.copy(pair(h_hi, k), pair(h_f32, k)))
            wait(dve, m)
            merged_ok.append(AV(dve.tensor_tensor(pair(h_lo, k), pair(h_f32, k), as_f32(pair(h_hi, k)),
                                                  ALU.subtract)))
    parity[0] = 0

    assert ada_sum["slab"] >= 10
    claim(4)
    wait(pe, ada_sum["ready"][9])
    ps = ada_columns(0, 2, 4, 0)
    wait(dve, ps)
    m = then_v(dve.tensor_tensor(adacol[:, 24:32], bank[4][:, 0:8], cols[:, B_ADA + 32:B_ADA + 40], ALU.add))
    bank_free[4] = [m]
    ffcols = then_v(dve.scalar_tensor_tensor(out=adacol[:, 24:32], in0=adacol[:, 24:32], scalar=1.0,
                                             in1=cols[:, G_FF:G_FF + KD], op0=ALU.add, op1=ALU.mult))

    def post_half(n, banks, ps, row, row_ok):
        wait(act, ps)
        wait(dve, row_ok)
        for tt in range(NT):
            i = 20 + 2 * tt + n
            sq = AA(act.activation(JUNK[:, tt * UN:tt * UN + UN], bank[banks[tt]][:, :], ACT.Square,
                                   accum_out=stat[:, i:i + 1]))
            wait(act, sq)
            wait(dve, sq)
            cs = slice(n * UN, n * UN + UN)
            m = AV(dve.tensor_tensor(NORM[:, tt, cs], bank[banks[tt]][:, :], row[:, cs], ALU.mult))
            bank_free[banks[tt]] = [m]
        return sq, m

    def post_sum(sq, scaled, factor=None):
        sums = stat[:, 20:24].rearrange("p (a b) -> p a b", b=2)
        wait(pool, sq)
        then_p(pool.tensor_tensor(stat[:, 24:26], sums[:, :, 0], sums[:, :, 1], ALU.add))
        if factor:
            then_p(pool.tensor_tensor(stat[:, 24:26], stat[:, 24:26], factor[1], ALU.mult))
        rs = rstd_of(stat[:, 24:26], stat[:, 26:28], stat[:, 28:30], D, [])
        if factor:
            rs = then_p(pool.tensor_tensor(stat[:, 28:30], stat[:, 28:30], factor[0], ALU.mult))
        wait(dve, scaled, rs)
        return [[AV(dve.scalar_tensor_tensor(out=x[:, tt, :], in0=NORM[:, tt, :], scalar=stat[:, 28 + tt:29 + tt],
                                             in1=x[:, tt, :], op0=ALU.mult, op1=ALU.add))] for tt in range(NT)]

    def out_projection(in_hi, in_lo, row, row_ok, before=None):
        for n in range(2):
            half_done = slab(unit_tokens, in_hi, in_lo, before=before if n == 0 else None,
                             finish=lambda b0, ps: post_half(n, (b0, b0 + 1), ps, row, row_ok), last_of_all=n == 1)
        return post_sum(*half_done)

    x_ok = out_projection(h_hi, h_lo, rows[:, 0, :], row0_ok, before=lambda j: wait(pe, merged_ok[j]))

    def feed_forward(name, ready_of, row, row_ok, factor=None):
        made = counter(name + "_made")
        first_used = at[0]
        hid = h_f32[:, 0:4]
        split_f = counter(name + "_relu")

        def w1_slab(u, b0=0, before=None):
            for q in range(RING):
                pe.wait_ge(lo_done, u + (q + 1))
                if before:
                    before(q)
                unit_features(q, UK * q, h_hi, h_lo, [bank[b0], bank[b0 + 1]], first=(q == 0),
                              last=(q == RING - 1)).then_inc(used, 1)
                split_ahead(u + q, q)

        def split_ahead(u, slot):
            if isinstance(u, int) and u + RING >= UNITS:
                return
            split(u + RING, slot)
            if isinstance(u, int):
                split_at[0] = max(split_at[0], u + RING + 1)

        def take_hidden(j, u_end, b0=0):
            act.wait_ge(used, u_end)
            if not (isinstance(j, int) and j == 0):
                act.wait_ge(made.sem, j)
            for i in range(2):
                act.activation(pair(hid, 2 * i), bank[b0 + i][:, :], ACT.Relu).then_inc(split_f.sem, 1)
            for i in range(2):
                dve.wait_ge(split_f.sem, j * 2 + (i + 1))
                r = pair(hid, 2 * i)
                m = AV(dve.tensor_tensor(r, r, r, ALU.mult))
            wait(dve, m)

        def split_hidden(w2_end, tile0=0):
            for i in range(2):
                f = slice(2 * i, 2 * i + 2)
                to = slice(tile0 + 2 * i, tile0 + 2 * i + 2)
                if i == 0 and w2_end is not None:
                    dve.wait_ge(used, w2_end)
                then_v(dve.tensor_copy(br_hi[:, to, :], hid[:, f, :]))
                ins = dve.tensor_tensor(br_lo[:, to, :], hid[:, f, :], as_f32(br_hi[:, to, :]), ALU.subtract)
                m = AV(ins)
            wait(dve, m)
            dve.sem_inc(made.sem, 1)

        def w2_step(j, u, first, last, after=None, tile0=0):
            pe.wait_ge(made.sem, j + 1)
            for q in range(RING):
                pe.wait_ge(lo_done, u + (q + 1))
                n = q // 2
                unit_tokens(q, tile0 + UK * (q % 2), br_hi, br_lo, [bank[4 + 2 * n][:, :], bank[5 + 2 * n][:, :]],
                            first=first and q % 2 == 0, last=last and q % 2 == 1).then_inc(used, 1)
                if after:
                    after(q)
                if not (last and q == RING - 1):
                    split_ahead(u + q, q)

        u = at[0]
        assert u % RING == 0
        claim(2, 3)
        w1_slab(u, 2, before=lambda q: wait(pe, ready_of(UK * q)))
        take_hidden(0, u + RING, 2)
        split_hidden(None)
        bank_free[2] = bank_free[3] = [(split_f, 2)]
        u += RING
        claim(0, 1, 4, 5, 6, 7)

        LAST_TILE = 4

        def step(i, u, first, final=False):
            if not (isinstance(i, int) and i == 0):
                pe.wait_ge(split_f.sem, i * 2 + 2)
            w1_slab(u)
            take_hidden(i + 1, u + RING)
            if not final:
                w2_step(i, u + RING, first, False)
            split_hidden(None if final else u + 2 * RING, tile0=LAST_TILE if final else 0)
            if final:
                w2_step(i, u + RING, first, False)
        step(0, u, True)
        u += 2 * RING
        with loop(nc, FF_STEPS - 3, {VE: VE_PER_STEP}) as i:
            step(i + 1, i * (2 * RING) + u, False)
        u += (FF_STEPS - 3) * 2 * RING
        step(FF_STEPS - 2, u, False, final=True)
        u += 2 * RING
        half_done = []

        def after(q):
            if q % 2:
                n = q // 2
                half_done.append(post_half(n, (4 + 2 * n, 5 + 2 * n), used_up_to(u + q + 1), row, row_ok))
        w2_step(FF_STEPS - 1, u, False, True, after, tile0=LAST_TILE)
        at[0] = u + RING
        if u + RING < UNITS:
            split_at[0] = u + 2 * RING - 1
        bank_free[0] = bank_free[1] = [(split_f, 2 * FF_STEPS)]
        parity[0] = 0
        return post_sum(*half_done[1], factor)

    VE_PER_STEP = 6
    wait(act, ffcols)
    h_ready = affine_and_split(turn(pre_norm(x, x_ok)), adacol[:, 24:32], adacol[:, 16:24])
    split_next()
    row_post_mix = load_row(rows[:, 0, :], "post_mix_g_2")
    assert ada_sum["slab"] == A_SLABS
    wait(pe, ada_sum["ready"][A_SLABS - 1])
    _, row1_ok = ada_row(2, rows[:, 1, :], row1_in, 2)
    x_ok = feed_forward("ff1", h_ready, rows[:, 1, :], row1_ok)
    wait(act, *x_ok[1])
    row_post_x = load_row(rows[:, 1, :], "post_x_g_2")

    h_ready = gain_and_split(turn(pre_norm(x, x_ok)), cols[:, G_MIX2:G_MIX2 + KD], h_hi, h_lo)
    split_next()
    pad_zero = then_p(pool.memset(pad_u[:, :, 0:TAPS31 - 1], 0.0))

    def take_glu(b0, ps):
        sig = gates[:, 16:18]
        wait(act, ps)
        sig_ok = AA(act.activation(pair(gates, 16), bank[b0 + 1][:, :], ACT.Sigmoid))
        bank_free[b0 + 1] = [sig_ok]
        wait(dve, sig_ok, pad_zero)
        for tile in range(2):
            m = AV(dve.tensor_tensor(pad_u[:, tile, TAPS31 - 1:], bank[b0][:, tile * S:tile * S + S],
                                     sig[:, tile, :], ALU.mult))
        bank_free[b0] = [m]
        return m
    glu_ok = slab(unit_features, h_hi, h_lo, before=wait_chunks(h_ready), finish=take_glu)

    conv_y = mix[:, 4:6]
    tap_marks = [glu_ok]
    late = {}

    def tap_column(k, tile):
        return cols[:, W_DW + 2 * k + tile:W_DW + 2 * k + tile + 1]

    def vector_tap(k):
        def emit_tap():
            wait(dve, tap_marks[-1])
            if k == 0:
                ins = dve.tensor_scalar(conv_y[:, 0, :], pad_u[:, 0, 0:S], tap_column(0, 0), cols[:, C_BDW:C_BDW + 1],
                                        ALU.mult, ALU.add)
            else:
                ins = dve.scalar_tensor_tensor(out=conv_y[:, 0, :], in0=pad_u[:, 0, k:k + S], scalar=tap_column(k, 0),
                                               in1=conv_y[:, 0, :], op0=ALU.mult, op1=ALU.add)
            tap_marks.append(AV(ins))
        return emit_tap
    background.extend(vector_tap(k) for k in range(TAPS31))
    wait(pool, glu_ok)
    tap = gates[:, 15, :]

    def pool_tap(k):
        def emit_tap():
            dst = tap if k else conv_y[:, 1, :]
            then_p(pool.tensor_tensor(dst, pad_u[:, 1, k:k + S], tap_column(k, 1).to_broadcast([P, S]), ALU.mult))
            other = tap if k else cols[:, C_BDW + 1:C_BDW + 2].to_broadcast([P, S])
            late["conv1"] = then_p(pool.tensor_tensor(conv_y[:, 1, :], conv_y[:, 1, :], other, ALU.add))
        return emit_tap
    pool_background.extend(pool_tap(k) for k in range(TAPS31))

    q_ok = slab(unit_features, h_hi, h_lo, finish=evac_to(lambda i: pair(qT, 2 * i)))
    k_ok = slab(unit_features, h_hi, h_lo, finish=evac_to(lambda i: pair(kT, 2 * i)))
    att2_waits = [*q_ok, *k_ok]
    wait(dve, dist_ok)

    def floats(a, b):
        return gates[:, a:b].rearrange("p a s -> p (a s)").rearrange("p (e c) -> p e c", e=2)
    pairs2 = [HeadPair(g, floats(3 * g, 3 * g + 3), probT_pair if g % 2 == 0 else floats(12, 15), False,
                       *[(4, 5) if g % 2 == 0 else (6, 7)] * 2) for g in range(4)]
    ya = gates[:, 18:20]
    u_T, vg = mix[:, 0:2], mix[:, 2:4]
    def take_gelu(b0, ps):
        wait(act, ps)
        u_ok = AA(act.activation(pair(mix, 0), bank[b0][:, :], ACT.Gelu))
        v_gelu = AA(act.activation(pair(mix, 2), bank[b0 + 1][:, :], ACT.Gelu))
        bank_free[b0], bank_free[b0 + 1] = [u_ok], [v_gelu]
        return u_ok, v_gelu

    def gate_norm():
        wait(dve, late["gelu"][1], small_in)
        for tt in range(NT):
            then_v(dve.bn_stats(stats6[:, tt, :], vg[:, tt, :]))
            m = then_v(dve.bn_aggr(stat[:, 2 * tt:2 * tt + 2], stats6[:, tt, :]))
        var = stat[:, 0:4].rearrange("p (a b) -> p a b", b=2)[:, :, 1]
        late["rstd"] = rstd_of(var, stat[:, 4:6], stat[:, 6:8], 1, [m])

    def gate_scale():
        wait(dve, late["rstd"])
        for tt in range(NT):
            then_v(dve.tensor_scalar(vg[:, tt, :], vg[:, tt, :], stat[:, 2 * tt:2 * tt + 1], stat[:, 6 + tt:7 + tt],
                                     ALU.subtract, ALU.mult))
            then_v(dve.tensor_tensor(vg[:, tt, :], vg[:, tt, :], ln_rows[:, 0, :], ALU.mult))
            late["v"] = then_v(dve.tensor_tensor(vg[:, tt, :], vg[:, tt, :], ln_rows[:, 1, :], ALU.add))

    def gate_mix():
        b = 2 * parity[0]
        claim(b)
        wait(pe, late["v"], wsT_ok)
        for h in range(4):
            for tt in range(NT):
                c0 = (h // 2) * S + tt * P
                mm = pe.matmul(bank[b][64 * (h % 2):64 * (h % 2) + 64, c0:c0 + P], vg[:, tt, h * 64:h * 64 + 64],
                               ws_T[:, h, :], start=True, stop=True)
        ps = done(mm, PE)
        wait(dve, ps, late["gelu"][0])
        for tile in range(2):
            for tt in range(NT):
                c = slice(tt * P, tt * P + P)
                m = AV(dve.tensor_tensor(ya[:, tile, c], bank[b][:, tile * S + tt * P:tile * S + tt * P + P],
                                         bs_row[:, tile, :], ALU.add))
        bank_free[b] = [m]
        wait(dve, m)
        m = then_v(dve.tensor_tensor(ya, ya, u_T, ALU.mult))
        late["ya"] = split_to_branch(ya, 4, 2, m)

    conv2, sq2 = pair(mix, 4), pair(mix, 6)
    NORM_BANK = 5

    def conv_center():
        assert not background and not pool_background
        conv1_ok = late["conv1"]
        claim(NORM_BANK)
        wait(pe, tap_marks[-1], conv1_ok, pool_consts)
        ps = done(pe.matmul(bank[NORM_BANK][:, :], blockmean[:, :], conv2, start=True, stop=True), PE)
        wait(dve, ps, tap_marks[-1], conv1_ok)
        cen = then_v(dve.tensor_tensor(conv2, conv2, bank[NORM_BANK][:, :], ALU.subtract))
        wait(act, cen)
        late["squares"] = AA(act.activation(sq2, conv2, ACT.Square))

    def conv_norm():
        wait(pe, late["squares"])
        for tile in range(2):
            for tt in range(NT):
                c = 4 * tile + 2 * tt
                mm = pe.matmul(bank[NORM_BANK][:, c:c + 2], sq2[:, tile * S + tt * P:tile * S + tt * P + P],
                               blockmean[:, 0:P:64], start=True, stop=True)
        ps = done(mm, PE)
        wait(dve, ps)
        m = AV(dve.tensor_copy(stat[:, 8:16], bank[NORM_BANK][:, 0:8]))
        bank_free[NORM_BANK] = [m]
        late["group_rstd"] = rstd_of(stat[:, 8:16], stat[:, 8:16], stat[:, 16:24], 1, [m])

    def conv_silu():
        claim(NORM_BANK)
        wait(pe, late["group_rstd"])
        for tile in range(2):
            for tt in range(NT):
                for g in range(2):
                    c = 16 + 4 * tile + 2 * tt + g
                    mm = pe.matmul(bank[NORM_BANK][64 * g:64 * g + 64, tile * S + tt * P:tile * S + tt * P + P],
                                   stat[:, c:c + 1].to_broadcast([P, 64]), ident[:, :], start=True, stop=True)
        ps = done(mm, PE)
        wait(dve, ps)
        m = then_v(dve.tensor_tensor(conv2, conv2, bank[NORM_BANK][:, :], ALU.mult))
        bank_free[NORM_BANK] = [m]
        wait(act, m)
        for tile in range(2):
            m = AA(act.activation(conv_y[:, tile, :], conv_y[:, tile, :], ACT.Silu,
                                  bias=cols[:, C_GNB + tile:C_GNB + tile + 1],
                                  scale=cols[:, C_GNG + tile:C_GNG + tile + 1]))
        late["yc"] = split_to_branch(conv_y, 6, 2, m)

    p0, p1, p2, p3 = pairs2

    def start_pair(pr):
        return lambda: pr.scores(att2_waits)

    def finish_pair(pr):
        return lambda: pr.attend(v_ok)
    plan = {0: [start_pair(p0)], 1: [p0.exponentials, start_pair(p1)], 2: [p1.exponentials, p0.reciprocals],
            3: [gate_norm, p0.normalize, p1.reciprocals], 4: [p1.normalize, gate_scale, start_pair(p2)],
            5: [p2.exponentials, start_pair(p3)], 6: [gate_mix, p0.turn, p2.reciprocals],
            7: [p1.turn, p3.exponentials, p2.normalize], 8: [finish_pair(p0), finish_pair(p1), p3.reciprocals],
            9: [p3.normalize, p2.turn], 10: [finish_pair(p2), p3.turn, conv_center], 11: [finish_pair(p3), conv_norm],
            12: [conv_silu]}

    def follow(unit):
        for step in plan.get(unit, ()):
            step()

    b0 = 2 * parity[0]
    parity[0] ^= 1
    claim(b0, b0 + 1)

    def unit_mixed(slot, k0, first, last):
        unit_features(slot, k0, h_hi, h_lo, [bank[b0]], first, last, tiles=2)
        return unit_tokens(slot, k0, h_hi, h_lo, [bank[b0 + 1][:, 0:S], bank[b0 + 1][:, S:2 * S]], first, last,
                           cols=slice(S, 2 * S), start_first=False)
    for j in range(RING):
        late["gelu"] = next_unit(unit_mixed, UK * j, first=(j == 0), last=(j == RING - 1),
                                 finish=(lambda ps: take_gelu(b0, ps)) if j == RING - 1 else None)
        follow(j)
    v_ok = slab(unit_tokens, h_hi, h_lo, between=lambda j: follow(RING + j), finish=evac_to(lambda i: v_tok[:, i, :]))

    tiles_of = {0: 4, 1: 0, 2: 2, 3: 6}
    claim(0, 1, 2, 3)
    follow(2 * RING)
    for i, (n, k) in enumerate(OUT2_ORDER):
        if k == 0:
            wait(pe, late["ya"])
        elif k == 3:
            wait(pe, late["yc"])
        else:
            wait(pe, pairs2[2 * k - 2].branch_ok, pairs2[2 * k - 1].branch_ok)
        half_done = next_unit(unit_tokens, tiles_of[k], br_hi, br_lo, [bank[2 * n][:, :], bank[2 * n + 1][:, :]],
                              first=(k == 1), last=(k == 3), last_of_all=(n == 1 and k == 3), finish=(lambda ps: post_half(
                                  n, (2 * n, 2 * n + 1), ps, rows[:, 0, :], row_post_mix)) if k == 3 else None)
        follow(2 * RING + 1 + i)
    parity[0] = 0
    x_ok = post_sum(*half_done)
    wait(act, *x_ok[1])
    row_post_ff = load_row(rows[:, 0, :], "post_ffn_g_2")

    h_ready = gain_and_split(turn(x_ok, x), cols[:, G_X2:G_X2 + KD], h_hi, h_lo)
    split_next()
    r_ok = sums_to_rstd(x, x_ok)
    r_logit = stat[:, 6:8]
    wait(pool, r_ok)
    r_logit_ok = then_p(pool.tensor_scalar(r_logit, R_TOKEN, 1.0 / 16, 1.0, ALU.mult, ALU.mult))
    xq = mix

    class CrossHead:

        def __init__(self, h, prob):
            self.h, self.prob, self.bank = h, prob, 4 + h % 2
            c = 6 * h
            self.mx, self.negmx, self.rsum = att[:, c:c + 2], att[:, c + 2:c + 4], att[:, c + 4:c + 6]

        def logits(self, tt):
            return bank[self.bank][:, tt * S:tt * S + S]

        def scores(self):
            claim(self.bank)
            wait(pe, *xq_ok[self.h // 2])
            for tt in range(NT):
                for c in range(2):
                    k = 2 * self.h + c
                    mm = pe.matmul(self.logits(tt), xq[:, k, tt * P:tt * P + P], mem_k[:, k, :],
                                   start=(c == 0), stop=(c == 1))
            wait(dve, done(mm, PE), r_logit_ok)
            for tt in range(NT):
                m = AV(dve.tensor_reduce(self.mx[:, tt:tt + 1], self.logits(tt), AX.X, ALU.max))
            wait(dve, m)
            self.max_ok = AV(dve.scalar_tensor_tensor(out=self.negmx, in0=self.mx, scalar=-1.0, in1=r_logit,
                                                      op0=ALU.mult, op1=ALU.mult))

        def exponentials(self):
            wait(act, self.max_ok)
            for tt in range(NT):
                m = AA(act.activation(self.prob[:, tt, :], self.logits(tt), ACT.Exp, bias=self.negmx[:, tt:tt + 1],
                                      scale=r_logit[:, tt:tt + 1], accum_out=self.rsum[:, tt:tt + 1]))
            bank_free[self.bank] = [m]
            self.exp_ok = m

        def normalize(self):
            wait(dve, self.exp_ok)
            then_v(dve.reciprocal(self.rsum, self.rsum))
            for tt in range(NT):
                self.prob_ok = AV(dve.tensor_scalar(self.prob[:, tt, :], self.prob[:, tt, :],
                                                    self.rsum[:, tt:tt + 1], None, ALU.mult))

        def turn(self):
            claim(6)
            wait(pe, self.prob_ok)
            for kt in range(NT):
                for tt in range(NT):
                    c0 = kt * S + tt * P
                    mm = pe.transpose(bank[6][:, c0:c0 + P], self.prob[:, tt, kt * P:kt * P + P], ident[:, :])
            wait(act, done(mm, PE))
            self.turned_ok = AA(act.copy(probT[:, self.h % 2, :], bank[6][:, :]))
            bank_free[6] = [self.turned_ok]

        def attend(self):
            claim(7)
            wait(pe, self.turned_ok)
            for c in range(2):
                for kt in range(NT):
                    fc = slice(self.h * XD + c * P, self.h * XD + c * P + P)
                    mm = pe.matmul(bank[7][:, c * S:c * S + S], mem_v[:, kt, fc],
                                   probT[:, self.h % 2, kt * S:kt * S + S], start=(kt == 0), stop=(kt == 1))
            self.branch_ok = to_branch(7, slice(0, 2 * S), 2 * self.h, done(mm, PE), n=2)

    x0, x1, x2, x3 = [CrossHead(h, gates[:, a:a + 2]) for h, a in enumerate((16, 18, 8, 10))]
    xq_ok = [slab(unit_features, h_hi, h_lo, before=wait_chunks(h_ready), finish=evac_to(lambda i: pair(xq, 2 * i)))]

    plan = {0: [x0.scores, x1.scores], 1: [x0.exponentials, x1.exponentials], 2: [x0.normalize, x1.normalize],
            3: [x0.turn], 4: [x2.exponentials, x3.exponentials], 5: [x1.attend, x2.normalize, x3.normalize],
            6: [x2.turn], 7: [x2.attend, x3.turn], 8: [x3.attend]}
    xq_ok.append(slab(unit_features, h_hi, h_lo, between=follow, finish=evac_to(lambda i: pair(xq, 4 + 2 * i))))
    for step in (x0.attend, x1.turn, x2.scores, x3.scores):
        step()
    claim(0, 1, 2, 3)
    for i, (n, k) in enumerate(XO_ORDER):
        wait(pe, (x0, x1, x2, x3)[k].branch_ok)
        half_done = next_unit(unit_tokens, UK * k, br_hi, br_lo, [bank[2 * n][:, :], bank[2 * n + 1][:, :]],
                              first=(k == 0), last=(k == 3), last_of_all=(n == 1 and k == 3), finish=(lambda ps: post_half(
                                  n, (2 * n, 2 * n + 1), ps, rows[:, 1, :], row_post_x)) if k == 3 else None)
        follow(RING + i)
    parity[0] = 0
    x_ok = post_sum(*half_done)

    h_ready = gain_and_split(turn(x_ok, x), cols[:, G_FF2:G_FF2 + KD], h_hi, h_lo)
    split_next()
    wait(pool, sums_to_rstd(x, x_ok))
    r2, r4 = stat[:, 8:10], stat[:, 10:12]
    then_p(pool.tensor_tensor(r2, R_TOKEN, R_TOKEN, ALU.mult))
    then_p(pool.tensor_tensor(r4, r2, r2, ALU.mult))
    x_ok = feed_forward("ff2", h_ready, rows[:, 0, :], row_post_ff, (r2, r4))
    ld_out = arrivals("out_done")
    for tt in range(NT):
        wait(sp, *x_ok[tt])
        out_done = ld_out(sp, out[0][tt * P:tt * P + P, :], x[:, tt, :])
    wait(sp, out_done)
    assert at[0] == UNITS and split_at[0] == UNITS, (at, split_at, UNITS)


_INS = ["x", "c", "w_ada", "b_ada", "g_mix_pre", "g_mix_post", "g_ff_pre", "g_ff_post", "w_in", "b_f", "w_pool",
        "pool_scale", "conv_w", "w_branch", "w_out", "w_ff1", "w_ff2", "mem_2", "pre_mix_g_2", "w_in_2",
        "gate_ln_g_2", "gate_ln_b_2", "w_s_2", "b_s_2", "w_dw_2", "b_dw_2", "conv_gn_g_2", "conv_gn_b_2", "w_out_2",
        "post_mix_g_2", "pre_x_g_2", "mem_g_2", "w_xq_2", "w_xkv_2", "w_xo_2", "post_x_g_2", "pre_ffn_g_2",
        "w_ff1_2", "w_ff2_2", "post_ffn_g_2"]


def kernel(**inputs):
    import concourse.bacc as bacc
    from concourse.bass_utils import run_bass_kernel_spmd

    nc = bacc.Bacc("TRN2", target_bir_lowering=False, num_devices=1)
    arrays, aps = {}, {}
    for name in _INS:
        a = np.ascontiguousarray(inputs[name])
        arrays[f"in_{name}"] = a
        aps[name] = nc.dram_tensor(f"in_{name}", a.shape, mybir.dt.from_np(a.dtype), kind="ExternalInput").ap()
    out = nc.dram_tensor("out", (1, S, D), F32, kind="ExternalOutput").ap()
    packed = {"columns": np.ascontiguousarray(np.concatenate([np.asarray(inputs[n]).reshape(-1, P)
                                                              for n, _ in COLUMNS]).T),
              "w_s_T": np.ascontiguousarray(np.asarray(inputs["w_s_2"])[0].transpose(2, 0, 1))}
    for name, a in packed.items():
        arrays[f"in_{name}"] = a
        aps[name] = nc.dram_tensor(f"in_{name}", a.shape, F32, kind="ExternalInput").ap()
    build(nc, aps, out)
    r = run_bass_kernel_spmd(nc, [arrays], core_ids=[0])
    return r.results[0]["out"]
```
